# Optimizing a Trainium2 kernel written in Bass

```python
import math
import jax, jax.numpy as jnp
from jax import lax
import numpy as np

D_MODEL = 1024
BATCH = 1
SEQ = 256
DEPTH = 2

N_MIXERS = 2
HEAD_DIM = 64
N_HEADS = D_MODEL // HEAD_DIM
N_RWKV = (DEPTH + 1) // 2
N_MOBA = DEPTH // 2
DECAY_LORA = max(32, int(round(1.8 * D_MODEL ** 0.5 / 32)) * 32)
AAA_LORA = max(32, int(round(1.8 * D_MODEL ** 0.5 / 32)) * 32)
GATE_LORA = max(32, int(round(0.6 * D_MODEL ** 0.8 / 32)) * 32)
GN_EPS = HEAD_DIM * 1e-5
MOBA_BLOCK = 256
MOBA_TOPK = 3
Q_CHUNK = 128
ROPE_THETA = 10000.0
D_FF = -(-8 * D_MODEL // (3 * 256)) * 256
ALPHA = (2 * DEPTH) ** 0.25
BETA = (8 * DEPTH) ** -0.25
LN_EPS = 1e-5


def layer_norm(x, g, b):
    xf = x.astype(jnp.float32)
    mu = xf.mean(-1, keepdims=True)
    var = jnp.square(xf - mu).mean(-1, keepdims=True)
    return ((xf - mu) * lax.rsqrt(var + LN_EPS) * g + b).astype(x.dtype)

def swiglu_ffn(x, w_in, w_down):
    gate, up = jnp.split(x @ w_in, 2, axis=-1)
    return (jax.nn.silu(gate) * up) @ w_down

def time_shift(x):
    return jnp.pad(x, ((0, 0), (1, 0), (0, 0)))[:, :-1, :]

def rwkv7_time_mix(x, mu, w_rkv, w0, w1, w2, a0, a1, a2, g1, g2, k_k, k_a, r_k, gn_g, gn_b, w_o):
    B, T, C = x.shape
    H, N = N_HEADS, HEAD_DIM
    f32 = jnp.float32
    xx = time_shift(x) - x
    xr, xw, xk, xv, xa, xg = [x + xx * mu[n] for n in range(6)]
    r, k, v = jnp.einsum('nbtc,ncd->nbtd', jnp.stack([xr, xk, xv]), w_rkv)
    w = -jax.nn.softplus(-(w0 + jnp.tanh(xw @ w1) @ w2)) - 0.5
    a = jax.nn.sigmoid(a0 + (xa @ a1) @ a2)
    g = jax.nn.sigmoid(xg @ g1) @ g2
    heads = lambda t: t.reshape(B, T, H, N).astype(f32)
    kk = heads(k * k_k)
    kk = kk / jnp.maximum(jnp.sqrt(jnp.sum(kk * kk, -1, keepdims=True)), 1e-12)
    k = k * (1 + (a - 1) * k_a)
    rh, kh, vh, ah = heads(r), heads(k), heads(v), heads(a)
    decay = jnp.exp(-jnp.exp(heads(w)))

    def step(S, inp):
        r_t, w_t, k_t, v_t, kk_t, b_t = inp
        sa = jnp.einsum('bhvk,bhk->bhv', S, -kk_t)
        S = S * w_t[:, :, None, :] + sa[..., None] * b_t[:, :, None, :] + v_t[..., None] * k_t[:, :, None, :]
        return S, jnp.einsum('bhvk,bhk->bhv', S, r_t)

    to_time = lambda t: jnp.swapaxes(t, 0, 1)
    S0 = jnp.zeros((B, H, N, N), f32)
    _, y = lax.scan(step, S0, tuple(to_time(t) for t in (rh, decay, kh, vh, kk, kk * ah)))
    y = to_time(y)
    mean = y.mean(-1, keepdims=True)
    var = jnp.square(y - mean).mean(-1, keepdims=True)
    y = ((y - mean) * lax.rsqrt(var + GN_EPS)).reshape(B, T, C) * gn_g + gn_b
    bonus = jnp.sum(rh * kh * r_k, -1, keepdims=True) * vh
    y = (y + bonus.reshape(B, T, C)).astype(x.dtype)
    return (y * g) @ w_o

def rope_tables(T):
    inv = ROPE_THETA ** (-jnp.arange(0, HEAD_DIM, 2, dtype=jnp.float32) / HEAD_DIM)
    ang = jnp.arange(T, dtype=jnp.float32)[:, None] * inv[None, :]
    return jnp.cos(ang), jnp.sin(ang)

def apply_rope(t, cos, sin):
    t1, t2 = jnp.split(t, 2, axis=-1)
    return jnp.concatenate([t1 * cos - t2 * sin, t2 * cos + t1 * sin], axis=-1)

def moba_attention(x, w_qkv, w_o):
    B, T, C = x.shape
    H, Dh = N_HEADS, HEAD_DIM
    f32 = jnp.float32
    qkv = (x @ w_qkv).reshape(B, T, 3, H, Dh)
    q, k, v = [jnp.transpose(qkv[:, :, n], (0, 2, 1, 3)).astype(f32) for n in range(3)]
    cos, sin = rope_tables(T)
    q = apply_rope(q, cos, sin) * (Dh ** -0.5)
    k = apply_rope(k, cos, sin)
    NB = -(-T // MOBA_BLOCK)
    K = min(MOBA_TOPK, NB)
    pad = NB * MOBA_BLOCK - T
    kb = jnp.pad(k, ((0, 0), (0, 0), (0, pad), (0, 0))).reshape(B, H, NB, MOBA_BLOCK, Dh)
    vb = jnp.pad(v, ((0, 0), (0, 0), (0, pad), (0, 0))).reshape(B, H, NB, MOBA_BLOCK, Dh)
    k_mean = kb.mean(axis=3)
    bi = jnp.arange(B)[:, None, None, None]
    hi = jnp.arange(H)[None, :, None, None]
    blk_ids = jnp.arange(NB)
    key_off = jnp.arange(MOBA_BLOCK)
    q_off = jnp.arange(Q_CHUNK)

    def attend_chunk(c):
        q0 = c * Q_CHUNK
        own = q0 // MOBA_BLOCK
        q_c = lax.dynamic_slice_in_dim(q, q0, Q_CHUNK, axis=2)
        gate = jnp.einsum('bhqd,bhnd->bhqn', q_c, k_mean)
        gate = jnp.where(blk_ids < own, gate, -jnp.inf)
        _, sel = lax.top_k(gate, K)
        valid = sel < own
        k_sel = kb[bi, hi, sel]
        v_sel = vb[bi, hi, sel]
        s_sel = jnp.einsum('bhqd,bhqksd->bhqks', q_c, k_sel)
        s_sel = jnp.where(valid[..., None], s_sel, -jnp.inf).reshape(B, H, Q_CHUNK, K * MOBA_BLOCK)
        k_own = lax.dynamic_index_in_dim(kb, own, axis=2, keepdims=False)
        v_own = lax.dynamic_index_in_dim(vb, own, axis=2, keepdims=False)
        s_own = jnp.einsum('bhqd,bhsd->bhqs', q_c, k_own)
        causal = (own * MOBA_BLOCK + key_off)[None, :] <= (q0 + q_off)[:, None]
        s_own = jnp.where(causal, s_own, -jnp.inf)
        p = jax.nn.softmax(jnp.concatenate([s_sel, s_own], axis=-1), axis=-1)
        p_sel = p[..., :K * MOBA_BLOCK].reshape(B, H, Q_CHUNK, K, MOBA_BLOCK)
        p_own = p[..., K * MOBA_BLOCK:]
        return (jnp.einsum('bhqks,bhqksd->bhqd', p_sel, v_sel)
                + jnp.einsum('bhqs,bhsd->bhqd', p_own, v_own))

    out = lax.map(attend_chunk, jnp.arange(T // Q_CHUNK))
    out = jnp.transpose(out, (1, 0, 3, 2, 4)).reshape(B, T, C)
    return out.astype(x.dtype) @ w_o

def first_inputs(seed: int = 0) -> dict:
    key = jax.random.key(seed)
    ks = iter(jax.random.split(key, 32))
    C, H, N, F = D_MODEL, N_HEADS, HEAD_DIM, D_FF
    nrm = lambda shape, s: jax.random.normal(next(ks), shape, jnp.float32) * s
    return {
        'x': nrm((BATCH, SEQ, C), 1.0),
        'rwkv_mu': jax.random.uniform(next(ks), (N_RWKV, 6, C), jnp.float32),
        'rwkv_w_rkv': nrm((N_RWKV, 3, C, C), C ** -0.5),
        'rwkv_w0': jax.random.uniform(next(ks), (N_RWKV, C), jnp.float32, -5.0, 0.5),
        'rwkv_w1': nrm((N_RWKV, C, DECAY_LORA), C ** -0.5),
        'rwkv_w2': nrm((N_RWKV, DECAY_LORA, C), 0.5 * DECAY_LORA ** -0.5),
        'rwkv_a0': nrm((N_RWKV, C), 0.1),
        'rwkv_a1': nrm((N_RWKV, C, AAA_LORA), C ** -0.5),
        'rwkv_a2': nrm((N_RWKV, AAA_LORA, C), 0.5 * AAA_LORA ** -0.5),
        'rwkv_g1': nrm((N_RWKV, C, GATE_LORA), C ** -0.5),
        'rwkv_g2': nrm((N_RWKV, GATE_LORA, C), GATE_LORA ** -0.5),
        'rwkv_k_k': 0.85 + nrm((N_RWKV, C), 0.05),
        'rwkv_k_a': 1.0 + nrm((N_RWKV, C), 0.05),
        'rwkv_r_k': nrm((N_RWKV, H, N), 0.1),
        'rwkv_gn_g': 1.0 + nrm((N_RWKV, C), 0.05),
        'rwkv_gn_b': nrm((N_RWKV, C), 0.02),
        'rwkv_w_o': nrm((N_RWKV, C, C), BETA * C ** -0.5),
        'moba_w_qkv': nrm((N_MOBA, C, 3 * C), C ** -0.5),
        'moba_w_o': nrm((N_MOBA, C, C), BETA * C ** -0.5),
        'ffn_w_in': nrm((DEPTH, C, 2 * F), C ** -0.5),
        'ffn_w_down': nrm((DEPTH, F, C), BETA * F ** -0.5),
        'ln_mix_g': 1.0 + nrm((DEPTH, C), 0.05),
        'ln_mix_b': nrm((DEPTH, C), 0.02),
        'ln_ffn_g': 1.0 + nrm((DEPTH, C), 0.05),
        'ln_ffn_b': nrm((DEPTH, C), 0.02),
    }

def first_block(x, rwkv_mu, rwkv_w_rkv, rwkv_w0, rwkv_w1, rwkv_w2, rwkv_a0, rwkv_a1, rwkv_a2,
              rwkv_g1, rwkv_g2, rwkv_k_k, rwkv_k_a, rwkv_r_k, rwkv_gn_g, rwkv_gn_b, rwkv_w_o,
              moba_w_qkv, moba_w_o, ffn_w_in, ffn_w_down, ln_mix_g, ln_mix_b, ln_ffn_g, ln_ffn_b):
    for i in range(DEPTH):
        j = i // N_MIXERS
        if i % N_MIXERS == 0:
            h = rwkv7_time_mix(x, rwkv_mu[j], rwkv_w_rkv[j], rwkv_w0[j], rwkv_w1[j], rwkv_w2[j],
                               rwkv_a0[j], rwkv_a1[j], rwkv_a2[j], rwkv_g1[j], rwkv_g2[j],
                               rwkv_k_k[j], rwkv_k_a[j], rwkv_r_k[j], rwkv_gn_g[j], rwkv_gn_b[j],
                               rwkv_w_o[j])
        else:
            h = moba_attention(x, moba_w_qkv[j], moba_w_o[j])
        x = layer_norm(ALPHA * x + h, ln_mix_g[i], ln_mix_b[i])
        x = layer_norm(ALPHA * x + swiglu_ffn(x, ffn_w_in[i], ffn_w_down[i]), ln_ffn_g[i], ln_ffn_b[i])
    return x


DEPTH_2 = 4

N_MIXERS_2 = 3
N_A_LAYERS = (DEPTH_2 + 2) // 3
N_B_LAYERS = (DEPTH_2 + 1) // 3
N_C_LAYERS = DEPTH_2 // 3

RMS_EPS = 1e-6
CONV_W = 3

NA_HEAD_DIM = 64
NA_HEADS = D_MODEL // NA_HEAD_DIM
GRID_W = 64
NA_MAX_ROWS = 8
NA_COLS = 16
NA_QCOLS = 16
NA_SPAN = NA_QCOLS + NA_COLS

HYENA_ORDER = 2
HYENA_BANDS = 16
HYENA_EMB = 1 + 2 * HYENA_BANDS
HYENA_FILTER_HIDDEN = 64
HYENA_DECAY_TARGET = 1e-2
HYENA_FAST_DECAY = 0.3
HYENA_SLOW_DECAY = 1.5

FFN_HIDDEN = ((8 * D_MODEL + 3 * 256 - 1) // (3 * 256)) * 256


def rmsnorm(x, g):
    xf = x.astype(jnp.float32)
    y = xf * lax.rsqrt(jnp.mean(xf * xf, axis=-1, keepdims=True) + RMS_EPS)
    return (y * g.astype(jnp.float32)).astype(x.dtype)

def depthwise_conv3(x, w, b=None):
    c = x.shape[-1]
    y = lax.conv_general_dilated(
        x, w.astype(x.dtype)[:, None, :], (1,), ((CONV_W // 2, CONV_W // 2),),
        dimension_numbers=('NWC', 'WIO', 'NWC'), feature_group_count=c)
    return y if b is None else y + b.astype(x.dtype)

def short_conv_mixer(h, w_in, conv_w, w_out):
    b_gate, c_gate, u = jnp.split(h @ w_in, 3, axis=-1)
    return (b_gate * depthwise_conv3(c_gate * u, conv_w)) @ w_out

def na_column_tables():
    cb = np.arange(GRID_W // NA_QCOLS)
    starts = np.clip(cb * NA_QCOLS - NA_COLS // 2, 0, GRID_W - NA_SPAN)
    key_col = starts[:, None] + np.arange(NA_SPAN)
    q_col = cb[:, None] * NA_QCOLS + np.arange(NA_QCOLS)
    col_start = np.clip(q_col - NA_COLS // 2, 0, GRID_W - NA_COLS)
    kc = key_col[:, None, :]
    valid = (kc >= col_start[:, :, None]) & (kc < col_start[:, :, None] + NA_COLS)
    dc_idx = np.clip(kc - q_col[:, :, None] + NA_COLS - 1, 0, 2 * NA_COLS - 2)
    return key_col, valid, dc_idx

def neighborhood_attention(h, w_qkv, q_g, k_g, rpb, w_out):
    bsz, seq, d = h.shape
    rows = seq // GRID_W
    wr = min(NA_MAX_ROWS, rows)
    q, k, v = jnp.split(h @ w_qkv, 3, axis=-1)
    grid = (bsz, rows, GRID_W, NA_HEADS, NA_HEAD_DIM)
    q = rmsnorm(q.reshape(grid), q_g)
    k = rmsnorm(k.reshape(grid), k_g)
    v = v.reshape(grid)
    key_col, valid, dc_idx = na_column_tables()
    ncb = key_col.shape[0]
    scale = NA_HEAD_DIM ** -0.5
    neg = jnp.finfo(jnp.float32).min
    mask = valid[None, None, :, :, None, :]

    def row_block(r):
        rs = jnp.clip(r - wr // 2, 0, rows - wr)
        q_r = lax.dynamic_index_in_dim(q, r, axis=1, keepdims=False)
        q_r = q_r.reshape(bsz, ncb, NA_QCOLS, NA_HEADS, NA_HEAD_DIM)
        k_r = lax.dynamic_slice_in_dim(k, rs, wr, axis=1)[:, :, key_col]
        v_r = lax.dynamic_slice_in_dim(v, rs, wr, axis=1)[:, :, key_col]
        s = jnp.einsum('bnqhd,brnkhd->bhnqrk', q_r, k_r).astype(jnp.float32) * scale
        dr_idx = rs + jnp.arange(wr) - r + NA_MAX_ROWS - 1
        bias = rpb[:, dr_idx[None, None, :, None], dc_idx[:, :, None, :]]
        s = jnp.where(mask, s + bias.astype(jnp.float32)[None], neg)
        p = jax.nn.softmax(s.reshape(s.shape[:4] + (wr * NA_SPAN,)), axis=-1)
        p = p.reshape(s.shape).astype(v.dtype)
        o = jnp.einsum('bhnqrk,brnkhd->bnqhd', p, v_r)
        return o.reshape(bsz, GRID_W, d)

    o = lax.map(row_block, jnp.arange(rows))
    return o.transpose(1, 0, 2, 3).reshape(bsz, seq, d) @ w_out

def hyena_filters(seq, w1, b1, w2, b2, w3, freq):
    f32 = jnp.float32
    t = jnp.linspace(0.0, 1.0, seq, dtype=f32)[:, None]
    bands = jnp.linspace(1e-4, HYENA_BANDS - 1, HYENA_BANDS, dtype=f32)
    ang = (2.0 * math.pi) * jnp.arange(seq, dtype=f32)[:, None] / seq * bands
    z = jnp.concatenate([t, jnp.cos(ang), -jnp.sin(ang)], axis=-1)
    fr = freq.astype(f32)
    hid = jnp.sin(fr * (z @ w1.astype(f32) + b1.astype(f32)))
    hid = jnp.sin(fr * (hid @ w2.astype(f32) + b2.astype(f32)))
    filt = (hid @ w3.astype(f32)).reshape(seq, HYENA_ORDER, 2, D_MODEL)
    lt = math.log(HYENA_DECAY_TARGET)
    deltas = jnp.abs(jnp.linspace(lt / HYENA_SLOW_DECAY, lt / HYENA_FAST_DECAY, D_MODEL, dtype=f32))
    filt = filt * jnp.exp(-t * deltas)[:, None, None, :]
    fwd, rev = filt[:, :, 0], filt[:, :, 1]
    h_full = jnp.concatenate([fwd[:1] + rev[:1], fwd[1:], jnp.zeros_like(fwd[:1]), rev[:0:-1]], axis=0)
    h_full = h_full / jnp.sum(jnp.abs(h_full), axis=0, keepdims=True)
    return jnp.fft.rfft(h_full, axis=0)

def hyena_mixer(h, w_in, short_w, short_b, f_w1, f_b1, f_w2, f_b2, f_w3, f_freq, f_skip, w_out):
    seq = h.shape[1]
    v, x1, x2 = jnp.split(depthwise_conv3(h @ w_in, short_w, short_b), 3, axis=-1)
    h_freq = hyena_filters(seq, f_w1, f_b1, f_w2, f_b2, f_w3, f_freq)

    def long_conv(u, n):
        uf = u.astype(jnp.float32)
        y = jnp.fft.irfft(jnp.fft.rfft(uf, n=2 * seq, axis=1) * h_freq[:, n], n=2 * seq, axis=1)[:, :seq]
        return (y + uf * f_skip[n].astype(jnp.float32)).astype(u.dtype)

    z = x1 * long_conv(v, 0)
    z = x2 * long_conv(z, 1)
    return z @ w_out

def swiglu(h, w13, w2):
    g, u = jnp.split(h @ w13, 2, axis=-1)
    return (jax.nn.silu(g) * u) @ w2

def second_inputs(seed: int = 0) -> dict:
    key = jax.random.key(seed)
    ks = jax.random.split(key, 24)
    f32 = jnp.float32

    def nrm(k, shape, fan_in):
        return jax.random.normal(k, shape, f32) * (fan_in ** -0.5)

    def gain(k, shape):
        return 1.0 + 0.02 * jax.random.normal(k, shape, f32)

    def small(k, shape, s=0.02):
        return s * jax.random.normal(k, shape, f32)

    D = D_MODEL
    return {
        'x': jax.random.normal(ks[0], (BATCH, SEQ, D), f32),
        'norm_mix_g': gain(ks[1], (DEPTH_2, D)),
        'norm_ffn_g': gain(ks[2], (DEPTH_2, D)),
        'a_w_in': nrm(ks[3], (N_A_LAYERS, D, 3 * D), D),
        'a_conv_w': nrm(ks[4], (N_A_LAYERS, CONV_W, D), CONV_W),
        'a_w_out': nrm(ks[5], (N_A_LAYERS, D, D), D),
        'b_w_qkv': nrm(ks[6], (N_B_LAYERS, D, 3 * D), D),
        'b_q_norm_g': gain(ks[7], (N_B_LAYERS, NA_HEAD_DIM)),
        'b_k_norm_g': gain(ks[8], (N_B_LAYERS, NA_HEAD_DIM)),
        'b_rpb': small(ks[9], (N_B_LAYERS, NA_HEADS, 2 * NA_MAX_ROWS - 1, 2 * NA_COLS - 1)),
        'b_w_out': nrm(ks[10], (N_B_LAYERS, D, D), D),
        'c_w_in': nrm(ks[11], (N_C_LAYERS, D, 3 * D), D),
        'c_short_w': nrm(ks[12], (N_C_LAYERS, CONV_W, 3 * D), CONV_W),
        'c_short_b': small(ks[13], (N_C_LAYERS, 3 * D)),
        'c_f_w1': nrm(ks[14], (N_C_LAYERS, HYENA_EMB, HYENA_FILTER_HIDDEN), HYENA_EMB),
        'c_f_b1': small(ks[15], (N_C_LAYERS, HYENA_FILTER_HIDDEN)),
        'c_f_w2': nrm(ks[16], (N_C_LAYERS, HYENA_FILTER_HIDDEN, HYENA_FILTER_HIDDEN), HYENA_FILTER_HIDDEN),
        'c_f_b2': small(ks[17], (N_C_LAYERS, HYENA_FILTER_HIDDEN)),
        'c_f_w3': nrm(ks[18], (N_C_LAYERS, HYENA_FILTER_HIDDEN, HYENA_ORDER * 2 * D), HYENA_FILTER_HIDDEN),
        'c_f_freq': gain(ks[19], (N_C_LAYERS, HYENA_FILTER_HIDDEN)),
        'c_f_skip': small(ks[20], (N_C_LAYERS, HYENA_ORDER, D), 0.5),
        'c_w_out': nrm(ks[21], (N_C_LAYERS, D, D), D),
        'f_w13': nrm(ks[22], (DEPTH_2, D, 2 * FFN_HIDDEN), D),
        'f_w2': nrm(ks[23], (DEPTH_2, FFN_HIDDEN, D), FFN_HIDDEN),
    }

def second_block(x, norm_mix_g, norm_ffn_g, a_w_in, a_conv_w, a_w_out,
              b_w_qkv, b_q_norm_g, b_k_norm_g, b_rpb, b_w_out,
              c_w_in, c_short_w, c_short_b, c_f_w1, c_f_b1, c_f_w2, c_f_b2,
              c_f_w3, c_f_freq, c_f_skip, c_w_out, f_w13, f_w2):
    ia = ib = ic = 0
    for i in range(DEPTH_2):
        h = rmsnorm(x, norm_mix_g[i])
        kind = i % N_MIXERS_2
        if kind == 0:
            y = short_conv_mixer(h, a_w_in[ia], a_conv_w[ia], a_w_out[ia])
            ia += 1
        elif kind == 1:
            y = neighborhood_attention(h, b_w_qkv[ib], b_q_norm_g[ib], b_k_norm_g[ib], b_rpb[ib], b_w_out[ib])
            ib += 1
        else:
            y = hyena_mixer(h, c_w_in[ic], c_short_w[ic], c_short_b[ic], c_f_w1[ic], c_f_b1[ic],
                            c_f_w2[ic], c_f_b2[ic], c_f_w3[ic], c_f_freq[ic], c_f_skip[ic], c_w_out[ic])
            ic += 1
        x = x + y
        x = x + swiglu(rmsnorm(x, norm_ffn_g[i]), f_w13[i], f_w2[i])
    return x


def setup_inputs(seed=0):
    out = dict(first_inputs(seed))
    for name, value in second_inputs(seed + 1).items():
        if name != "x":
            out[name + "_2"] = value
    return out


def reference(
    x, rwkv_mu, rwkv_w_rkv, rwkv_w0, rwkv_w1, rwkv_w2, rwkv_a0, rwkv_a1, rwkv_a2, rwkv_g1,
    rwkv_g2, rwkv_k_k, rwkv_k_a, rwkv_r_k, rwkv_gn_g, rwkv_gn_b, rwkv_w_o, moba_w_qkv, moba_w_o,
    ffn_w_in, ffn_w_down, ln_mix_g, ln_mix_b, ln_ffn_g, ln_ffn_b, norm_mix_g_2, norm_ffn_g_2,
    a_w_in_2, a_conv_w_2, a_w_out_2, b_w_qkv_2, b_q_norm_g_2, b_k_norm_g_2, b_rpb_2, b_w_out_2,
    c_w_in_2, c_short_w_2, c_short_b_2, c_f_w1_2, c_f_b1_2, c_f_w2_2, c_f_b2_2, c_f_w3_2,
    c_f_freq_2, c_f_skip_2, c_w_out_2, f_w13_2, f_w2_2,
):
    x = first_block(
        x, rwkv_mu, rwkv_w_rkv, rwkv_w0, rwkv_w1, rwkv_w2, rwkv_a0, rwkv_a1, rwkv_a2, rwkv_g1,
        rwkv_g2, rwkv_k_k, rwkv_k_a, rwkv_r_k, rwkv_gn_g, rwkv_gn_b, rwkv_w_o, moba_w_qkv,
        moba_w_o, ffn_w_in, ffn_w_down, ln_mix_g, ln_mix_b, ln_ffn_g, ln_ffn_b,
    )
    return second_block(
        x, norm_mix_g_2, norm_ffn_g_2, a_w_in_2, a_conv_w_2, a_w_out_2, b_w_qkv_2, b_q_norm_g_2,
        b_k_norm_g_2, b_rpb_2, b_w_out_2, c_w_in_2, c_short_w_2, c_short_b_2, c_f_w1_2,
        c_f_b1_2, c_f_w2_2, c_f_b2_2, c_f_w3_2, c_f_freq_2, c_f_skip_2, c_w_out_2, f_w13_2,
        f_w2_2,
    )


_drawn_inputs = setup_inputs


def setup_inputs(seed=0):
    import zlib

    import numpy as np

    out = dict(_drawn_inputs(seed))
    spreads = {}
    factors = {'rwkv_w1': 3.936,
     'rwkv_w2': 3.85,
     'rwkv_a0': 2.766,
     'rwkv_k_k': 3.86,
     'rwkv_gn_b': 5.739,
     'b_q_norm_g_2': 8.0,
     'b_k_norm_g_2': 8.0,
     'b_rpb_2': 36.557,
     'c_short_b_2': 6.875,
     'c_f_b1_2': 8.0,
     'c_f_b2_2': 8.0,
     'c_f_freq_2': 8.0}
    for name, (base, spread) in spreads.items():
        noise = np.random.default_rng([zlib.crc32(name.encode()), seed]).standard_normal(out[name].shape)
        drawn = base * np.exp(spread * noise) if base else spread * noise
        out[name] = __import__('jax').numpy.asarray(drawn.astype(out[name].dtype))
    for name, factor in factors.items():
        out[name] = (out[name] * factor).astype(out[name].dtype)
    return out
```

```python
from contextlib import ExitStack, contextmanager

import numpy as np

import concourse.bass as bass
from concourse import mybir

F32 = mybir.dt.float32
F32R = mybir.dt.float32r
BF16 = mybir.dt.bfloat16
U32 = mybir.dt.uint32
ALU = mybir.AluOpType
ACT = mybir.ActivationFunctionType
AX_X = mybir.AxisListType.X

P = 128
SEQ, D = 256, 1024
TT, KT = SEQ // P, D // P
HEADS, HD = 16, 64
PAIRS = HEADS // 2
FF = 2816
FK = FF // P
FB = FF // 256
SLOTS = 4
QW = 1024
LORA, GLORA = 64, 160
ALPHA = 4.0 ** 0.25
LN_EPS, RMS_EPS, GN_EPS = 1e-5, 1e-6, HD * 1e-5
DECAY = float(np.exp(-0.5))
LEVELS = (2, 4, 8, 16, 32, 64)
GROUP = 4
GRID_W, ROWS = 64, SEQ // 64
RPB_ROWS, RPB_COLS, RPB_PAD = 15, 31, 127
MAGIC = 1.5 * 2.0 ** 23
TWO_PI = 2.0 * np.pi
TWO_PI_HI = float(np.float32(TWO_PI))
TWO_PI_LO = float(TWO_PI - TWO_PI_HI)
PI_BELOW = 3.1415925
ORDER, BANDS, FHID = 2, 16, 64
EMB = 1 + 2 * BANDS
IN_Q, OUT_Q, FFN_Q = 3 * D // 512 * 4, KT, FB * 4 + FK
LAYERS = ("rwkv", "ffn", "moba", "ffn", "conv", "ffn", "near", "ffn", "hyena", "ffn", "conv", "ffn")
LAYER_NORMS = 4


class Tally:

    def __init__(self, engine):
        self.engine, self.count, self.inside = engine, {}, None

    def __call__(self, sem, n=1):
        self.count[sem.name] = self.count.get(sem.name, 0) + n
        if self.inside is None:
            return self.count[sem.name]
        i, each = self.inside
        return i * each[sem.name] + self.count[sem.name]

    @contextmanager
    def loop(self, times, each):
        each = {sem.name: n for sem, n in each.items()}
        before = dict(self.count)
        with self.engine.Fori(0, times) as i:
            self.inside = (i, each)
            yield i
            self.inside = None
        for name, n in self.count.items():
            assert n - before.get(name, 0) == each.get(name, 0), (name, n - before.get(name, 0))
        for name, n in each.items():
            self.count[name] = before.get(name, 0) + n * times


def program(nc, A, out, layers=LAYERS):
    ctx = ExitStack()
    quarters = sum(FFN_Q if kind == "ffn" else IN_Q + OUT_Q for kind in layers)

    def keep(name, shape, dtype=F32):
        return ctx.enter_context(nc.sbuf_tensor(name, shape, dtype))

    def sem(name):
        return ctx.enter_context(nc.semaphore(name))

    def scope(*tensors):
        with ExitStack() as s:
            return [s.enter_context(nc.sbuf_tensor(n, shape, (dtype or [F32])[0])) for n, shape, *dtype in tensors]

    X = keep("residual", [P, TT, D])
    raw = keep("w_raw", [P, SLOTS, QW])
    whi = keep("w_hi", [P, SLOTS, QW], F32R)
    wlo = keep("w_lo", [P, SLOTS, QW], F32R)
    ah = keep("operand_hi", [P, KT, SEQ], F32R)
    al = keep("operand_lo", [P, KT, SEQ], F32R)
    tok = keep("token_scratch", [P, TT, D])
    ident = keep("ident_sb", [P, P])
    identb = keep("identb_sb", [P, GROUP * P], BF16)
    gains = keep("gains_sb", [P, 8, KT])
    taps = keep("taps_sb", [P, 2, 3, KT])
    lng = keep("ln_gain", [P, D])
    lnb = keep("ln_bias", [P, D])
    half = keep("minus_half", [P, 32])
    stat = keep("stat", [P, 64])
    mom = keep("moments", [P, TT, 2])
    rstd = keep("rstd", [P, 32])
    acc = ctx.enter_context(nc.psum_tensor("acc", [P, 4, 512], F32))
    aux = ctx.enter_context(nc.psum_tensor("aux", [P, 4, 512], F32))

    with ExitStack() as s:
        def rwkv(name, shape, dtype=F32):
            return s.enter_context(nc.sbuf_tensor(name, shape, dtype))

        R, K, V = rwkv("r_rw", [P, TT, D]), rwkv("k_rw", [P, TT, D]), rwkv("v_rw", [P, TT, D])
        IC = rwkv("iclr_rw", [P, TT, D])
        KK = rwkv("kk_rw", [P, TT, D])
        DEC = rwkv("decay_rw", [P, TT, D])
        TMP = rwkv("tmp_rw", [P, TT, D])
        G2 = rwkv("g2_rw", [P, D])
        G2b = rwkv("g2b_rw", [GLORA - P, D])
        SG, SGb = rwkv("sg_rw", [P, SEQ]), rwkv("sgb_rw", [GLORA - P, SEQ])
        CUM = rwkv("cum_rw", [P, 2, P])
        SPAN = rwkv("span_rw", [P, TT])
        DCOL = rwkv("decay_col", [P, KT])
        LMASK = rwkv("level_masks", [P, len(LEVELS) + 2, P])
        STRICT = rwkv("strict_mask", [P, P])
        PICK = rwkv("pick_masks", [P, 2, P], U32)
        BONUS = rwkv("bonus_rw", [P, TT, HEADS])
        VEC, L1, L2, LW, LA, MU = scope(
            ("vec_rw", [P, 3, D]), ("l1_rw", [P, KT, 2 * LORA + GLORA]), ("l2_rw", [LORA + 1, 2, D]),
            ("lora_w", [LORA + 1, SEQ]), ("lora_a", [LORA + 1, SEQ]), ("mu_sb", [P, 6, KT]))
        ART, KTT, BTT, NM, INV, INVT, QM, AK, RB, RK, RHS, U, ST = scope(
            ("ar_turned", [P, 2, TT, 2, P]), ("k_turned", [P, GROUP, SEQ]), ("b_turned", [P, GROUP, SEQ]),
            ("n_rw", [P, TT, GROUP, P]), ("inv_rw", [P, TT, GROUP, P]), ("invt_rw", [P, TT, GROUP, P]),
            ("q_rw", [P, TT, GROUP, P]), ("ak_rw", [P, TT, GROUP, P]), ("rb_rw", [P, TT, GROUP, P]),
            ("rk_rw", [P, TT, GROUP, P]), ("rhs_rw", [P, GROUP * HD]), ("u_rw", [P, TT, GROUP * HD]),
            ("state_rw", [P, 2, 2, HD]))
    XT, XX = IC[:].rearrange("p t (k n) -> p (t k) n", n=SEQ), DEC[:].rearrange("p t (k n) -> p (t k) n", n=SEQ)
    MIX = [TMP[:].rearrange("p t (k n) -> p (t k) n", n=SEQ), KK[:].rearrange("p t (k n) -> p (t k) n", n=SEQ)]

    HH, HL, SILU, HM = scope(
        ("hidden_hi", [P, FK, SEQ], F32R), ("hidden_lo", [P, FK, SEQ], F32R),
        ("silu_ff", [P, 2, TT, 256]), ("hidden_ff", [P, 2, TT, 256]))
    QTOK, KTOK, VTOK, QT, KTT2, SC, PR, PT, SUMS, NMAX, RSUM, ROPE, ROT, CAUSAL, QG, BIAS, BMASK, FLIP = scope(
        ("q_at", [P, TT, D]), ("k_at", [P, TT, D]), ("v_at", [P, TT, D]), ("q_turned", [P, KT, SEQ]),
        ("k_turned_at", [P, KT, SEQ]), ("scores_at", [P, 2, TT, 2, SEQ]), ("probs_at", [P, 2, TT, 2, SEQ]),
        ("probs_turned", [P, 2, 2, TT, SEQ]), ("sums_at", [P, TT, HEADS]), ("nmax_at", [P, TT, HEADS]),
        ("rsum_at", [P, TT, HEADS]), ("rope_sb", [P, TT, 2, 2, HD]), ("rot_at", [P, TT, 512]),
        ("causal_sb", [P, P], BF16), ("qk_gain", [P, 3, HD]), ("bias_at", [P, TT, HEADS, SEQ]),
        ("bias_mask", [P, TT, SEQ]), ("flip_sb", [P, P]))
    OH, OL, CT, ZT, CV, YT = scope(
        ("conv_hi", [P, KT, SEQ], F32R), ("conv_lo", [P, KT, SEQ], F32R), ("c_conv", [P, KT, SEQ]),
        ("z_conv", [P, KT, SEQ]), ("conv_out", [P, KT, SEQ]), ("y_conv", [P, KT, SEQ]))
    HV, HX1, HX2, HF, FR, EO, WIN, SKIP, RN, DFT, IDFT, EMBT, FW, FW3, TAPS3, FCOL, H1, ARG, ONES = scope(
        ("v_hy", [P, TT, D]), ("x1_hy", [P, TT, D]), ("x2_hy", [P, TT, D]), ("filter_freq", [P, 5, D]),
        ("taps_or_freq", [P, 4, D]), ("even_odd", [P, 4, D]), ("window_sb", [P, TT, D]), ("skip_sb", [P, D]),
        ("norm_hy", [P, D]), ("dft_sb", [P, TT, 6, P]), ("idft_sb", [P, 4, SEQ]), ("emb_sb", [EMB, SEQ]),
        ("f_w12", [FHID, 2, FHID]), ("f_w3_sb", [FHID, 2 * D]), ("taps3_sb", [P, 4, 3 * KT]), ("f_cols", [FHID, 3]),
        ("hid_hy", [FHID, SEQ]), ("arg_hy", [FHID, 2, SEQ]), ("ones_sb", [P, P]))
    HCV = tok[:].rearrange("p b (k n) -> p b k n", n=SEQ)

    w_full = [sem(f"w_full{s}") for s in range(SLOTS)]
    w_hi = [sem(f"w_hi{s}") for s in range(SLOTS)]
    w_lo = [sem(f"w_lo{s}") for s in range(SLOTS)]
    w_used = [sem(f"w_used{s}") for s in range(SLOTS)]
    m = {n: sem(n) for n in (
        "x_in", "rwkv_in", "vec_in", "gn_in", "consts_in", "res_in", "ln_in", "moba_in", "causal_in", "near_in", "bias_in", "hyena_in", "hyena2_in",
        "halves_set", "presets", "ones_set", "identb_set", "causal_set", "bias_ready",
        "residual_done", "ms_ready", "rstd_ready", "token_ready", "turned", "hi_ready", "operand_ready", "dve_step",
        "mix_f_ready", "mix_ready", "rkv_done", "lora1_ready", "lora_mid", "lora2_ready", "lora_out", "cum_ready", "span_ready",
        "exp_ready", "scaled_ready",
        "group_turned", "group_copied", "pair_ready", "pair_masked", "pair2_ready", "level_ready", "level_masked", "level2_ready",
        "level_copied", "rhs_ready", "rhs_copied", "u_ready", "u_copied", "state_ready", "state_copied", "y_ready", "y_copied",
        "gate_ready",
        "silu_ready", "hidden_ready", "hidden_turned", "hidden_hi", "hidden_lo", "hidden_last",
        "in_done", "qk_square", "qk_summed", "qk_done", "qk_turned", "qk_copied", "scores_ready", "max_ready", "probs_ready",
        "probs_turned", "probs_copied_a", "probs_copied_v", "o_ready", "o_done",
        "c_done", "z_done", "y_done", "conv_hi_done", "conv_lo_done",
        "mlp_ready", "arg_ready", "mlp_done", "filt_ready", "filt_done", "filt_abs", "eo_ready", "norm_ready", "freq_ready", "freq_done",
        "cv_ready", "cv_turned", "cv_copied", "dft_ready", "dft_done", "idft_ready", "idft_done",
        "y_final", "out_written")}

    PE_PASSES = ((0, 0), (0, 1), (1, 0))
    W = (whi, wlo)

    def nth(q, at=None):
        n = q // SLOTS + 1
        return n if at is None else at[0] * (at[1] // SLOTS) + n

    start = {}
    total = 0
    for n, kind in enumerate(layers):
        start[n] = total
        total += FFN_Q if kind == "ffn" else IN_Q + OUT_Q

    block = ctx.enter_context(nc.Block())

    @block.sync
    def _(sp):
        sp.dma_start(XT, A["xT"]).then_inc(m["x_in"], 16)
        sp.dma_start(MU[:], A["mu"]).then_inc(m["x_in"], 16)
        for q in range(SLOTS):
            sp.dma_start(raw[:, q, :], A["weights"][q]).then_inc(w_full[q], 16)
            if q == 1:
                sp.dma_start(L1[:], A["lora1"]).then_inc(m["rwkv_in"], 16)
        rest = (quarters - SLOTS) // SLOTS
        with sp.Fori(0, rest) as i:
            for s in range(SLOTS):
                sp.wait_ge(w_lo[s], i + 1)
                sp.dma_start(raw[:, s, :], A["weights"][bass.ds(i * SLOTS + (SLOTS + s), 1)].rearrange("q p n -> (q p) n"))\
                  .then_inc(w_full[s], 16)
        for q in range((rest + 1) * SLOTS, quarters):
            sp.wait_ge(w_lo[q % SLOTS], nth(q) - 1)
            sp.dma_start(raw[:, q % SLOTS, :], A["weights"][q]).then_inc(w_full[q % SLOTS], 16)
        sp.wait_ge(m["y_final"], TT)
        sp.dma_start(out, X[:]).then_inc(m["out_written"], 16)
        sp.wait_ge(m["out_written"], 16)

    @block.tensor
    def _(pe):
        due = Tally(pe)

        def block_tokens(q, pair, at=None, operand_waits=False):
            for i in range(4):
                s = (q + i) % SLOTS
                if operand_waits:
                    pe.wait_ge(m["operand_ready"], due(m["operand_ready"]))
                pe.wait_ge(w_lo[s], nth(q + i, at))
                for kk in range(2):
                    kt = 2 * i + kk
                    for t in range(TT):
                        for x, w in PE_PASSES:
                            mm = pe.matmul(acc[:, 2 * pair + t, :], (ah, al)[x][:, kt, t * P:(t + 1) * P],
                                           W[w][:, s, kk * 512:(kk + 1) * 512],
                                           start=(kt == 0 and (x, w) == (0, 0)), stop=(kt == KT - 1 and (x, w) == (1, 0)))
                mm.then_inc(w_used[s], 1)

        def block_channels(q, pair, operand_waits=False):
            for i in range(4):
                s = (q + i) % SLOTS
                if operand_waits:
                    pe.wait_ge(m["operand_ready"], due(m["operand_ready"]))
                pe.wait_ge(w_lo[s], nth(q + i))
                for kk in range(2):
                    kt = 2 * i + kk
                    for c in range(4):
                        for x, w in PE_PASSES:
                            mm = pe.matmul(acc[:, 2 * pair + c // 2, (c % 2) * SEQ:(c % 2 + 1) * SEQ],
                                           W[w][:, s, kk * 512 + c * P:kk * 512 + (c + 1) * P], (ah, al)[x][:, kt, :],
                                           start=(kt == 0 and c % 2 == 0 and (x, w) == (0, 0)),
                                           stop=(kt == KT - 1 and c % 2 == 1 and (x, w) == (1, 0)), skip_group_check=True)
                mm.then_inc(w_used[s], 1)

        def project(q, tiles, hi, lo, ready, step, each=1):
            for kt in range(tiles):
                s = (q + kt) % SLOTS
                if kt % step == 0:
                    pe.wait_ge(ready, due(ready, each))
                pe.wait_ge(w_lo[s], nth(q + kt))
                for t in range(TT):
                    for c in range(2):
                        for x, w in PE_PASSES:
                            mm = pe.matmul(acc[:, 2 * t + c, :], (hi, lo)[x][:, kt, t * P:(t + 1) * P],
                                           W[w][:, s, c * 512:(c + 1) * 512],
                                           start=(kt == 0 and (x, w) == (0, 0)), stop=(kt == tiles - 1 and (x, w) == (1, 0)))
                mm.then_inc(w_used[s], 1)

        def turn_tile(dst, src, flipped=False):
            return pe.matmul(dst, src, FLIP[:], start=True, stop=True) if flipped else pe.transpose(dst, src, ident[:])

        def turn(src, at_once=False, flipped=False):
            for t in range(TT):
                if not at_once:
                    pe.wait_ge(m["token_ready"], due(m["token_ready"]))
                elif t == 0:
                    pe.wait_ge(m["token_ready"], due(m["token_ready"], TT))
                for kt in range(KT):
                    mm = turn_tile(aux[:, kt // 2, (kt % 2) * SEQ + t * P:(kt % 2) * SEQ + (t + 1) * P],
                                   src[:, t, kt * P:(kt + 1) * P], flipped)
                    if t == TT - 1 and kt % 2:
                        mm.then_inc(m["turned"], 1)

        def rwkv(q):
            def lora1(lo, hi, bank, src):
                for kt in range(KT):
                    mm = pe.matmul(aux[0:hi - lo, bank, 0:SEQ], L1[:, kt, lo:hi], src[:, kt, :],
                                   start=(kt == 0), stop=(kt == KT - 1))
                return mm

            def pair(q, first):
                for b in range(2):
                    if not first:
                        pe.wait_ge(m["rkv_done"], due(m["rkv_done"]))
                    block_tokens(q + 4 * b, b)

            pe.wait_ge(m["mix_ready"], due(m["mix_ready"]))
            pair(q, True)
            pe.wait_ge(m["rwkv_in"], due(m["rwkv_in"], 16))
            pe.wait_ge(m["mix_f_ready"], due(m["mix_f_ready"], 2))
            lora1(0, LORA, 0, MIX[1]).then_inc(m["lora1_ready"], 1)
            pe.wait_ge(m["mix_f_ready"], due(m["mix_f_ready"]))
            lora1(LORA, 2 * LORA, 1, MIX[0]).then_inc(m["lora1_ready"], 1)
            pe.wait_ge(m["mix_ready"], due(m["mix_ready"]))
            pair(q + 8, False)
            pe.wait_ge(m["mix_f_ready"], due(m["mix_f_ready"], 2))
            lora1(2 * LORA, 2 * LORA + P, 2, MIX[0])
            lora1(2 * LORA + P, 2 * LORA + GLORA, 3, MIX[0]).then_inc(m["lora1_ready"], 1)
            pe.wait_ge(m["mix_ready"], due(m["mix_ready"]))
            pair(q + 16, False)
            pe.wait_ge(m["vec_in"], due(m["vec_in"], 16 * 9))
            pe.wait_ge(m["consts_in"], due(m["consts_in"], 16 * 3))
            pe.wait_ge(m["identb_set"], due(m["identb_set"], GROUP))
            pe.wait_ge(m["lora_mid"], due(m["lora_mid"], 3))
            for t in range(TT):
                for c in range(2):
                    mm = pe.matmul(aux[:, 2 * t + c, :], LW[:, t * P:(t + 1) * P], L2[:, 0, c * 512:(c + 1) * 512], start=True, stop=True)
            mm.then_inc(m["lora2_ready"], 1)
            pe.wait_ge(m["rkv_done"], due(m["rkv_done"], 2))
            for t in range(TT):
                for c in range(2):
                    mm = pe.matmul(acc[:, 2 * t + c, :], LA[:, t * P:(t + 1) * P], L2[:, 1, c * 512:(c + 1) * 512], start=True, stop=True)
            mm.then_inc(m["lora2_ready"], 1)
            pe.wait_ge(m["lora_out"], due(m["lora_out"], 2))
            for t in range(TT):
                if t:
                    pe.wait_ge(m["exp_ready"], due(m["exp_ready"], 3))
                for e in range(2):
                    for c in range(2):
                        mm = pe.matmul(acc[:, 2 * e + c, :], CUM[:, e, :], DEC[:, t, c * 512:(c + 1) * 512], start=True, stop=True)
                mm.then_inc(m["cum_ready"], 1)
            for k in range(KT):
                for t in range(TT):
                    mm = pe.matmul(aux[:, 0, k:k + 1], DEC[:, t, k * P:(k + 1) * P], SPAN[:, t:t + 1], start=(t == 0), stop=(t == TT - 1))
            mm.then_inc(m["span_ready"], 1)
            pe.wait_ge(m["exp_ready"], due(m["exp_ready"], 4))
            pe.wait_ge(m["scaled_ready"], due(m["scaled_ready"], 1 + TT))
            bank = lambda c, b: (acc, aux)[c][:, b, :]
            for g in range(HEADS // GROUP):
                if g:
                    pe.wait_ge(m["y_copied"], due(m["y_copied"], TT))
                for n, src in enumerate((R, KK, K, IC)):
                    for k in range(2):
                        for t in range(TT):
                            mm = pe.transpose(aux[:, n, k * SEQ + t * P:k * SEQ + (t + 1) * P],
                                              src[:, t, (2 * g + k) * P:(2 * g + k + 1) * P], ident[:])
                    mm.then_inc(m["group_turned"], 1)
                pe.wait_ge(m["group_copied"], due(m["group_copied"], 4))
                for c in range(TT):
                    at = slice(c * P, (c + 1) * P)
                    for k in range(2):
                        mm = pe.matmul(bank(c, 0)[:, k * SEQ:(k + 1) * SEQ], ART[:, k, c, 0, :], BTT[:, 2 * k:2 * k + 2, at],
                                       start=True, stop=True, skip_group_check=True)
                    for h in range(GROUP):
                        mm = pe.matmul(bank(c, 1 + h // 2)[:, (h % 2) * SEQ:(h % 2 + 1) * SEQ], BTT[:, h, at],
                                       ART[:, h // 2, c, :, :], start=True, stop=True, skip_group_check=True)
                    mm.then_inc(m["pair_ready"], 1)
                for c in range(TT):
                    pe.wait_ge(m["pair_masked"], due(m["pair_masked"]))
                    at = slice(c * P, (c + 1) * P)
                    for h in range(GROUP):
                        mm = pe.matmul(bank(c, (3, 0)[h // 2])[:, (h % 2) * SEQ:(h % 2 + 1) * SEQ], KTT[:, h, at],
                                       ART[:, h // 2, c, :, :], start=True, stop=True, skip_group_check=True)
                    mm.then_inc(m["pair2_ready"], 1)
                for n, size in enumerate(LEVELS):
                    for c in range(TT):
                        if n == 0:
                            pe.wait_ge(m["pair_masked"], due(m["pair_masked"]))
                        else:
                            pe.wait_ge(m["level_copied"], due(m["level_copied"]))
                        pe.matmul(bank(c, 0), identb[:, 0:P], identb[:, :], start=True, stop=False, skip_group_check=True)
                        for h in range(GROUP):
                            mm = pe.matmul(bank(c, 0)[:, h * P:(h + 1) * P], NM[:, c, h, :], INVT[:, c, h, :],
                                           start=False, stop=(h == GROUP - 1), skip_group_check=True)
                        mm.then_inc(m["level_ready"], 1)
                    for c in range(TT):
                        pe.wait_ge(m["level_masked"], due(m["level_masked"]))
                        for h in range(GROUP):
                            mm = pe.matmul(bank(c, 1)[:, h * P:(h + 1) * P], INV[:, c, h, :], QM[:, c, h, :], start=True, stop=True,
                                           skip_group_check=True)
                            if n < len(LEVELS) - 1:
                                mm = pe.matmul(bank(c, 2)[:, h * P:(h + 1) * P], QM[:, c, h, :], INV[:, c, h, :], start=True, stop=True,
                                               skip_group_check=True)
                        mm.then_inc(m["level2_ready"], 1)
                pe.wait_ge(m["level_copied"], due(m["level_copied"], TT))
                for c in range(TT):
                    head = lambda h: slice((GROUP * g + h) * HD, (GROUP * g + h + 1) * HD)
                    if c:
                        pe.wait_ge(m["state_copied"], due(m["state_copied"], 4))
                    for h in range(GROUP):
                        own = slice(h * HD, (h + 1) * HD)
                        mm = pe.matmul(bank(c, 0)[:, own], AK[:, c, h, :], V[:, c, head(h)], start=(h == 0), stop=(c == 0 and h == GROUP - 1),
                                       skip_group_check=True)
                    if c:
                        for k in range(2):
                            mm = pe.matmul(bank(c, 0)[:, k * P:(k + 1) * P], ART[:, k, c, 0, :], ST[:, k], start=False, stop=(k == 1),
                                           skip_group_check=True)
                    mm.then_inc(m["rhs_ready"], 1)
                    pe.wait_ge(m["rhs_copied"], due(m["rhs_copied"]))
                    for h in range(GROUP):
                        own = slice(h * HD, (h + 1) * HD)
                        mm = pe.matmul(bank(c, 1)[:, own], INVT[:, c, h, :], RHS[:, own], start=True, stop=True, skip_group_check=True)
                    mm.then_inc(m["u_ready"], 1)
                    pe.wait_ge(m["u_copied"], due(m["u_copied"]))
                    if c == 0:
                        for k in range(2):
                            pr = slice((2 * g + k) * P, (2 * g + k + 1) * P)
                            pe.matmul(bank(c, 3)[:, k * P:(k + 1) * P], IC[:, c, pr], U[:, c, k * P:(k + 1) * P], start=True, stop=False,
                                      skip_group_check=True)
                            mm = pe.matmul(bank(c, 3)[:, k * P:(k + 1) * P], K[:, c, pr], V[:, c, pr], start=False, stop=True,
                                           skip_group_check=True)
                        mm.then_inc(m["state_ready"], 1)
                    for h in range(GROUP):
                        own = slice(h * HD, (h + 1) * HD)
                        pe.matmul(bank(c, 2)[:, own], RB[:, c, h, :], U[:, c, own], start=(h == 0), stop=False, skip_group_check=True)
                        mm = pe.matmul(bank(c, 2)[:, own], RK[:, c, h, :], V[:, c, head(h)], start=False, stop=(c == 0 and h == GROUP - 1),
                                       skip_group_check=True)
                    if c:
                        for k in range(2):
                            mm = pe.matmul(bank(c, 2)[:, k * P:(k + 1) * P], ART[:, k, c, 1, :], ST[:, k], start=False, stop=(k == 1),
                                           skip_group_check=True)
                    mm.then_inc(m["y_ready"], 1)
            pe.wait_ge(m["y_copied"], due(m["y_copied"], TT))
            for t in range(TT):
                for c in range(2):
                    cs = slice(c * 512, (c + 1) * 512)
                    pe.matmul(acc[:, 2 * t + c, :], SG[:, t * P:(t + 1) * P], G2[:, cs], start=True, stop=False)
                    mm = pe.matmul(acc[:, 2 * t + c, :], SGb[:, t * P:(t + 1) * P], G2b[:, cs], start=False, stop=True)
            mm.then_inc(m["gate_ready"], 1)
            turn(tok)
            project(q + IN_Q, KT, ah, al, m["operand_ready"], 2)

        def ffn(q, normed):
            def turn_hidden(odd, last=False):
                pe.wait_ge(m["hidden_ready"], due(m["hidden_ready"], TT))
                pe.wait_ge(m["hidden_lo"], due(m["hidden_lo"], 0) + 1 if last else due(m["hidden_lo"]))
                for kk in range(2):
                    for t in range(TT):
                        mm = pe.transpose(aux[:, odd, kk * SEQ + t * P:kk * SEQ + (t + 1) * P],
                                          HM[:, odd, t, kk * P:(kk + 1) * P], ident[:])
                mm.then_inc(m["hidden_turned"], 1)

            turn(tok if normed else X)
            block_tokens(q, 0, operand_waits=True)
            with due.loop((FB - 1) // 2, {m["hidden_ready"]: 2 * TT, m["hidden_lo"]: 2}) as i:
                for b in range(2):
                    block_tokens(q + 4 + 4 * b, 1 - b, at=(i, 8))
                    turn_hidden(b)
            turn_hidden(0, last=True)
            project(q + FB * 4, FK, HH, HL, m["hidden_last"], FK)

        def attention(q, near):
            if near:
                pe.wait_ge(m["near_in"], due(m["near_in"], 16 * 3))
            turn(tok if near else X)

            def turn_qk(src, flipped=False):
                for b in range(4):
                    for kk in range(2):
                        k = 2 * b + kk
                        for t in range(TT):
                            mm = turn_tile(aux[:, b, kk * SEQ + t * P:kk * SEQ + (t + 1) * P], src[:, t, k * P:(k + 1) * P], flipped)
                    mm.then_inc(m["qk_turned"], 1)

            for j in range(6):
                if j >= 2:
                    pe.wait_ge(m["in_done"], due(m["in_done"]))
                block_tokens(q + 4 * j, j % 2, operand_waits=(j == 0))
                if j == 4:
                    pe.wait_ge(m["qk_done"], due(m["qk_done"], 2))
                    turn_qk(QTOK, near)
            pe.wait_ge(m["qk_done"], due(m["qk_done"], 2))
            pe.wait_ge(m["qk_copied"], due(m["qk_copied"], 4))
            turn_qk(KTOK)
            pe.wait_ge(m["in_done"], due(m["in_done"], 2))
            pe.wait_ge(m["qk_copied"], due(m["qk_copied"], 4))
            if not near:
                pe.wait_ge(m["causal_set"], due(m["causal_set"]))

            def scores(p):
                for t in range(TT):
                    keys = SEQ if near else (t + 1) * P
                    for h in range(2):
                        of = slice(h * HD, (h + 1) * HD)
                        mm = pe.matmul(acc[:, 2 * (p % 2) + h, t * SEQ:t * SEQ + keys], QT[of, p, t * P:(t + 1) * P], KTT2[of, p, 0:keys],
                                       start=True, stop=near, skip_group_check=True)
                        if not near:
                            mm = pe.matmul(acc[:, 2 * (p % 2) + h, t * SEQ + t * P:t * SEQ + (t + 1) * P], identb[:, 0:P], CAUSAL[:],
                                           start=False, stop=True, skip_group_check=True)
                mm.then_inc(m["scores_ready"], 1)

            def turn_probs(p):
                pe.wait_ge(m["probs_ready"], due(m["probs_ready"], TT))
                if p:
                    pe.wait_ge(m["probs_copied_a"], due(m["probs_copied_a"]))
                    pe.wait_ge(m["probs_copied_v"], due(m["probs_copied_v"]))
                for h in range(2):
                    for t in range(TT):
                        for k in range(TT if near else t + 1):
                            mm = pe.transpose(aux[:, h, k * SEQ + t * P:k * SEQ + (t + 1) * P], PR[:, p % 2, t, h, k * P:(k + 1) * P], ident[:])
                    mm.then_inc(m["probs_turned"], 1)

            def values(p):
                if p >= 2:
                    pe.wait_ge(m["o_done"], due(m["o_done"]))
                for t in range(TT):
                    for h in range(2):
                        tiles = TT if near else t + 1
                        for k in range(tiles):
                            mm = pe.matmul(aux[:, 2 + p % 2, (t * 2 + h) * HD:(t * 2 + h + 1) * HD], PT[:, p % 2, h, k, t * P:(t + 1) * P],
                                           VTOK[:, k, (2 * p + h) * HD:(2 * p + h + 1) * HD], start=(k == 0), stop=(k == tiles - 1),
                                           skip_group_check=True)
                mm.then_inc(m["o_ready"], 1)

            scores(0)
            for p in range(PAIRS):
                if p + 1 < PAIRS:
                    scores(p + 1)
                turn_probs(p)
                if p:
                    values(p - 1)
            pe.wait_ge(m["probs_copied_a"], due(m["probs_copied_a"]))
            pe.wait_ge(m["probs_copied_v"], due(m["probs_copied_v"]))
            values(PAIRS - 1)
            turn(tok, at_once=True, flipped=near)
            project(q + IN_Q, KT, ah, al, m["operand_ready"], 2)

        def conv(q):
            turn(tok)
            for j in range(6):
                if j >= 2:
                    freed = m["c_done"] if j < 4 else m["z_done"]
                    pe.wait_ge(freed, due(freed))
                block_channels(q + 4 * j, j % 2, operand_waits=(j == 0))
            project(q + IN_Q, KT, OH, OL, m["conv_lo_done"], KT, 2)

        def hyena(q):
            turn(tok)
            pe.wait_ge(m["hyena_in"], due(m["hyena_in"], 16 * 10))
            pe.wait_ge(m["ones_set"], due(m["ones_set"]))

            def filters(n):
                for r in range(4):
                    t, d = r // 2, r % 2
                    if r >= 2:
                        pe.wait_ge(m["filt_done"], due(m["filt_done"]))
                    if n == 0 and r == 0:
                        pe.wait_ge(m["mlp_done"], due(m["mlp_done"]))
                    for c in range(2):
                        mm = pe.matmul(aux[:, 2 * d + c, :], H1[:, t * P:(t + 1) * P], FW3[:, d * D + c * 512:d * D + (c + 1) * 512],
                                       start=True, stop=True)
                    mm.then_inc(m["filt_ready"], 1)

            def spectrum(n):
                pe.wait_ge(m["filt_done"], due(m["filt_done"], 2))
                pe.wait_ge(m["filt_abs"], due(m["filt_abs"], 4))
                for c in range(2):
                    for k in range(4):
                        mm = pe.matmul(aux[:, c, :], ONES[:], FR[:, k, c * 512:(c + 1) * 512], start=(k == 0), stop=(k == 3))
                mm.then_inc(m["norm_ready"], 1)
                pe.wait_ge(m["eo_ready"], due(m["eo_ready"], TT))
                for r, (part, mats) in enumerate(((0, 0), (0, 1), (1, 4), (1, 3), (0, 5))):
                    if r >= 1:
                        pe.wait_ge(m["freq_done"], due(m["freq_done"]))
                    for c in range(2):
                        for t in range(TT):
                            mm = pe.matmul(aux[:, 2 * ((r + 1) % 2) + c, :], DFT[:, t, mats, :], EO[:, 2 * part + t, c * 512:(c + 1) * 512],
                                           start=(t == 0), stop=(t == TT - 1))
                    mm.then_inc(m["freq_ready"], 1)
                pe.wait_ge(m["freq_done"], due(m["freq_done"], 2))

            pe.wait_ge(m["operand_ready"], due(m["operand_ready"], 4))
            pe.matmul(aux[0:FHID, 0, 0:SEQ], FW[0:EMB, 0, :], EMBT[:], start=True, stop=True).then_inc(m["mlp_ready"], 1)
            pe.wait_ge(m["mlp_done"], due(m["mlp_done"]))
            pe.matmul(aux[0:FHID, 0, 0:SEQ], FW[:, 1, :], H1[:], start=True, stop=True).then_inc(m["mlp_ready"], 1)
            filters(0)
            spectrum(0)

            def turn_cv(j):
                pe.wait_ge(m["cv_ready"], due(m["cv_ready"]))
                if j >= 2:
                    pe.wait_ge(m["cv_copied"], due(m["cv_copied"]))
                for t in range(TT):
                    for c in range(4):
                        mm = pe.transpose(aux[:, 2 * (j % 2) + t, c * P:(c + 1) * P], HCV[:, j % 2, c, t * P:(t + 1) * P], ident[:])
                mm.then_inc(m["cv_turned"], 1)

            for j in range(6):
                block_channels(q + 4 * j, j % 2)
                if j:
                    turn_cv(j - 1)
            turn_cv(5)
            pe.wait_ge(m["cv_copied"], due(m["cv_copied"], 2))
            for n in range(ORDER):
                if n:
                    pe.wait_ge(m["hyena2_in"], due(m["hyena2_in"], 16 * 2))
                    filters(n)
                    spectrum(n)
                    pe.wait_ge(m["idft_done"], due(m["idft_done"]))
                for r in range(4):
                    f, c = r // 2, r % 2
                    if r >= 2:
                        pe.wait_ge(m["dft_done"], due(m["dft_done"]))
                    for part, mat in enumerate((f, 2 + f)):
                        for t in range(TT):
                            mm = pe.matmul(acc[:, 2 * (r % 2) + part, :], DFT[:, t, mat, :], HV[:, t, c * 512:(c + 1) * 512],
                                           start=(t == 0), stop=(t == TT - 1))
                    mm.then_inc(m["dft_ready"], 1)
                pe.wait_ge(m["dft_done"], due(m["dft_done"], 2))
                for t in range(TT):
                    for c in range(2):
                        for f in range(4):
                            mm = pe.matmul(acc[:, 2 * t + c, :], IDFT[:, f, t * P:(t + 1) * P], FR[:, f, c * 512:(c + 1) * 512],
                                           start=(f == 0), stop=(f == 3))
                mm.then_inc(m["idft_ready"], 1)
            turn(tok)
            project(q + IN_Q, KT, ah, al, m["operand_ready"], 2)

        for n, kind in enumerate(layers):
            {"rwkv": rwkv, "ffn": lambda q: ffn(q, n > LAYER_NORMS), "moba": lambda q: attention(q, False), "near": lambda q: attention(q, True),
             "conv": conv, "hyena": hyena}[kind](start[n])

    @block.scalar
    def _(act):
        due = Tally(act)

        def split(q, at=None):
            s = q % SLOTS
            act.wait_ge(w_full[s], 16 * nth(q) if at is None else at[0] * (16 * at[1] // SLOTS) + 16 * nth(q))
            if q >= SLOTS:
                act.wait_ge(w_used[s], nth(q - SLOTS, at))
            act.activation(whi[:, s, :], raw[:, s, :], ACT.Copy).then_inc(w_hi[s], 1)

        def ahead(q, n, at=None):
            for k in range(n):
                if q + k + SLOTS < quarters:
                    split(q + k + SLOTS, at)

        def step(instruction):
            instruction.then_inc(m["act_step"], 1)
            act.wait_ge(m["act_step"], due(m["act_step"]))

        def operand(gain=None):
            for b in range(4):
                act.wait_ge(m["turned"], due(m["turned"]))
                if gain is None:
                    last = act.activation(ah[:, 2 * b:2 * b + 2, :], aux[:, b, :], ACT.Copy)
                else:
                    for k in range(2):
                        last = act.activation(ah[:, 2 * b + k, :], aux[:, b, k * SEQ:(k + 1) * SEQ], ACT.Copy,
                                              scale=gains[:, gain, 2 * b + k:2 * b + k + 1])
                last.then_inc(m["hi_ready"], 1)

        def rwkv(q):
            def mixed(n):
                act.wait_ge(m["mix_f_ready"], due(m["mix_f_ready"]))
                act.activation(ah[:], MIX[n], ACT.Copy).then_inc(m["hi_ready"], 1)

            def copy_out(dst, c, s, q):
                act.wait_ge(w_used[s], nth(q))
                for t in range(TT):
                    last = act.activation(dst[:, t, c * 512:(c + 1) * 512], acc[:, 2 * c + t, :], ACT.Copy)
                last.then_inc(m["rkv_done"], 1)

            def project_out(dst, q):
                for c in range(2):
                    ahead(q + 4 * c, 4)
                    copy_out(dst, c, (q + 4 * c + 3) % SLOTS, q + 4 * c + 3)

            for k in range(SLOTS):
                split(q + k)
            act.wait_ge(m["mix_f_ready"], due(m["mix_f_ready"]))
            act.activation(ah[:], MIX[0], ACT.Copy).then_inc(m["hi_ready"], 1)
            project_out(R, q)
            act.wait_ge(m["halves_set"], due(m["halves_set"], 3))
            act.wait_ge(m["lora1_ready"], due(m["lora1_ready"]))
            act.activation(LW[0:LORA, :], aux[0:LORA, 0, 0:SEQ], ACT.Tanh).then_inc(m["lora_mid"], 1)
            act.wait_ge(m["mix_f_ready"], due(m["mix_f_ready"], 3))
            act.activation(ah[:], MIX[1], ACT.Copy).then_inc(m["hi_ready"], 1)
            act.wait_ge(m["lora1_ready"], due(m["lora1_ready"]))
            act.activation(LA[0:LORA, :], aux[0:LORA, 1, 0:SEQ], ACT.Copy).then_inc(m["lora_mid"], 1)
            project_out(K, q + 8)
            act.wait_ge(m["lora1_ready"], due(m["lora1_ready"]))
            act.activation(SG[:], aux[:, 2, 0:SEQ], ACT.Sigmoid)
            act.activation(SGb[:], aux[0:GLORA - P, 3, 0:SEQ], ACT.Sigmoid).then_inc(m["lora_mid"], 1)
            act.wait_ge(m["mix_f_ready"], due(m["mix_f_ready"], 2))
            act.activation(ah[:], MIX[1], ACT.Copy).then_inc(m["hi_ready"], 1)
            project_out(V, q + 16)
            for dst, src in ((DEC, aux), (IC, acc)):
                act.wait_ge(m["lora2_ready"], due(m["lora2_ready"]))
                for t in range(TT):
                    for c in range(2):
                        last = act.activation(dst[:, t, c * 512:(c + 1) * 512], src[:, 2 * t + c, :], ACT.Sigmoid)
                last.then_inc(m["lora_out"], 1)
            for t in range(TT):
                act.wait_ge(m["cum_ready"], due(m["cum_ready"]))
                act.wait_ge(m["scaled_ready"], due(m["scaled_ready"]))
                for dst, b, sign in ((TMP[:, 0, :], 0, 1.0), (TMP[:, 1, :], 0, -1.0), (tok[:, 0, :], 2, 1.0)):
                    act.activation(dst.rearrange("p (c n) -> p c n", c=2), acc[:, b:b + 2, :], ACT.Exp, scale=sign).then_inc(m["exp_ready"], 1)
            act.wait_ge(m["span_ready"], due(m["span_ready"]))
            act.activation(DCOL[:], aux[:, 0, 0:KT], ACT.Exp).then_inc(m["exp_ready"], 1)
            bank = lambda c, b: (acc, aux)[c][:, b, :]
            for g in range(HEADS // GROUP):
                for n in range(2):
                    act.wait_ge(m["group_turned"], due(m["group_turned"]))
                    act.activation(ART[:, :, :, 1 - n, :], aux[:, n, :].rearrange("p (k t n) -> p k t n", k=2, t=TT), ACT.Copy)\
                       .then_inc(m["group_copied"], 1)
                due(m["group_turned"], 2)
                for n in range(len(LEVELS)):
                    for c in range(TT):
                        act.wait_ge(m["level2_ready"], due(m["level2_ready"]))
                        last = act.activation(INVT[:, c], bank(c, 1), ACT.Copy)
                        if n < len(LEVELS) - 1:
                            last = act.activation(INV[:, c], bank(c, 2), ACT.Copy)
                        last.then_inc(m["level_copied"], 1)
                for c in range(TT):
                    act.wait_ge(m["rhs_ready"], due(m["rhs_ready"]))
                    act.activation(RHS[:], bank(c, 0)[:, 0:GROUP * HD], ACT.Copy).then_inc(m["rhs_copied"], 1)
                    act.wait_ge(m["u_ready"], due(m["u_ready"]))
                    act.activation(U[:, c, :], bank(c, 1)[:, 0:GROUP * HD], ACT.Copy).then_inc(m["u_copied"], 1)
                    act.wait_ge(m["y_ready"], due(m["y_ready"]))
                    act.activation(tok[:, c, g * GROUP * HD:(g + 1) * GROUP * HD], bank(c, 2)[:, 0:GROUP * HD], ACT.Copy)\
                       .then_inc(m["y_copied"], 1)
            operand()
            ahead(q + IN_Q, OUT_Q)

        def ffn(q, gain):
            operand(gain)

            def silu(q, odd, pair, at=None):
                act.wait_ge(w_used[(q + 3) % SLOTS], nth(q + 3, at))
                for t in range(TT):
                    last = act.activation(SILU[:, odd, t, :], acc[:, 2 * pair + t, 0:256], ACT.Silu)
                last.then_inc(m["silu_ready"], 1)

            def hidden_hi(dst, odd):
                act.wait_ge(m["hidden_turned"], due(m["hidden_turned"]))
                act.activation(dst, aux[:, odd, :].rearrange("p (k n) -> p k n", k=2), ACT.Copy).then_inc(m["hidden_hi"], 1)

            ahead(q, 4)
            silu(q, 0, 0)
            with due.loop((FB - 1) // 2, {m["hidden_turned"]: 2}) as i:
                for b in range(2):
                    ahead(q + 4 + 4 * b, 4, (i, 8))
                    silu(q + 4 + 4 * b, 1 - b, 1 - b, (i, 8))
                    hidden_hi(HH[:, bass.ds(i * 4 + 2 * b, 2), :], b)
            hidden_hi(HH[:, FK - 2:FK, :], 0)
            ahead(q + FB * 4, FK)

        def attention(q, near, gain):
            operand(gain)
            for j in range(6):
                ahead(q + 4 * j, 4)
                if near and j < 4:
                    act.wait_ge(w_used[(q + 4 * j + 3) % SLOTS], nth(q + 4 * j + 3))
                    dst = (QTOK, KTOK)[j // 2]
                    act.activation(dst[:, :, (j % 2) * 512:(j % 2 + 1) * 512], acc[:, 2 * (j % 2):2 * (j % 2) + 2, :], ACT.Copy)
                    if j:
                        act.wait_ge(m["qk_summed"], due(m["qk_summed"]))
                    act.activation(ROT[:], acc[:, 2 * (j % 2):2 * (j % 2) + 2, :], ACT.Square).then_inc(m["qk_square"], 1)
                if j == 4:
                    for b in range(4):
                        act.wait_ge(m["qk_turned"], due(m["qk_turned"]))
                        act.activation(QT[:, 2 * b:2 * b + 2, :], aux[:, b, :], ACT.Copy).then_inc(m["qk_copied"], 1)
            for b in range(4):
                act.wait_ge(m["qk_turned"], due(m["qk_turned"]))
                act.activation(KTT2[:, 2 * b:2 * b + 2, :], aux[:, b, :], ACT.Copy).then_inc(m["qk_copied"], 1)

            def copy_probs(p):
                act.wait_ge(m["probs_turned"], due(m["probs_turned"]))
                if near:
                    act.activation(PT[:, p % 2, 0], aux[:, 0, :], ACT.Copy).then_inc(m["probs_copied_a"], 1)
                else:
                    act.activation(PT[:, p % 2, 0, 0, :], aux[:, 0, 0:SEQ], ACT.Copy)
                    act.activation(PT[:, p % 2, 0, 1, P:SEQ], aux[:, 0, SEQ + P:2 * SEQ], ACT.Copy).then_inc(m["probs_copied_a"], 1)
                due(m["probs_turned"])

            for p in range(PAIRS):
                act.wait_ge(m["max_ready"], due(m["max_ready"]))
                for t in range(TT):
                    keys = SEQ if near else (t + 1) * P
                    for h in range(2):
                        src = SC[:, p % 2, t, h, :] if near else acc[:, 2 * (p % 2) + h, t * SEQ:t * SEQ + keys]
                        last = act.activation(PR[:, p % 2, t, h, 0:keys], src, ACT.Exp, bias=NMAX[:, t, 2 * p + h:2 * p + h + 1],
                                              accum_out=SUMS[:, t, 2 * p + h:2 * p + h + 1])
                    last.then_inc(m["probs_ready"], 1)
                if p:
                    copy_probs(p - 1)
            copy_probs(PAIRS - 1)
            operand()
            ahead(q + IN_Q, OUT_Q)

        def conv(q, gain):
            operand(gain)
            for j in range(6):
                ahead(q + 4 * j, 4)
                if j < 2:
                    act.wait_ge(w_used[(q + 4 * j + 3) % SLOTS], nth(q + 4 * j + 3))
                    act.activation(CT[:, 4 * j:4 * j + 4, :].rearrange("p (b k) n -> p b (k n)", b=2), acc[:, 2 * j:2 * j + 2, :], ACT.Copy)\
                       .then_inc(m["c_done"], 1)
                if j >= 4:
                    act.wait_ge(m["y_done"], due(m["y_done"]))
                    act.activation(OH[:, 4 * (j - 4):4 * (j - 3), :], YT[:, 4 * (j - 4):4 * (j - 3), :], ACT.Copy).then_inc(m["conv_hi_done"], 1)
            ahead(q + IN_Q, OUT_Q)

        def hyena(q, gain):
            operand(gain)

            def absolute():
                act.wait_ge(m["eo_ready"], due(m["eo_ready"], TT))
                for k in range(4):
                    act.activation(FR[:, k, :], FR[:, k, :], ACT.Abs).then_inc(m["filt_abs"], 1)

            for _ in range(2):
                act.wait_ge(m["arg_ready"], due(m["arg_ready"]))
                act.activation(H1[:], ARG[:, 0, :], ACT.Sin).then_inc(m["mlp_done"], 1)
            absolute()
            for j in range(6):
                ahead(q + 4 * j, 4)
                if j:
                    act.wait_ge(m["cv_turned"], due(m["cv_turned"]))
                    dst, c = (HV, HX1, HX2)[(j - 1) // 2], (j - 1) % 2
                    act.activation(dst[:, :, c * 512:(c + 1) * 512], aux[:, 2 * ((j - 1) % 2):2 * ((j - 1) % 2) + 2, :], ACT.Copy).then_inc(m["cv_copied"], 1)
            act.wait_ge(m["cv_turned"], due(m["cv_turned"]))
            act.activation(HX2[:, :, 512:D], aux[:, 2:4, :], ACT.Copy).then_inc(m["cv_copied"], 1)
            absolute()
            operand()
            ahead(q + IN_Q, OUT_Q)

        for n, kind in enumerate(layers):
            gain = n - LAYER_NORMS if n >= LAYER_NORMS else None
            {"rwkv": lambda q, g: rwkv(q), "ffn": ffn, "moba": lambda q, g: attention(q, False, g),
             "near": lambda q, g: attention(q, True, g), "conv": conv, "hyena": hyena}[kind](start[n], gain)

    @block.vector
    def _(dve):
        due = Tally(dve)

        def split(q, at=None):
            s = q % SLOTS
            dve.wait_ge(w_hi[s], nth(q, at))
            dve.tensor_tensor(wlo[:, s, :], raw[:, s, :], whi[:, s, :].bitcast(F32), ALU.subtract).then_inc(w_lo[s], 1)

        def ahead(q, n, at=None):
            for k in range(n):
                if q + k + SLOTS < quarters:
                    split(q + k + SLOTS, at)

        def used(q, at=None):
            dve.wait_ge(w_used[q % SLOTS], nth(q, at))

        def step(instruction):
            instruction.then_inc(m["dve_step"], 1)
            dve.wait_ge(m["dve_step"], due(m["dve_step"]))

        def operand(gain=None):
            for b in range(4):
                dve.wait_ge(m["hi_ready"], due(m["hi_ready"]))
                if gain is None:
                    last = dve.tensor_tensor(al[:, 2 * b:2 * b + 2, :], aux[:, b, :].rearrange("p (k n) -> p k n", k=2),
                                             ah[:, 2 * b:2 * b + 2, :].bitcast(F32), ALU.subtract)
                else:
                    for k in range(2):
                        last = dve.scalar_tensor_tensor(out=al[:, 2 * b + k, :], in0=aux[:, b, k * SEQ:(k + 1) * SEQ],
                                                        scalar=gains[:, gain, 2 * b + k:2 * b + k + 1],
                                                        in1=ah[:, 2 * b + k, :].bitcast(F32), op0=ALU.mult, op1=ALU.subtract)
                last.then_inc(m["operand_ready"], 1)

        def wide(v, shape, axis):
            return v.unsqueeze(axis).to_broadcast(shape)

        def by_head(x):
            return x.rearrange("p t (h d) -> p (t h) d", d=HD)

        def residual(n, q):
            used(q - 1)
            last_layer = n == len(layers) - 1
            layer_norm = n < LAYER_NORMS
            if n == 0:
                dve.wait_ge(m["res_in"], due(m["res_in"], 16))
            for t in range(TT):
                cols = X[:, t, :].rearrange("p (c n) -> p c n", c=2)
                if layer_norm:
                    add = dve.scalar_tensor_tensor(out=cols, in0=cols, scalar=ALPHA, in1=acc[:, 2 * t:2 * t + 2, :], op0=ALU.mult, op1=ALU.add)
                else:
                    add = dve.tensor_tensor(cols, cols, acc[:, 2 * t:2 * t + 2, :], ALU.add)
                add.then_inc(m["y_final"] if last_layer and not layer_norm else m["residual_done"], 1)
            if layer_norm:
                for t in range(TT):
                    dve.wait_ge(m["residual_done"], due(m["residual_done"]))
                    for c in range(2):
                        last = dve.bn_stats(stat[:, 32 + 12 * t + 6 * c:38 + 12 * t + 6 * c], X[:, t, c * 512:(c + 1) * 512])
                step(last)
                for t in range(TT):
                    last = dve.bn_aggr(mom[:, t, :], stat[:, 32 + 12 * t:44 + 12 * t])
                step(last)
                dve.tensor_scalar(stat[:, 0:TT], mom[:, :, 1], LN_EPS, None, ALU.add).then_inc(m["ms_ready"], 1)
                dve.wait_ge(m["rstd_ready"], due(m["rstd_ready"]))
                dve.wait_ge(m["ln_in"], due(m["ln_in"], 32))
                for t in range(TT):
                    step(dve.tensor_scalar(X[:, t, :], X[:, t, :], mom[:, t, 0:1], rstd[:, t:t + 1], ALU.subtract, ALU.mult))
                    step(dve.tensor_tensor(X[:, t, :], X[:, t, :], lng[:], ALU.mult))
                    add = dve.tensor_tensor(X[:, t, :], X[:, t, :], lnb[:], ALU.add)
                    if last_layer:
                        add.then_inc(m["y_final"], 1)
                    elif n < LAYER_NORMS - 1:
                        add.then_inc(m["token_ready"], 1)
                    else:
                        step(add)
            if n >= LAYER_NORMS - 1 and not last_layer:
                for t in range(TT):
                    if not layer_norm:
                        dve.wait_ge(m["residual_done"], due(m["residual_done"]))
                    last = dve.tensor_tensor_reduce(out=tok[:, t, :], in0=X[:, t, :], in1=X[:, t, :], scale=1.0, scalar=0.0, op0=ALU.mult,
                                                    op1=ALU.add, accum_out=stat[:, 56 + t:57 + t])
                step(last)
                dve.tensor_scalar(stat[:, 0:TT], stat[:, 56:56 + TT], 1.0 / D, RMS_EPS, ALU.mult, ALU.add).then_inc(m["ms_ready"], 1)
                dve.wait_ge(m["rstd_ready"], due(m["rstd_ready"]))
                for t in range(TT):
                    dve.tensor_scalar(tok[:, t, :], X[:, t, :], rstd[:, t:t + 1], None, ALU.mult).then_inc(m["token_ready"], 1)

        def rwkv(q, gain):
            def mix(n, dst):
                for k in range(KT):
                    last = dve.scalar_tensor_tensor(out=MIX[dst][:, k, :], in0=XX[:, k, :], scalar=MU[:, n, k:k + 1], in1=XT[:, k, :],
                                                    op0=ALU.mult, op1=ALU.add)
                last.then_inc(m["mix_f_ready"], 1)

            def mix_lo(src):
                dve.wait_ge(m["hi_ready"], due(m["hi_ready"]))
                dve.tensor_tensor(al[:], MIX[src], ah[:].bitcast(F32), ALU.subtract).then_inc(m["mix_ready"], 1)
                dve.wait_ge(m["mix_ready"], due(m["mix_ready"]))

            dve.wait_ge(m["x_in"], due(m["x_in"], 32))
            dve.tensor_tensor(XX[:, :, 1:SEQ], XT[:, :, 0:SEQ - 1], XT[:, :, 1:SEQ], ALU.subtract)
            step(dve.tensor_scalar(XX[:, :, 0:1], XT[:, :, 0:1], -1.0, None, ALU.mult))
            mix(0, 0)
            for k in range(SLOTS):
                split(q + k)
            mix_lo(0)
            mix(1, 1)
            mix(4, 0)
            ahead(q, 8)
            dve.wait_ge(m["lora1_ready"], due(m["lora1_ready"]))
            mix(2, 1)
            mix_lo(1)
            dve.wait_ge(m["lora1_ready"], due(m["lora1_ready"]))
            mix(5, 0)
            ahead(q + 8, 8)
            mix(3, 1)
            mix_lo(1)
            ahead(q + 16, 8)
            dve.wait_ge(m["lora1_ready"], due(m["lora1_ready"]))
            dve.wait_ge(m["vec_in"], due(m["vec_in"], 16 * 9))
            dve.wait_ge(m["rkv_done"], due(m["rkv_done"], 6))
            vec = lambda n: wide(VEC[:, n, :], [P, TT, D], 1)
            step(dve.tensor_tensor(KK[:], K[:], vec(0), ALU.mult))
            step(dve.tensor_tensor(TMP[:], KK[:], KK[:], ALU.mult))
            step(dve.tensor_reduce(stat[:, 0:32], by_head(TMP[:]), AX_X, ALU.add))
            dve.tensor_scalar(stat[:, 0:32], stat[:, 0:32], 1e-24, None, ALU.max).then_inc(m["ms_ready"], 1)
            dve.wait_ge(m["lora_out"], due(m["lora_out"], 2))
            step(dve.scalar_tensor_tensor(out=tok[:], in0=IC[:], scalar=-1.0, in1=vec(1), op0=ALU.add, op1=ALU.mult))
            step(dve.scalar_tensor_tensor(out=K[:], in0=tok[:], scalar=1.0, in1=K[:], op0=ALU.add, op1=ALU.mult))
            step(dve.tensor_tensor(TMP[:], R[:], K[:], ALU.mult))
            step(dve.tensor_tensor(TMP[:], TMP[:], vec(2), ALU.mult))
            dve.tensor_reduce(BONUS[:].rearrange("p t h -> p (t h)"), by_head(TMP[:]), AX_X, ALU.add)
            dve.wait_ge(m["rstd_ready"], due(m["rstd_ready"]))
            step(dve.tensor_tensor(by_head(KK[:]), by_head(KK[:]), wide(rstd[:], [P, TT * HEADS, HD], 2), ALU.mult))
            dve.tensor_tensor(IC[:], KK[:], IC[:], ALU.mult).then_inc(m["scaled_ready"], 1)
            dve.wait_ge(m["scaled_ready"], due(m["scaled_ready"]))
            for t in range(TT):
                dve.wait_ge(m["exp_ready"], due(m["exp_ready"], 3))
                dve.tensor_tensor(R[:, t, :], R[:, t, :], TMP[:, 0, :], ALU.mult)
                dve.tensor_tensor(K[:, t, :], K[:, t, :], TMP[:, 1, :], ALU.mult)
                dve.tensor_tensor(IC[:, t, :], IC[:, t, :], TMP[:, 1, :], ALU.mult)
                dve.scalar_tensor_tensor(out=KK[:, t, :], in0=KK[:, t, :], scalar=-1.0, in1=tok[:, 0, :], op0=ALU.mult, op1=ALU.mult)\
                   .then_inc(m["scaled_ready"], 1)
            due(m["scaled_ready"], TT)
            dve.wait_ge(m["exp_ready"], due(m["exp_ready"]))
            dve.wait_ge(m["presets"], due(m["presets"], 6))
            bank = lambda c, b: (acc, aux)[c][:, b, :]
            heads4 = lambda v: wide(v, [P, GROUP, P], 1)
            heads2 = lambda v: wide(v, [P, 2, P], 1)
            for g in range(HEADS // GROUP):
                for n, dst in enumerate((KTT, BTT)):
                    dve.wait_ge(m["group_turned"], due(m["group_turned"], 3 - 2 * n))
                    for e in range(2):
                        of = slice(e * HD, (e + 1) * HD)
                        last = dve.tensor_copy(dst[of, e:GROUP:2, :], aux[of, 2 + n, :].rearrange("p (k n) -> p k n", k=2))
                    last.then_inc(m["group_copied"], 1)
                for c in range(TT):
                    dve.wait_ge(m["pair_ready"], due(m["pair_ready"]))
                    one = bank(c, 0).rearrange("p (h n) -> p h n", h=GROUP)
                    dve.tensor_tensor(NM[:, c], one, heads4(STRICT[:]), ALU.mult)
                    dve.tensor_tensor(INV[:, c], one, heads4(LMASK[:, 0, :]), ALU.mult)
                    for k in range(2):
                        two = bank(c, 1 + k).rearrange("p (h x n) -> p h x n", h=2, x=2)
                        dve.tensor_tensor(INVT[:, c, 2 * k:2 * k + 2, :], two[:, :, 0, :], heads2(LMASK[:, 1, :]), ALU.mult)
                        last = dve.copy_predicated(RB[:, c, 2 * k:2 * k + 2, :], heads2(PICK[:, 1, :]), two[:, :, 1, :])
                    step(last)
                    dve.tensor_tensor(INV[:, c], INV[:, c], heads4(ident[:]), ALU.add)
                    dve.tensor_tensor(INVT[:, c], INVT[:, c], heads4(ident[:]), ALU.add).then_inc(m["pair_masked"], 1)
                for c in range(TT):
                    dve.wait_ge(m["pair2_ready"], due(m["pair2_ready"]))
                    for k in range(2):
                        two = bank(c, (3, 0)[k]).rearrange("p (h x n) -> p h x n", h=2, x=2)
                        dve.copy_predicated(AK[:, c, 2 * k:2 * k + 2, :], heads2(PICK[:, 0, :]), two[:, :, 0, :])
                        last = dve.copy_predicated(RK[:, c, 2 * k:2 * k + 2, :], heads2(PICK[:, 1, :]), two[:, :, 1, :])
                    last.then_inc(m["pair_masked"], 1)
                for n in range(len(LEVELS)):
                    for c in range(TT):
                        dve.wait_ge(m["level_ready"], due(m["level_ready"]))
                        dve.tensor_tensor(QM[:, c], bank(c, 0).rearrange("p (h n) -> p h n", h=GROUP), heads4(LMASK[:, 2 + n, :]), ALU.mult)\
                           .then_inc(m["level_masked"], 1)
                dve.wait_ge(m["state_ready"], due(m["state_ready"]))
                for k in range(2):
                    for h in range(2):
                        of = slice(h * HD, (h + 1) * HD)
                        dve.tensor_scalar(ST[of, k, h, :], bank(0, 3)[of, k * P + h * HD:k * P + (h + 1) * HD], DCOL[of, 2 * g + k:2 * g + k + 1], None,
                                          ALU.mult).then_inc(m["state_copied"], 1)
            GN = DEC
            dve.wait_ge(m["y_copied"], due(m["y_copied"], TT * HEADS // GROUP))
            dve.wait_ge(m["gn_in"], due(m["gn_in"], 32))
            per_head = lambda v: wide(v, [P, TT * HEADS, HD], 2)
            step(dve.tensor_reduce(stat[:, 0:32], by_head(tok[:]), AX_X, ALU.add))
            step(dve.tensor_scalar(stat[:, 0:32], stat[:, 0:32], 1.0 / HD, None, ALU.mult))
            step(dve.tensor_tensor(by_head(tok[:]), by_head(tok[:]), per_head(stat[:, 0:32]), ALU.subtract))
            step(dve.tensor_tensor(TMP[:], tok[:], tok[:], ALU.mult))
            step(dve.tensor_reduce(stat[:, 0:32], by_head(TMP[:]), AX_X, ALU.add))
            dve.tensor_scalar(stat[:, 0:32], stat[:, 0:32], 1.0 / HD, GN_EPS, ALU.mult, ALU.add).then_inc(m["ms_ready"], 1)
            step(dve.tensor_tensor(by_head(IC[:]), by_head(V[:]), per_head(BONUS[:].rearrange("p t h -> p (t h)")), ALU.mult))
            step(dve.tensor_tensor(IC[:], IC[:], wide(GN[:, 1, :], [P, TT, D], 1), ALU.add))
            dve.wait_ge(m["rstd_ready"], due(m["rstd_ready"]))
            step(dve.tensor_tensor(by_head(tok[:]), by_head(tok[:]), per_head(rstd[:]), ALU.mult))
            step(dve.tensor_tensor(tok[:], tok[:], wide(GN[:, 0, :], [P, TT, D], 1), ALU.mult))
            step(dve.tensor_tensor(tok[:], tok[:], IC[:], ALU.add))
            dve.wait_ge(m["gate_ready"], due(m["gate_ready"]))
            for t in range(TT):
                cols = tok[:, t, :].rearrange("p (c n) -> p c n", c=2)
                dve.tensor_tensor(cols, cols, acc[:, 2 * t:2 * t + 2, :], ALU.mult).then_inc(m["token_ready"], 1)
            operand()
            ahead(q + IN_Q, OUT_Q)

        def ffn(q, gain):
            operand(gain)

            def hidden(odd, pair):
                dve.wait_ge(m["silu_ready"], due(m["silu_ready"]))
                for t in range(TT):
                    dve.tensor_tensor(HM[:, odd, t, :], SILU[:, odd, t, :], acc[:, 2 * pair + t, 256:512], ALU.mult).then_inc(m["hidden_ready"], 1)

            def hidden_lo(dst, src_hi, odd, done):
                dve.wait_ge(m["hidden_hi"], due(m["hidden_hi"]))
                dve.tensor_tensor(dst, aux[:, odd, :].rearrange("p (k n) -> p k n", k=2), src_hi.bitcast(F32), ALU.subtract).then_inc(done, 1)

            ahead(q, 4)
            hidden(0, 0)
            with due.loop((FB - 1) // 2, {m["silu_ready"]: 2, m["hidden_hi"]: 2}) as i:
                for b in range(2):
                    ahead(q + 4 + 4 * b, 4, (i, 8))
                    hidden(1 - b, 1 - b)
                    ks = bass.ds(i * 4 + 2 * b, 2)
                    hidden_lo(HL[:, ks, :], HH[:, ks, :], b, m["hidden_lo"])
            hidden_lo(HL[:, FK - 2:FK, :], HH[:, FK - 2:FK, :], 0, m["hidden_last"])
            ahead(q + FB * 4, FK)

        def attention(q, near, gain):
            operand(gain)
            if near:
                dve.wait_ge(m["near_in"], due(m["near_in"], 48))
                step(dve.tensor_scalar(QG[:, 2, :], QG[:, 0, :], HD ** -0.5, None, ALU.mult))
            else:
                dve.wait_ge(m["moba_in"], due(m["moba_in"], 16))
            for j in range(6):
                ahead(q + 4 * j, 4)
                used(q + 4 * j + 3)
                dst, cs, banks = (QTOK, KTOK, VTOK)[j // 2], slice((j % 2) * 512, (j % 2 + 1) * 512), acc[:, 2 * (j % 2):2 * (j % 2) + 2, :]
                if j >= 4:
                    dve.tensor_copy(dst[:, :, cs], banks).then_inc(m["in_done"], 1)
                elif near:
                    own = dst[:, :, cs].rearrange("p t (h d) -> p t h d", d=HD)
                    dve.wait_ge(m["qk_square"], due(m["qk_square"]))
                    dve.tensor_reduce(stat[:, 0:16], ROT[:].rearrange("p t (h d) -> p (t h) d", d=HD), AX_X, ALU.add).then_inc(m["qk_summed"], 1)
                    dve.wait_ge(m["qk_summed"], due(m["qk_summed"]))
                    dve.tensor_scalar(stat[:, 0:16], stat[:, 0:16], 1.0 / HD, RMS_EPS, ALU.mult, ALU.add).then_inc(m["ms_ready"], 1)
                    dve.wait_ge(m["rstd_ready"], due(m["rstd_ready"]))
                    for t in range(TT):
                        last = dve.tensor_tensor(own[:, t], own[:, t], wide(rstd[:, 8 * t:8 * t + 8], [P, 8, HD], 2), ALU.mult)
                    last.then_inc(m["in_done"], 1)
                    dve.wait_ge(m["in_done"], due(m["in_done"]))
                    for t in range(TT):
                        last = dve.tensor_tensor(own[:, t], own[:, t], wide(QG[:, 2 - j // 2, :], [P, 8, HD], 1), ALU.mult)
                    last.then_inc(m["qk_done"], 1)
                    dve.wait_ge(m["qk_done"], due(m["qk_done"]))
                else:
                    for t in range(TT):
                        src = banks[:, t, :].rearrange("p (h d) -> p h d", d=HD)
                        own = dst[:, t, cs].rearrange("p (h d) -> p h d", d=HD)
                        rot = ROT[:, t, :].rearrange("p (h d) -> p h d", d=HD)
                        cos, sin = ROPE[:, t, j // 2, 0, :], ROPE[:, t, j // 2, 1, :]
                        dve.tensor_tensor(own, src, wide(cos, [P, 8, HD], 1), ALU.mult)
                        dve.tensor_tensor(rot[:, :, 0:32], src[:, :, 32:64], wide(sin[:, 0:32], [P, 8, 32], 1), ALU.mult)
                        last = dve.tensor_tensor(rot[:, :, 32:64], src[:, :, 0:32], wide(sin[:, 32:64], [P, 8, 32], 1), ALU.mult)
                    last.then_inc(m["in_done"], 1)
                    dve.wait_ge(m["in_done"], due(m["in_done"]))
                    last = dve.tensor_tensor(dst[:, :, cs], dst[:, :, cs], ROT[:], ALU.add)
                    last.then_inc(m["qk_done"], 1)
                    dve.wait_ge(m["qk_done"], due(m["qk_done"]))
            due(m["in_done"], 2)
            if near:
                dve.wait_ge(m["bias_ready"], due(m["bias_ready"], TT))

            def maxima(p):
                dve.wait_ge(m["scores_ready"], due(m["scores_ready"]))
                for t in range(TT):
                    keys = SEQ if near else (t + 1) * P
                    src = acc[:, 2 * (p % 2):2 * (p % 2) + 2, t * SEQ:(t + 1) * SEQ]
                    if near:
                        step(dve.tensor_tensor(SC[:, p % 2, t], src, BIAS[:, t, 2 * p:2 * p + 2, :], ALU.add))
                        src = SC[:, p % 2, t]
                    last = dve.tensor_reduce(NMAX[:, t, 2 * p:2 * p + 2], src[:, :, 0:keys], AX_X, ALU.max, negate=True)
                last.then_inc(m["max_ready"], 1)

            def copy_probs(p):
                dve.wait_ge(m["probs_turned"], due(m["probs_turned"], 2))
                if near:
                    last = dve.tensor_copy(PT[:, p % 2, 1], aux[:, 1, :].rearrange("p (k n) -> p k n", k=TT))
                else:
                    dve.tensor_copy(PT[:, p % 2, 1, 0, :], aux[:, 1, 0:SEQ])
                    last = dve.tensor_copy(PT[:, p % 2, 1, 1, P:SEQ], aux[:, 1, SEQ + P:2 * SEQ])
                last.then_inc(m["probs_copied_v"], 1)

            def outputs(p):
                dve.wait_ge(m["o_ready"], due(m["o_ready"]))
                two = slice(2 * p, 2 * p + 2)
                step(dve.reciprocal(RSUM[:, :, two], SUMS[:, :, two]))
                for t in range(TT):
                    last = dve.tensor_tensor(tok[:, t, 2 * p * HD:2 * (p + 1) * HD].rearrange("p (h d) -> p h d", h=2),
                                             aux[:, 2 + p % 2, 2 * t * HD:2 * (t + 1) * HD].rearrange("p (h d) -> p h d", h=2),
                                             wide(RSUM[:, t, two], [P, 2, HD], 2), ALU.mult)
                    if p == PAIRS - 1:
                        last.then_inc(m["token_ready"], 1)
                if p < PAIRS - 2:
                    last.then_inc(m["o_done"], 1)

            for p in range(PAIRS + 2):
                if p < PAIRS:
                    maxima(p)
                if 1 <= p <= PAIRS:
                    copy_probs(p - 1)
                if p >= 2:
                    outputs(p - 2)
            operand()
            ahead(q + IN_Q, OUT_Q)

        def conv(q, gain, layer):
            operand(gain)
            tap = lambda n, k: taps[:, layer, n, k:k + 1]
            for j in range(6):
                ahead(q + 4 * j, 4)
                banks = acc[:, 2 * (j % 2):2 * (j % 2) + 2, :]
                ks = range(4 * (j % 2), 4 * (j % 2) + 4)
                part = lambda x: x[:, ks[0]:ks[-1] + 1, :]
                pairs = lambda x: part(x).rearrange("p (b k) n -> p b (k n)", b=2)
                if j >= 2:
                    used(q + 4 * j + 3)
                if j in (2, 3):
                    dve.wait_ge(m["c_done"], due(m["c_done"]))
                    dve.tensor_tensor(pairs(ZT), pairs(CT), banks, ALU.mult).then_inc(m["z_done"], 1)
                    dve.wait_ge(m["z_done"], due(m["z_done"]))
                    for k in ks:
                        last = dve.tensor_scalar(CV[:, k, :], ZT[:, k, :], tap(1, k), None, ALU.mult)
                    step(last)
                    for k in ks:
                        last = dve.scalar_tensor_tensor(out=CV[:, k, 1:SEQ], in0=ZT[:, k, 0:SEQ - 1], scalar=tap(0, k), in1=CV[:, k, 1:SEQ],
                                                        op0=ALU.mult, op1=ALU.add)
                    step(last)
                    for k in ks:
                        last = dve.scalar_tensor_tensor(out=CV[:, k, 0:SEQ - 1], in0=ZT[:, k, 1:SEQ], scalar=tap(2, k), in1=CV[:, k, 0:SEQ - 1],
                                                        op0=ALU.mult, op1=ALU.add)
                    step(last)
                if j >= 4:
                    dve.tensor_tensor(pairs(YT), pairs(CV), banks, ALU.mult).then_inc(m["y_done"], 1)
                    dve.wait_ge(m["conv_hi_done"], due(m["conv_hi_done"]))
                    dve.tensor_tensor(part(OL), part(YT), part(OH).bitcast(F32), ALU.subtract).then_inc(m["conv_lo_done"], 1)
            ahead(q + IN_Q, OUT_Q)

        def hyena(q, gain):
            operand(gain)
            dve.wait_ge(m["hyena_in"], due(m["hyena_in"], 16 * 10))

            def filters():
                for r in range(4):
                    t, d = r // 2, r % 2
                    dve.wait_ge(m["filt_ready"], due(m["filt_ready"]))
                    dve.tensor_tensor(FR[:, 2 * d + t, :].rearrange("p (c n) -> p c n", c=2), aux[:, 2 * d:2 * d + 2, :],
                                      WIN[:, t, :].rearrange("p (c n) -> p c n", c=2), ALU.mult).then_inc(m["filt_done"], 1)
                dve.wait_ge(m["filt_done"], due(m["filt_done"], 4))
                step(dve.tensor_tensor(FR[0:1, 0, :], FR[0:1, 0, :], FR[0:1, 2, :], ALU.add))
                step(dve.memset(FR[0:1, 2, :], 0.0))
                for t in range(TT):
                    dve.tensor_tensor(EO[:, t, :], FR[:, t, :], FR[:, 2 + t, :], ALU.add)
                    dve.tensor_tensor(EO[:, 2 + t, :], FR[:, t, :], FR[:, 2 + t, :], ALU.subtract).then_inc(m["eo_ready"], 1)
                dve.wait_ge(m["norm_ready"], due(m["norm_ready"]))
                dve.reciprocal(RN[:].rearrange("p (c n) -> p c n", c=2), aux[:, 0:2, :]).then_inc(m["freq_done"], 1)
                for r in range(5):
                    dve.wait_ge(m["freq_ready"], due(m["freq_ready"]))
                    b = 2 * ((r + 1) % 2)
                    dve.tensor_copy(HF[:, r, :].rearrange("p (c n) -> p c n", c=2), aux[:, b:b + 2, :]).then_inc(m["freq_done"], 1)
                dve.wait_ge(m["freq_done"], due(m["freq_done"], 6))

            for n in range(2):
                dve.wait_ge(m["mlp_ready"], due(m["mlp_ready"]))
                step(dve.tensor_scalar(ARG[:, 0, :], aux[0:FHID, 0, 0:SEQ], FCOL[:, n:n + 1], FCOL[:, 2:3], ALU.add, ALU.mult))
                step(dve.tensor_scalar(ARG[:, 1, :], ARG[:, 0, :], 1.0 / TWO_PI, MAGIC, ALU.mult, ALU.add))
                step(dve.tensor_scalar(ARG[:, 1, :], ARG[:, 1, :], -MAGIC, None, ALU.add))
                for c in (-TWO_PI_HI, -TWO_PI_LO):
                    step(dve.scalar_tensor_tensor(out=ARG[:, 0, :], in0=ARG[:, 1, :], scalar=c, in1=ARG[:, 0, :], op0=ALU.mult, op1=ALU.add))
                dve.tensor_scalar(ARG[:, 0, :], ARG[:, 0, :], PI_BELOW, -PI_BELOW, ALU.min, ALU.max).then_inc(m["arg_ready"], 1)
            filters()
            for j in range(6):
                ahead(q + 4 * j, 4)
                used(q + 4 * j + 3)
                if j >= 2:
                    dve.wait_ge(m["cv_turned"], due(m["cv_turned"]))
                src = lambda c: acc[:, 2 * (j % 2) + c // 2, (c % 2) * SEQ:(c % 2 + 1) * SEQ]
                tap = lambda n, c: TAPS3[:, n, 4 * j + c:4 * j + c + 1]
                for c in range(4):
                    last = dve.tensor_scalar(HCV[:, j % 2, c, :], src(c), tap(1, c), tap(3, c), ALU.mult, ALU.add)
                step(last)
                for c in range(4):
                    last = dve.scalar_tensor_tensor(out=HCV[:, j % 2, c, 1:SEQ], in0=src(c)[:, 0:SEQ - 1], scalar=tap(0, c),
                                                    in1=HCV[:, j % 2, c, 1:SEQ], op0=ALU.mult, op1=ALU.add)
                step(last)
                for c in range(4):
                    last = dve.scalar_tensor_tensor(out=HCV[:, j % 2, c, 0:SEQ - 1], in0=src(c)[:, 1:SEQ], scalar=tap(2, c),
                                                    in1=HCV[:, j % 2, c, 0:SEQ - 1], op0=ALU.mult, op1=ALU.add)
                last.then_inc(m["cv_ready"], 1)
            due(m["cv_turned"], 2)
            for n in range(ORDER):
                if n:
                    filters()
                for r in range(4):
                    f, c = r // 2, r % 2
                    cs = slice(c * 512, (c + 1) * 512)
                    re, im = acc[:, 2 * (r % 2), :], acc[:, 2 * (r % 2) + 1, :]
                    dve.wait_ge(m["dft_ready"], due(m["dft_ready"]))
                    dve.tensor_tensor(FR[:, f, cs], re, HF[:, f, cs], ALU.mult)
                    dve.tensor_tensor(EO[:, 0, cs], im, HF[:, 2 + f, cs], ALU.mult)
                    dve.tensor_tensor(FR[:, 2 + f, cs], re, HF[:, 2 + f, cs], ALU.mult)
                    step(dve.tensor_tensor(EO[:, 1, cs], im, HF[:, 1 if f else 4, cs], ALU.mult))
                    dve.tensor_tensor(FR[:, f, cs], FR[:, f, cs], EO[:, 0, cs], ALU.subtract)
                    dve.tensor_tensor(FR[:, 2 + f, cs], FR[:, 2 + f, cs], EO[:, 1, cs], ALU.add).then_inc(m["dft_done"], 1)
                    dve.wait_ge(m["dft_done"], due(m["dft_done"]))
                if n:
                    dve.wait_ge(m["hyena2_in"], due(m["hyena2_in"], 32))
                for t in range(TT):
                    step(dve.tensor_tensor(EO[:, 2 + t, :], HV[:, t, :], SKIP[:], ALU.mult))
                dve.wait_ge(m["idft_ready"], due(m["idft_ready"]))
                for t in range(TT):
                    step(dve.tensor_tensor(EO[:, t, :].rearrange("p (c n) -> p c n", c=2), acc[:, 2 * t:2 * t + 2, :],
                                           RN[:].rearrange("p (c n) -> p c n", c=2), ALU.mult))
                    step(dve.tensor_tensor(EO[:, t, :], EO[:, t, :], EO[:, 2 + t, :], ALU.add))
                    if n == 0:
                        last = dve.tensor_tensor(HV[:, t, :], EO[:, t, :], HX1[:, t, :], ALU.mult)
                        if t == TT - 1:
                            last.then_inc(m["idft_done"], 1)
                            dve.wait_ge(m["idft_done"], due(m["idft_done"]))
                    else:
                        dve.tensor_tensor(tok[:, t, :], EO[:, t, :], HX2[:, t, :], ALU.mult).then_inc(m["token_ready"], 1)
            operand()
            ahead(q + IN_Q, OUT_Q)

        convs = 0
        for n, kind in enumerate(layers):
            gain = n - LAYER_NORMS if n >= LAYER_NORMS else None
            if kind == "conv":
                conv(start[n], gain, convs)
                convs += 1
            else:
                {"rwkv": rwkv, "ffn": ffn, "moba": lambda q, g: attention(q, False, g),
                 "near": lambda q, g: attention(q, True, g), "hyena": hyena}[kind](start[n], gain)
            residual(n, start[n] + (FFN_Q if kind == "ffn" else IN_Q + OUT_Q))

    @block.gpsimd
    def _(pool):
        due = Tally(pool)

        def load(dst, src, done):
            pool.dma_start(dst, src).then_inc(done, 16)

        def rsqrt(n):
            pool.wait_ge(m["ms_ready"], due(m["ms_ready"]))
            pool.tensor_tensor(rstd[:, 0:n], stat[:, 0:n], half[:, 0:n], ALU.pow).then_inc(m["rstd_ready"], 1)

        def load_ln(n):
            load(lng[:], A["ln_g"][n].partition_broadcast(P), m["ln_in"])
            load(lnb[:], A["ln_b"][n].partition_broadcast(P), m["ln_in"])

        pool.memset(half[:], -0.5).then_inc(m["halves_set"], 1)
        pool.memset(LW[:], 1.0).then_inc(m["halves_set"], 1)
        pool.memset(LA[:], 1.0).then_inc(m["halves_set"], 1)
        for dst, name in ((VEC, "vec"), ):
            load(dst[:], A[name].partition_broadcast(P), m["vec_in"])
        for dst, name in ((L2, "lora2"), (CUM, "cum"), (SPAN, "span"), (LMASK, "level_masks"), (STRICT, "strict"), (PICK, "pick"),
                          (G2, "g2a"), (G2b, "g2b")):
            load(dst[:], A[name], m["vec_in"])
        for dst, name in ((ident, "ident"), (gains, "gains"), (taps, "taps")):
            load(dst[:], A[name], m["consts_in"])
        load(X[:], A["x"], m["res_in"])
        load_ln(0)
        pool.wait_ge(m["consts_in"], due(m["consts_in"], 16 * 3))
        for h in range(GROUP):
            pool.tensor_copy(identb[:, h * P:(h + 1) * P], ident[:]).then_inc(m["identb_set"], 1)
        pool.wait_ge(m["halves_set"], due(m["halves_set"], 3))
        for _ in range(2):
            pool.memset(stat[:, 60:61], 0.0).then_inc(m["hidden_lo"], 1)
            pool.wait_ge(m["hidden_lo"], due(m["hidden_lo"]))

        def rwkv(n):
            rsqrt(32)
            pool.wait_ge(m["scaled_ready"], due(m["scaled_ready"]))
            for zeros in (AK, RB, RK, KTT, BTT, ST):
                pool.memset(zeros[:], 0.0).then_inc(m["presets"], 1)
            pool.wait_ge(m["exp_ready"], due(m["exp_ready"], 7))
            for k, name in enumerate(("gn_g", "gn_b")):
                load(DEC[:, k, :], A[name].partition_broadcast(P), m["gn_in"])
            rsqrt(32)

        def before(n):
            pool.wait_ge(m["residual_done"], TT * n)

        def moba(n):
            before(n)
            load(ROPE[:], A["rope"], m["moba_in"])
            load(FLIP[:], A["causal"], m["causal_in"])
            pool.wait_ge(m["causal_in"], due(m["causal_in"], 16))
            pool.tensor_copy(CAUSAL[:], FLIP[:]).then_inc(m["causal_set"], 1)

        def near(n):
            before(n)
            load(FLIP[:], A["flip"], m["near_in"])
            load(QG[:, 0, :], A["q_gain"].partition_broadcast(P), m["near_in"])
            load(QG[:, 1, :], A["k_gain"].partition_broadcast(P), m["near_in"])
            load(BMASK[:], A["near_mask"], m["bias_in"])
            rpb = A["rpb"]
            for r in range(ROWS):
                for s in range(ROWS):
                    src = bass.AP(tensor=rpb.tensor, offset=rpb.offset + (s - r + RPB_ROWS // 2) * RPB_PAD,
                                  ap=[[1, GRID_W], [RPB_ROWS * RPB_PAD, HEADS], [1, GRID_W]])
                    of = slice((r % 2) * GRID_W, (r % 2 + 1) * GRID_W)
                    load(BIAS[of, r // 2, :, s * GRID_W:(s + 1) * GRID_W], src, m["bias_in"])
            for _ in range(2):
                rsqrt(16)
            pool.wait_ge(m["bias_in"], due(m["bias_in"], 16 * (1 + ROWS * ROWS)))
            for t in range(TT):
                pool.tensor_tensor(BIAS[:, t], BIAS[:, t], BMASK[:, t, :].unsqueeze(1).to_broadcast([P, HEADS, SEQ]), ALU.add)\
                    .then_inc(m["bias_ready"], 1)
                rsqrt(16)

        def hyena(n):
            before(n)
            pool.memset(ONES[:], 1.0).then_inc(m["ones_set"], 1)
            for dst, name in ((WIN, "window"), (DFT, "dft"), (IDFT, "idft"), (EMBT, "emb"), (TAPS3, "taps3"), (FCOL, "f_cols")):
                load(dst[:], A[name], m["hyena_in"])
            load(SKIP[:], A["f_skip"][0].partition_broadcast(P), m["hyena_in"])
            load(FW[0:EMB, 0, :], A["f_w1"], m["hyena_in"])
            load(FW[:, 1, :], A["f_w2"], m["hyena_in"])
            load(FW3[:], A["f_w3"][0], m["hyena_in"])
            pool.wait_ge(m["filt_done"], due(m["filt_done"], 4))
            load(FW3[:], A["f_w3"][1], m["hyena2_in"])
            pool.wait_ge(m["idft_done"], due(m["idft_done"]))
            load(SKIP[:], A["f_skip"][1].partition_broadcast(P), m["hyena2_in"])

        banks = {0: 8, 1: 12, 2: 20}
        for n, kind in enumerate(layers):
            if kind in ("rwkv", "moba", "near", "hyena"):
                {"rwkv": rwkv, "moba": moba, "near": near, "hyena": hyena}[kind](n)
            if n < LAYER_NORMS:
                rsqrt(TT)
                if n + 1 < min(LAYER_NORMS, len(layers)):
                    pool.wait_ge(m["operand_ready"], banks[n])
                    load_ln(n + 1)
            if LAYER_NORMS - 1 <= n < len(layers) - 1:
                rsqrt(TT)

    ctx.close()


def constants():
    c = {}
    f32 = np.float32
    i, j = np.arange(P)[:, None], np.arange(P)[None, :]
    c["ident"] = np.eye(P, dtype=f32)
    middle = i < P // 2
    c["cum"] = np.stack([-DECAY * ((i <= j).astype(f32) - middle), -DECAY * ((i < j).astype(f32) - middle)], 1).astype(f32)
    c["span"] = (-DECAY * np.stack([np.arange(P) >= P // 2, np.arange(P) < P // 2], 1)).astype(f32)
    c["strict"] = (j < i).astype(f32)
    low = lambda a, b, n: (a // n % 2 == 1) & (b // n % 2 == 0) & (a // (2 * n) == b // (2 * n))
    eye = np.eye(P)
    c["level_masks"] = np.stack([low(i, j, 1) + 0 * eye, low(j, i, 1) + 0 * eye] + [low(j, i, n) + eye for n in LEVELS], 1).astype(f32)
    c["pick"] = np.stack([(i < j), (i <= j)], 1).astype(np.uint32)
    inv = (f32(10000.0) ** (-np.arange(0, HD, 2, dtype=f32) / f32(HD))).astype(f32)
    ang = np.arange(SEQ, dtype=f32)[:, None] * inv[None, :]
    cos, sin = np.cos(ang).astype(f32), np.sin(ang).astype(f32)
    both = np.stack([np.concatenate([cos, cos], 1), np.concatenate([-sin, sin], 1)], 1)
    rope = np.stack([both * f32(HD ** -0.5), both], 1)
    c["rope"] = rope.reshape(TT, P, 2, 2, HD).transpose(1, 0, 2, 3, 4).astype(f32)
    c["causal"] = np.where(j <= i, 0.0, -3.0e38).astype(f32)
    c["flip"] = (i // GRID_W * GRID_W + GRID_W - 1 - i % GRID_W == j).astype(f32)
    col = np.arange(GRID_W)
    first = np.clip(col - 8, 0, GRID_W - 16)
    sees = (col[None, :] >= first[:, None]) & (col[None, :] < first[:, None] + 16)
    c["near_mask"] = np.tile(np.where(sees[::-1], 0.0, -3.0e38), (ROWS, ROWS)).reshape(TT, P, SEQ).transpose(1, 0, 2).astype(f32)
    t = np.linspace(0.0, 1.0, SEQ, dtype=f32)[:, None]
    bands = np.linspace(1e-4, BANDS - 1, BANDS, dtype=f32)
    ang = (f32(TWO_PI) * np.arange(SEQ, dtype=f32)[:, None] / f32(SEQ) * bands).astype(f32)
    c["emb"] = np.concatenate([t, np.cos(ang), -np.sin(ang)], 1).astype(f32).T
    lt = np.log(1e-2)
    deltas = np.abs(np.linspace(lt / 1.5, lt / 0.3, D, dtype=f32))
    c["window"] = np.exp(-t * deltas).astype(f32).reshape(TT, P, D).transpose(1, 0, 2)
    n = 2 * SEQ
    w = 2.0 * np.pi / n * (np.arange(SEQ)[:, None] * np.arange(SEQ)[None, :] % n)
    re, im, nyquist = np.cos(w), -np.sin(w), np.cos(np.pi * np.arange(SEQ))
    put = lambda a: np.concatenate([nyquist[:, None], a[:, 1:P]], 1)
    dft = np.stack([re[:, :P], re[:, P:], put(im), im[:, P:], im[:, :P], put(re)], 1)
    c["dft"] = dft.reshape(TT, P, 6, P).transpose(1, 0, 2, 3).astype(f32)
    back_re, back_im = 2.0 * re.T / n, 2.0 * im.T / n
    back_re[0] /= 2.0
    back_im[0] = nyquist / n
    c["idft"] = np.concatenate([back_re, back_im]).reshape(4, P, SEQ).transpose(1, 0, 2).astype(f32)
    return {k: np.ascontiguousarray(v) for k, v in c.items()}


def column_blocks(w):
    return w.reshape(4, 2, P, -1, 512).transpose(3, 0, 2, 1, 4).reshape(-1, P, QW)


def layout(x, **w):
    a = constants()
    rows = lambda v: v.reshape(-1, P)
    quarters = []

    def ffn(w_in, w_down):
        blocks = w_in.reshape(4, 2, P, 2, FB, 256).transpose(4, 0, 2, 1, 3, 5).reshape(-1, P, QW)
        quarters.extend([blocks, w_down.reshape(FK, P, D)])

    def mixer(w_in, w_out):
        quarters.extend([column_blocks(w_in), w_out.reshape(KT, P, D)])

    def gated(w_in):
        b, c, u = np.split(w_in, 3, axis=1)
        return np.concatenate([c, u, b], axis=1)

    mixer(np.concatenate(list(w["rwkv_w_rkv"][0]), axis=1), w["rwkv_w_o"][0])
    ffn(w["ffn_w_in"][0], w["ffn_w_down"][0])
    mixer(w["moba_w_qkv"][0], w["moba_w_o"][0])
    ffn(w["ffn_w_in"][1], w["ffn_w_down"][1])
    mixer(gated(w["a_w_in_2"][0]), w["a_w_out_2"][0])
    ffn(w["f_w13_2"][0], w["f_w2_2"][0])
    mixer(w["b_w_qkv_2"][0], w["b_w_out_2"][0])
    ffn(w["f_w13_2"][1], w["f_w2_2"][1])
    mixer(w["c_w_in_2"][0], w["c_w_out_2"][0])
    ffn(w["f_w13_2"][2], w["f_w2_2"][2])
    mixer(gated(w["a_w_in_2"][1]), w["a_w_out_2"][1])
    ffn(w["f_w13_2"][3], w["f_w2_2"][3])
    a["weights"] = np.concatenate(quarters)

    a["x"] = x[0].reshape(TT, P, D).transpose(1, 0, 2)
    a["xT"] = x[0].T.reshape(KT, P, SEQ).transpose(1, 0, 2)
    a["mu"] = w["rwkv_mu"][0].reshape(6, KT, P).transpose(2, 0, 1)
    lora1 = np.concatenate([w["rwkv_w1"][0], w["rwkv_a1"][0], w["rwkv_g1"][0]], axis=1)
    a["lora1"] = lora1.reshape(KT, P, -1).transpose(1, 0, 2)
    a["lora2"] = np.stack([np.concatenate([w["rwkv_w2"][0], w["rwkv_w0"]]), np.concatenate([w["rwkv_a2"][0], w["rwkv_a0"]])], axis=1)
    a["vec"] = np.concatenate([w["rwkv_k_k"], w["rwkv_k_a"], w["rwkv_r_k"].reshape(1, D)])
    a["g2a"], a["g2b"] = w["rwkv_g2"][0, :P], w["rwkv_g2"][0, P:]
    a["gn_g"], a["gn_b"] = w["rwkv_gn_g"][0], w["rwkv_gn_b"][0]
    a["ln_g"] = np.stack([w["ln_mix_g"][0], w["ln_ffn_g"][0], w["ln_mix_g"][1], w["ln_ffn_g"][1]])
    a["ln_b"] = np.stack([w["ln_mix_b"][0], w["ln_ffn_b"][0], w["ln_mix_b"][1], w["ln_ffn_b"][1]])
    a["gains"] = np.stack([w["norm_mix_g_2"], w["norm_ffn_g_2"]], 1).reshape(8, KT, P).transpose(2, 0, 1)
    a["taps"] = w["a_conv_w_2"].reshape(2, 3, KT, P).transpose(3, 0, 1, 2)
    a["q_gain"], a["k_gain"] = w["b_q_norm_g_2"][0], w["b_k_norm_g_2"][0]
    pad = (RPB_PAD - RPB_COLS) // 2
    a["rpb"] = np.pad(w["b_rpb_2"][0], ((0, 0), (0, 0), (pad, pad)))
    a["taps3"] = np.concatenate([w["c_short_w_2"][0], w["c_short_b_2"]]).reshape(4, 3 * KT, P).transpose(2, 0, 1)
    a["f_w1"], a["f_w2"] = w["c_f_w1_2"][0], w["c_f_w2_2"][0]
    a["f_w3"] = w["c_f_w3_2"][0].reshape(FHID, ORDER, 2 * D).transpose(1, 0, 2)
    a["f_cols"] = np.stack([w["c_f_b1_2"][0], w["c_f_b2_2"][0], w["c_f_freq_2"][0]], axis=1)
    a["f_skip"] = w["c_f_skip_2"][0]
    return {k: np.ascontiguousarray(v) for k, v in a.items()}


def kernel(**inputs):
    import concourse.bacc as bacc
    from concourse.bass_utils import run_bass_kernel_spmd

    arrays = layout(**{k: np.asarray(v) for k, v in inputs.items()})
    nc = bacc.Bacc("TRN2", target_bir_lowering=False, num_devices=1)
    A = {k: nc.dram_tensor(f"in_{k}", v.shape, mybir.dt.from_np(v.dtype), kind="ExternalInput").ap() for k, v in arrays.items()}
    out = nc.dram_tensor("out_x", (SEQ, D), F32, kind="ExternalOutput").ap()
    program(nc, A, out.rearrange("(t p) c -> p t c", p=P))
    r = run_bass_kernel_spmd(nc, [{f"in_{k}": v for k, v in arrays.items()}], core_ids=[0])
    return r.results[0]["out_x"].reshape(1, SEQ, D)
```

```python
from contextlib import ExitStack, contextmanager

import numpy as np

import concourse.bass as bass
from concourse import mybir

F32 = mybir.dt.float32
F32R = mybir.dt.float32r
BF16 = mybir.dt.bfloat16
U32 = mybir.dt.uint32
ALU = mybir.AluOpType
ACT = mybir.ActivationFunctionType
AX_X = mybir.AxisListType.X

P = 128
SEQ, D = 256, 1024
TT, KT = SEQ // P, D // P
HEADS, HD = 16, 64
PAIRS = HEADS // 2
FF = 2816
FK = FF // P
FB = FF // 256
SLOTS = 4
QW = 1024
LORA, GLORA = 64, 160
ALPHA = 4.0 ** 0.25
LN_EPS, RMS_EPS, GN_EPS = 1e-5, 1e-6, HD * 1e-5
DECAY = float(np.exp(-0.5))
LEVELS = (2, 4, 8, 16, 32, 64)
GROUP = 4
GRID_W, ROWS = 64, SEQ // 64
RPB_ROWS, RPB_COLS, RPB_PAD = 15, 31, 127
MAGIC = 1.5 * 2.0 ** 23
TWO_PI = 2.0 * np.pi
TWO_PI_HI = float(np.float32(TWO_PI))
TWO_PI_LO = float(TWO_PI - TWO_PI_HI)
PI_BELOW = 3.1415925
ORDER, BANDS, FHID = 2, 16, 64
SPECTRA = ((0, 0), (0, 1), (0, 5), (1, 4), (1, 3))
EMB = 1 + 2 * BANDS
IN_Q, OUT_Q, FFN_Q = 3 * D // 512 * 4, KT, FB * 4 + FK
LAYERS = ("rwkv", "ffn", "moba", "ffn", "conv", "ffn", "near", "ffn", "hyena", "ffn", "conv", "ffn")
LAYER_NORMS = 4


class Tally:

    def __init__(self, engine):
        self.engine, self.count, self.inside = engine, {}, None

    def __call__(self, sem, n=1):
        self.count[sem.name] = self.count.get(sem.name, 0) + n
        if self.inside is None:
            return self.count[sem.name]
        i, each = self.inside
        return i * each[sem.name] + self.count[sem.name]

    @contextmanager
    def loop(self, times, each):
        each = {sem.name: n for sem, n in each.items()}
        before = dict(self.count)
        with self.engine.Fori(0, times) as i:
            self.inside = (i, each)
            yield i
            self.inside = None
        for name, n in self.count.items():
            assert n - before.get(name, 0) == each.get(name, 0), (name, n - before.get(name, 0))
        for name, n in each.items():
            self.count[name] = before.get(name, 0) + n * times


def program(nc, A, out, layers=LAYERS):
    ctx = ExitStack()
    quarters = sum(FFN_Q if kind == "ffn" else IN_Q + OUT_Q for kind in layers)

    def keep(name, shape, dtype=F32):
        return ctx.enter_context(nc.sbuf_tensor(name, shape, dtype))

    def sem(name):
        return ctx.enter_context(nc.semaphore(name))

    def scope(*tensors):
        with ExitStack() as s:
            return [s.enter_context(nc.sbuf_tensor(n, shape, (dtype or [F32])[0])) for n, shape, *dtype in tensors]

    X = keep("residual", [P, TT, D])
    raw = keep("w_raw", [P, SLOTS, QW])
    whi = keep("w_hi", [P, SLOTS, QW], F32R)
    wlo = keep("w_lo", [P, SLOTS, QW], F32R)
    ah = keep("operand_hi", [P, KT, SEQ], F32R)
    al = keep("operand_lo", [P, KT, SEQ], F32R)
    tok = keep("token_scratch", [P, TT, D])
    ident = keep("ident_sb", [P, P])
    identb = keep("identb_sb", [P, GROUP * P], BF16)
    taps = keep("taps_sb", [P, 2, 3, KT])
    lng = keep("ln_gain", [P, D])
    lnb = keep("ln_bias", [P, D])
    half = keep("minus_half", [P, 32])
    stat = keep("stat", [P, 64])
    mom = keep("moments", [P, TT, 2])
    rstd = keep("rstd", [P, 32])
    acc = ctx.enter_context(nc.psum_tensor("acc", [P, 4, 512], F32))
    aux = ctx.enter_context(nc.psum_tensor("aux", [P, 4, 512], F32))

    with ExitStack() as s:
        def rwkv(name, shape, dtype=F32):
            return s.enter_context(nc.sbuf_tensor(name, shape, dtype))

        R, K, V = rwkv("r_rw", [P, TT, D]), rwkv("k_rw", [P, TT, D]), rwkv("v_rw", [P, TT, D])
        IC = rwkv("iclr_rw", [P, TT, D])
        KK = rwkv("kk_rw", [P, TT, D])
        DEC = rwkv("decay_rw", [P, TT, D])
        TMP = rwkv("tmp_rw", [P, TT, D])
        G2 = rwkv("g2_rw", [P, D])
        G2b = rwkv("g2b_rw", [GLORA - P, D])
        SG, SGb = rwkv("sg_rw", [P, SEQ]), rwkv("sgb_rw", [GLORA - P, SEQ])
        CUM = rwkv("cum_rw", [P, 2, P])
        SPAN = rwkv("span_rw", [P, TT])
        DCOL = rwkv("decay_col", [P, KT])
        LMASK = rwkv("level_masks", [P, len(LEVELS) + 2, P])
        STRICT = rwkv("strict_mask", [P, P])
        PICK = rwkv("pick_masks", [P, 2, P], U32)
        BONUS = rwkv("bonus_rw", [P, TT, HEADS])
        VEC, L1, L2, LW, LA, MU = scope(
            ("vec_rw", [P, 3, D]), ("l1_rw", [P, KT, 2 * LORA + GLORA]), ("l2_rw", [LORA + 1, 2, D]),
            ("lora_w", [LORA + 1, SEQ]), ("lora_a", [LORA + 1, SEQ]), ("mu_sb", [P, 6, KT]))
        ART, KTT, BTT, NM, INV, INVT, QM, AK, RB, RK, RHS, U, ST = scope(
            ("ar_turned", [P, 2, TT, 2, P]), ("k_turned", [P, GROUP, SEQ]), ("b_turned", [P, GROUP, SEQ]),
            ("n_rw", [P, TT, GROUP, P]), ("inv_rw", [P, TT, GROUP, P]), ("invt_rw", [P, TT, GROUP, P]),
            ("q_rw", [P, TT, GROUP, P]), ("ak_rw", [P, TT, GROUP, P]), ("rb_rw", [P, TT, GROUP, P]),
            ("rk_rw", [P, TT, GROUP, P]), ("rhs_rw", [P, GROUP * HD]), ("u_rw", [P, TT, GROUP * HD]),
            ("state_rw", [P, 2, 2, HD]))
    L1_FLAT = L1[:].rearrange("p k n -> p (k n)")
    DECAYS = [L1_FLAT[:, 0:D], L1_FLAT[:, D:2 * D], tok[:, 0, :]]
    XT, XX = IC[:].rearrange("p t (k n) -> p (t k) n", n=SEQ), DEC[:].rearrange("p t (k n) -> p (t k) n", n=SEQ)
    MIX = [TMP[:].rearrange("p t (k n) -> p (t k) n", n=SEQ), KK[:].rearrange("p t (k n) -> p (t k) n", n=SEQ)]

    HH, HL, SILU, HM, FIRSTG = scope(
        ("hidden_hi", [P, FK, SEQ], F32R), ("hidden_lo", [P, FK, SEQ], F32R),
        ("silu_ff", [P, 2, TT, 256]), ("hidden_ff", [P, 2, TT, 256]), ("first_rms_gain", [P, D]))
    QTOK, KTOK, VTOK, QT, KTT2, SC, PR, PT, SUMS, NMAX, RSUM, ROPE, ROT, CAUSAL, QG, BIAS, BMASK, FLIP = scope(
        ("q_at", [P, TT, D]), ("k_at", [P, TT, D]), ("v_at", [P, TT, D]), ("q_turned", [P, KT, SEQ]),
        ("k_turned_at", [P, KT, SEQ]), ("scores_at", [P, 2, TT, 2, SEQ]), ("probs_at", [P, 2, TT, 2, SEQ]),
        ("probs_turned", [P, 2, 2, TT, SEQ]), ("sums_at", [P, TT, HEADS]), ("nmax_at", [P, TT, HEADS]),
        ("rsum_at", [P, TT, HEADS]), ("rope_sb", [P, TT, 2, 2, HD]), ("rot_at", [P, TT, 512]),
        ("causal_sb", [P, P], BF16), ("qk_gain", [P, 3, HD]), ("bias_at", [P, TT, HEADS, SEQ]),
        ("bias_mask", [P, TT, SEQ]), ("flip_sb", [P, P]))
    OH, OL, CT, ZT, CV, YT = scope(
        ("conv_hi", [P, KT, SEQ], F32R), ("conv_lo", [P, KT, SEQ], F32R), ("c_conv", [P, KT, SEQ]),
        ("z_conv", [P, KT, SEQ]), ("conv_out", [P, KT, SEQ]), ("y_conv", [P, KT, SEQ]))
    HV, HX1, HX2, HF, FR, EO, WIN, SKIP, RN, DFT, IDFT, EMBT, FW, FW3, TAPS3, FCOL, H1, ARG, ONES = scope(
        ("v_hy", [P, TT, D]), ("x1_hy", [P, TT, D]), ("x2_hy", [P, TT, D]), ("filter_freq", [P, 5, D]),
        ("taps_or_freq", [P, 4, D]), ("even_odd", [P, 4, D]), ("window_sb", [P, TT, D]), ("skip_sb", [P, D]),
        ("norm_hy", [P, D]), ("dft_sb", [P, TT, 6, P]), ("idft_sb", [P, 4, SEQ]), ("emb_sb", [EMB, SEQ]),
        ("f_w12", [FHID, 2, FHID]), ("f_w3_sb", [FHID, 2 * D]), ("taps3_sb", [P, 4, 3 * KT]), ("f_cols", [FHID, 3]),
        ("hid_hy", [FHID, SEQ]), ("arg_hy", [FHID, 2, SEQ]), ("ones_sb", [P, P]))
    HCV = tok[:].rearrange("p b (k n) -> p b k n", n=SEQ)

    w_full = [sem(f"w_full{s}") for s in range(SLOTS)]
    w_hi = [sem(f"w_hi{s}") for s in range(SLOTS)]
    w_lo = [sem(f"w_lo{s}") for s in range(SLOTS)]
    w_used = [sem(f"w_used{s}") for s in range(SLOTS)]
    m = {n: sem(n) for n in (
        "x_in", "x2_in", "rwkv_in", "vec_in", "gn_in", "consts_in", "res_in", "ln_in", "moba_in", "causal_in", "near_in", "bias_in", "hyena_in", "taps2_in", "skip2_in",
        "halves_set", "presets", "ones_set", "identb_set", "causal_set", "bias_ready",
        "gain_in", "half_done", "residual_done", "ln_done", "square_ready", "eps_added", "ms_ready", "rstd_ready", "token_ready", "turned", "hi_ready", "operand_ready", "dve_step",
        "mix_f_ready", "mix_ready", "rkv_done", "lora1_ready", "lora_mid", "lora2_ready", "lora_out", "cum_ready", "span_ready",
        "exp_ready", "k_done", "scaled_ready",
        "group_turned", "group_copied", "pair_ready", "pair_masked", "pair2_ready", "level_ready", "level_masked", "level2_ready",
        "level_copied", "rhs_ready", "rhs_copied", "u_ready", "u_copied", "state_ready", "state_copied", "y_ready", "y_copied",
        "gate_ready",
        "silu_ready", "hidden_ready", "hidden_turned", "hidden_hi", "hidden_lo", "hidden_last",
        "in_done", "qk_square", "qk_summed", "qk_done", "qk_turned", "qk_copied", "scores_ready", "max_ready", "probs_ready",
        "probs_turned", "probs_copied_a", "probs_copied_v", "o_ready", "o_done",
        "c_done", "z_done", "y_done", "conv_hi_done", "conv_lo_done",
        "mlp_ready", "arg_ready", "mlp_done", "filt_ready", "filt_done", "filt_abs", "eo_ready", "norm_ready", "norm_copied", "freq_ready", "freq_done",
        "cv_ready", "cv_turned", "cv_copied", "dft_ready", "dft_done", "idft_ready", "idft_done",
        "y_final", "out_written")}

    PE_PASSES = ((0, 0), (0, 1), (1, 0))
    W = (whi, wlo)

    def nth(q, at=None):
        n = q // SLOTS + 1
        return n if at is None else at[0] * (at[1] // SLOTS) + n

    start = {}
    total = 0
    for n, kind in enumerate(layers):
        start[n] = total
        total += FFN_Q if kind == "ffn" else IN_Q + OUT_Q

    block = ctx.enter_context(nc.Block())

    @block.sync
    def _(sp):
        sp.dma_start(MU[:], A["mu"]).then_inc(m["x_in"], 16)
        sp.dma_start(XT[:, 0:4, :], A["xT"][:, 0:4, :]).then_inc(m["x_in"], 16)
        sp.dma_start(XT[:, 4:KT, :], A["xT"][:, 4:KT, :]).then_inc(m["x2_in"], 16)
        for q in range(SLOTS):
            sp.dma_start(raw[:, q, :], A["weights"][q]).then_inc(w_full[q], 16)
        sp.dma_start(L1[:], A["lora1"]).then_inc(m["rwkv_in"], 16)
        rest = (quarters - SLOTS) // SLOTS
        with sp.Fori(0, rest) as i:
            for s in range(SLOTS):
                sp.wait_ge(w_lo[s], i + 1)
                sp.dma_start(raw[:, s, :], A["weights"][bass.ds(i * SLOTS + (SLOTS + s), 1)].rearrange("q p n -> (q p) n"))\
                  .then_inc(w_full[s], 16)
        for q in range((rest + 1) * SLOTS, quarters):
            sp.wait_ge(w_lo[q % SLOTS], nth(q) - 1)
            sp.dma_start(raw[:, q % SLOTS, :], A["weights"][q]).then_inc(w_full[q % SLOTS], 16)
        for t in range(TT):
            sp.wait_ge(m["y_final"], t + 1)
            sp.dma_start(out[:, t], X[:, t, :]).then_inc(m["out_written"], 16)
        sp.wait_ge(m["out_written"], 16 * TT)

    @block.tensor
    def _(pe):
        due = Tally(pe)

        def part_tokens(q, i, pair, t):
            s = (q + i) % SLOTS
            for kk in range(2):
                kt = 2 * i + kk
                for x, w in PE_PASSES:
                    mm = pe.matmul(acc[:, 2 * pair + t, :], (ah, al)[x][:, kt, t * P:(t + 1) * P],
                                   W[w][:, s, kk * 512:(kk + 1) * 512],
                                   start=(kt == 0 and (x, w) == (0, 0)), stop=(kt == KT - 1 and (x, w) == (1, 0)))
            return mm

        def block_tokens(q, pair, at=None, operand_half=None):
            for i in range(4):
                if operand_half and i % 2 == 0:
                    operand_half()
                pe.wait_ge(w_lo[(q + i) % SLOTS], nth(q + i, at))
                for t in range(TT):
                    mm = part_tokens(q, i, pair, t)
                mm.then_inc(w_used[(q + i) % SLOTS], 1)

        def first_block(q, src, turn_after):
            turn(src, 0)
            for t in range(TT):
                for i in range(4):
                    if i % 2 == 0:
                        pe.wait_ge(m["operand_ready"], due(m["operand_ready"]))
                    if t == 0:
                        pe.wait_ge(w_lo[(q + i) % SLOTS], nth(q + i))
                    mm = part_tokens(q, i, 0, t)
                    if t == TT - 1:
                        mm.then_inc(w_used[(q + i) % SLOTS], 1)
                    elif i == turn_after:
                        turn(src, 1)

        def block_channels(q, pair, operand_waits=False, after={}):
            for i in range(4):
                s = (q + i) % SLOTS
                if operand_waits and i % 2 == 0:
                    pe.wait_ge(m["operand_ready"], due(m["operand_ready"], 3 if i == 0 else 1))
                pe.wait_ge(w_lo[s], nth(q + i))
                for kk in range(2):
                    kt = 2 * i + kk
                    for c in range(4):
                        for x, w in PE_PASSES:
                            mm = pe.matmul(acc[:, 2 * pair + c // 2, (c % 2) * SEQ:(c % 2 + 1) * SEQ],
                                           W[w][:, s, kk * 512 + c * P:kk * 512 + (c + 1) * P], (ah, al)[x][:, kt, :],
                                           start=(kt == 0 and c % 2 == 0 and (x, w) == (0, 0)),
                                           stop=(kt == KT - 1 and c % 2 == 1 and (x, w) == (1, 0)), skip_group_check=True)
                mm.then_inc(w_used[s], 1)
                if i in after:
                    after[i]()

        def project(q, tiles, hi, lo, before, first=0):
            steps = [(kt, t) for t in (first, 1 - first) for kt in range(4)]
            steps += [(kt, t) for kt in range(4, tiles - 4) for t in range(TT)]
            steps += [(kt, t) for t in range(TT) for kt in range(tiles - 4, tiles)]
            seen = set()
            for kt, t in steps:
                s = (q + kt) % SLOTS
                if (kt, t) in before:
                    before[kt, t]()
                if kt not in seen:
                    pe.wait_ge(w_lo[s], nth(q + kt))
                for c in range(2):
                    for x, w in PE_PASSES:
                        mm = pe.matmul(acc[:, 2 * t + c, :], (hi, lo)[x][:, kt, t * P:(t + 1) * P],
                                       W[w][:, s, c * 512:(c + 1) * 512],
                                       start=(kt == 0 and (x, w) == (0, 0)), stop=(kt == tiles - 1 and (x, w) == (1, 0)))
                if kt in seen:
                    mm.then_inc(w_used[s], 1)
                elif kt == tiles - 1:
                    mm.then_inc(m["half_done"], 1)
                seen.add(kt)

        def operand_steps():
            wait = lambda n: lambda: pe.wait_ge(m["operand_ready"], due(m["operand_ready"], n))
            return {(0, 0): wait(1), (0, 1): wait(2), (4, 1): wait(1)}

        def turn_tile(dst, src, flipped=False):
            return pe.matmul(dst, src, FLIP[:], start=True, stop=True) if flipped else pe.transpose(dst, src, ident[:])

        def turn(src, t, ready=1, flipped=False):
            if ready:
                pe.wait_ge(m["token_ready"], due(m["token_ready"], ready))
            for kt in range(KT):
                mm = turn_tile(aux[:, 2 * t + kt // 4, (kt % 4) * P:(kt % 4 + 1) * P], src[:, t, kt * P:(kt + 1) * P], flipped)
                if kt % 4 == 3:
                    mm.then_inc(m["turned"], 1)

        def rwkv(q):
            def lora1(lo, hi, bank, src):
                for kt in range(KT):
                    mm = pe.matmul(aux[0:hi - lo, bank, 0:SEQ], L1[:, kt, lo:hi], src[:, kt, :],
                                   start=(kt == 0), stop=(kt == KT - 1))
                return mm

            def mix_half():
                pe.wait_ge(m["mix_ready"], due(m["mix_ready"]))

            def mixed(mixes):
                pe.wait_ge(m["mix_f_ready"], due(m["mix_f_ready"], 2 * mixes))

            def pair(q, first=False):
                for b in range(2):
                    if not first:
                        pe.wait_ge(m["rkv_done"], due(m["rkv_done"]))
                    block_tokens(q + 4 * b, b, operand_half=None if b else mix_half)

            pair(q, True)
            pe.wait_ge(m["rwkv_in"], due(m["rwkv_in"], 16))
            mixed(3)
            lora1(0, LORA, 0, MIX[0]).then_inc(m["lora1_ready"], 1)
            pair(q + 8)
            mixed(2)
            lora1(LORA, 2 * LORA, 1, MIX[0]).then_inc(m["lora1_ready"], 1)
            pair(q + 16)
            mixed(1)
            lora1(2 * LORA, 2 * LORA + P, 2, MIX[0])
            lora1(2 * LORA + P, 2 * LORA + GLORA, 3, MIX[0]).then_inc(m["lora1_ready"], 1)
            pe.wait_ge(m["vec_in"], due(m["vec_in"], 16 * 11))
            pe.wait_ge(m["consts_in"], due(m["consts_in"], 16 * 2))
            pe.wait_ge(m["identb_set"], due(m["identb_set"], GROUP))
            pe.wait_ge(m["lora_mid"], due(m["lora_mid"], 3))
            for t in range(TT):
                for c in range(2):
                    mm = pe.matmul(aux[:, 2 * t + c, :], LW[:, t * P:(t + 1) * P], L2[:, 0, c * 512:(c + 1) * 512], start=True, stop=True)
            mm.then_inc(m["lora2_ready"], 1)
            pe.wait_ge(m["rkv_done"], due(m["rkv_done"], 2))
            for t in range(TT):
                for c in range(2):
                    mm = pe.matmul(acc[:, 2 * t + c, :], LA[:, t * P:(t + 1) * P], L2[:, 1, c * 512:(c + 1) * 512], start=True, stop=True)
            mm.then_inc(m["lora2_ready"], 1)
            pe.wait_ge(m["lora_out"], due(m["lora_out"], 2))
            for t in range(TT):
                if t:
                    pe.wait_ge(m["exp_ready"], due(m["exp_ready"], 3))
                for e in range(2):
                    for c in range(2):
                        mm = pe.matmul(acc[:, 2 * e + c, :], CUM[:, e, :], DEC[:, t, c * 512:(c + 1) * 512], start=True, stop=True)
                mm.then_inc(m["cum_ready"], 1)
            for k in range(KT):
                for t in range(TT):
                    mm = pe.matmul(aux[:, 0, k:k + 1], DEC[:, t, k * P:(k + 1) * P], SPAN[:, t:t + 1], start=(t == 0), stop=(t == TT - 1))
            mm.then_inc(m["span_ready"], 1)
            pe.wait_ge(m["exp_ready"], due(m["exp_ready"], 4))
            pe.wait_ge(m["scaled_ready"], due(m["scaled_ready"], 1 + TT))
            bank = lambda c, b: (acc, aux)[c][:, b, :]
            for g in range(HEADS // GROUP):
                if g:
                    pe.wait_ge(m["y_copied"], due(m["y_copied"], TT))
                for n, src in enumerate((R, KK, K, IC)):
                    for k in range(2):
                        for t in range(TT):
                            mm = pe.transpose(aux[:, n, k * SEQ + t * P:k * SEQ + (t + 1) * P],
                                              src[:, t, (2 * g + k) * P:(2 * g + k + 1) * P], ident[:])
                    mm.then_inc(m["group_turned"], 1)
                pe.wait_ge(m["group_copied"], due(m["group_copied"], 4))
                for c in range(TT):
                    at = slice(c * P, (c + 1) * P)
                    for k in range(2):
                        mm = pe.matmul(bank(c, 0)[:, k * SEQ:(k + 1) * SEQ], ART[:, k, c, 0, :], BTT[:, 2 * k:2 * k + 2, at],
                                       start=True, stop=True, skip_group_check=True)
                    for h in range(GROUP):
                        mm = pe.matmul(bank(c, 1 + h // 2)[:, (h % 2) * SEQ:(h % 2 + 1) * SEQ], BTT[:, h, at],
                                       ART[:, h // 2, c, :, :], start=True, stop=True, skip_group_check=True)
                    mm.then_inc(m["pair_ready"], 1)
                for k in range(2):
                    for c in range(TT):
                        if k:
                            pe.wait_ge(m["pair_masked"], due(m["pair_masked"]))
                        for h in (2 * k, 2 * k + 1):
                            mm = pe.matmul(bank(c, (3, 0)[k])[:, (h % 2) * SEQ:(h % 2 + 1) * SEQ], KTT[:, h, c * P:(c + 1) * P],
                                           ART[:, k, c, :, :], start=True, stop=True, skip_group_check=True)
                        if k:
                            mm.then_inc(m["pair2_ready"], 1)
                for n, size in enumerate(LEVELS):
                    for c in range(TT):
                        if n == 0:
                            pe.wait_ge(m["pair_masked"], due(m["pair_masked"]))
                        else:
                            pe.wait_ge(m["level_copied"], due(m["level_copied"]))
                        pe.matmul(bank(c, 0), identb[:, 0:P], identb[:, :], start=True, stop=False, skip_group_check=True)
                        for h in range(GROUP):
                            mm = pe.matmul(bank(c, 0)[:, h * P:(h + 1) * P], NM[:, c, h, :], INVT[:, c, h, :],
                                           start=False, stop=(h == GROUP - 1), skip_group_check=True)
                        mm.then_inc(m["level_ready"], 1)
                    for c in range(TT):
                        pe.wait_ge(m["level_masked"], due(m["level_masked"]))
                        for h in range(GROUP):
                            mm = pe.matmul(bank(c, 1)[:, h * P:(h + 1) * P], INV[:, c, h, :], QM[:, c, h, :], start=True, stop=True,
                                           skip_group_check=True)
                            if n < len(LEVELS) - 1:
                                mm = pe.matmul(bank(c, 2)[:, h * P:(h + 1) * P], QM[:, c, h, :], INV[:, c, h, :], start=True, stop=True,
                                               skip_group_check=True)
                        mm.then_inc(m["level2_ready"], 1)
                pe.wait_ge(m["level_copied"], due(m["level_copied"], TT))
                for c in range(TT):
                    head = lambda h: slice((GROUP * g + h) * HD, (GROUP * g + h + 1) * HD)
                    if c:
                        pe.wait_ge(m["state_copied"], due(m["state_copied"], 4))
                    for h in range(GROUP):
                        own = slice(h * HD, (h + 1) * HD)
                        mm = pe.matmul(bank(c, 0)[:, own], AK[:, c, h, :], V[:, c, head(h)], start=(h == 0), stop=(c == 0 and h == GROUP - 1),
                                       skip_group_check=True)
                    if c:
                        for k in range(2):
                            mm = pe.matmul(bank(c, 0)[:, k * P:(k + 1) * P], ART[:, k, c, 0, :], ST[:, k], start=False, stop=(k == 1),
                                           skip_group_check=True)
                    mm.then_inc(m["rhs_ready"], 1)
                    pe.wait_ge(m["rhs_copied"], due(m["rhs_copied"]))
                    for h in range(GROUP):
                        own = slice(h * HD, (h + 1) * HD)
                        mm = pe.matmul(bank(c, 1)[:, own], INVT[:, c, h, :], RHS[:, own], start=True, stop=True, skip_group_check=True)
                    mm.then_inc(m["u_ready"], 1)
                    pe.wait_ge(m["u_copied"], due(m["u_copied"]))
                    if c == 0:
                        for k in range(2):
                            pr = slice((2 * g + k) * P, (2 * g + k + 1) * P)
                            pe.matmul(bank(c, 3)[:, k * P:(k + 1) * P], IC[:, c, pr], U[:, c, k * P:(k + 1) * P], start=True, stop=False,
                                      skip_group_check=True)
                            mm = pe.matmul(bank(c, 3)[:, k * P:(k + 1) * P], K[:, c, pr], V[:, c, pr], start=False, stop=True,
                                           skip_group_check=True)
                        mm.then_inc(m["state_ready"], 1)
                    for h in range(GROUP):
                        own = slice(h * HD, (h + 1) * HD)
                        pe.matmul(bank(c, 2)[:, own], RB[:, c, h, :], U[:, c, own], start=(h == 0), stop=False, skip_group_check=True)
                        mm = pe.matmul(bank(c, 2)[:, own], RK[:, c, h, :], V[:, c, head(h)], start=False, stop=(c == 0 and h == GROUP - 1),
                                       skip_group_check=True)
                    if c:
                        for k in range(2):
                            mm = pe.matmul(bank(c, 2)[:, k * P:(k + 1) * P], ART[:, k, c, 1, :], ST[:, k], start=False, stop=(k == 1),
                                           skip_group_check=True)
                    mm.then_inc(m["y_ready"], 1)
            pe.wait_ge(m["y_copied"], due(m["y_copied"], TT))
            for t in range(TT):
                for c in range(2):
                    cs = slice(c * 512, (c + 1) * 512)
                    pe.matmul(acc[:, 2 * t + c, :], SG[:, t * P:(t + 1) * P], G2[:, cs], start=True, stop=False)
                    mm = pe.matmul(acc[:, 2 * t + c, :], SGb[:, t * P:(t + 1) * P], G2b[:, cs], start=False, stop=True)
            mm.then_inc(m["gate_ready"], 1)
            for t in range(TT):
                turn(tok, t)
            project(q + IN_Q, KT, ah, al, operand_steps())

        def ffn(q, normed):
            def turn_hidden(odd, last=False):
                pe.wait_ge(m["hidden_ready"], due(m["hidden_ready"], TT))
                pe.wait_ge(m["hidden_lo"], due(m["hidden_lo"], 0) + 1 if last else due(m["hidden_lo"]))
                for kk in range(2):
                    for t in range(TT):
                        mm = pe.transpose(aux[:, odd, kk * SEQ + t * P:kk * SEQ + (t + 1) * P],
                                          HM[:, odd, t, kk * P:(kk + 1) * P], ident[:])
                mm.then_inc(m["hidden_turned"], 1)

            first_block(q, tok if normed else X, 1 if normed else 3)
            with due.loop((FB - 1) // 2, {m["hidden_ready"]: 2 * TT, m["hidden_lo"]: 2}) as i:
                for b in range(2):
                    block_tokens(q + 4 + 4 * b, 1 - b, at=(i, 8))
                    turn_hidden(b)
            project(q + FB * 4, FK, HH, HL, {(0, 0): lambda: turn_hidden(0, last=True),
                                             (FK - 4, 0): lambda: pe.wait_ge(m["hidden_last"], due(m["hidden_last"]))}, first=1)

        def attention(q, near):
            def turn_qk(src, flipped=False):
                for b in range(4):
                    for kk in range(2):
                        k = 2 * b + kk
                        for t in range(TT):
                            mm = turn_tile(aux[:, b, kk * SEQ + t * P:kk * SEQ + (t + 1) * P], src[:, t, k * P:(k + 1) * P], flipped)
                    mm.then_inc(m["qk_turned"], 1)

            for j in range(6):
                if j >= 2:
                    pe.wait_ge(m["in_done"], due(m["in_done"]))
                if j:
                    block_tokens(q + 4 * j, j % 2)
                else:
                    first_block(q, tok if near else X, 1 if near else 3)
                if j == 4:
                    pe.wait_ge(m["qk_done"], due(m["qk_done"], 2))
                    if near:
                        pe.wait_ge(m["near_in"], due(m["near_in"], 16 * 3))
                    turn_qk(QTOK, near)
            pe.wait_ge(m["qk_done"], due(m["qk_done"], 2))
            pe.wait_ge(m["qk_copied"], due(m["qk_copied"], 4))
            turn_qk(KTOK)
            pe.wait_ge(m["in_done"], due(m["in_done"], 2))
            pe.wait_ge(m["qk_copied"], due(m["qk_copied"], 4))
            if not near:
                pe.wait_ge(m["causal_set"], due(m["causal_set"]))

            def scores(p):
                for t in range(TT):
                    keys = SEQ if near else (t + 1) * P
                    for h in range(2):
                        of = slice(h * HD, (h + 1) * HD)
                        mm = pe.matmul(acc[:, 2 * (p % 2) + h, t * SEQ:t * SEQ + keys], QT[of, p, t * P:(t + 1) * P], KTT2[of, p, 0:keys],
                                       start=True, stop=near, skip_group_check=True)
                        if not near:
                            mm = pe.matmul(acc[:, 2 * (p % 2) + h, t * SEQ + t * P:t * SEQ + (t + 1) * P], identb[:, 0:P], CAUSAL[:],
                                           start=False, stop=True, skip_group_check=True)
                mm.then_inc(m["scores_ready"], 1)

            def turn_probs(p):
                pe.wait_ge(m["probs_ready"], due(m["probs_ready"], TT))
                if p:
                    pe.wait_ge(m["probs_copied_a"], due(m["probs_copied_a"]))
                    pe.wait_ge(m["probs_copied_v"], due(m["probs_copied_v"]))
                for h in range(2):
                    for t in range(TT):
                        for k in range(TT if near else t + 1):
                            mm = pe.transpose(aux[:, h, k * SEQ + t * P:k * SEQ + (t + 1) * P], PR[:, p % 2, t, h, k * P:(k + 1) * P], ident[:])
                    mm.then_inc(m["probs_turned"], 1)

            def values(p):
                if p >= 2:
                    pe.wait_ge(m["o_done"], due(m["o_done"]))
                for t in range(TT):
                    for h in range(2):
                        tiles = TT if near else t + 1
                        for k in range(tiles):
                            mm = pe.matmul(aux[:, 2 + p % 2, (t * 2 + h) * HD:(t * 2 + h + 1) * HD], PT[:, p % 2, h, k, t * P:(t + 1) * P],
                                           VTOK[:, k, (2 * p + h) * HD:(2 * p + h + 1) * HD], start=(k == 0), stop=(k == tiles - 1),
                                           skip_group_check=True)
                mm.then_inc(m["o_ready"], 1)

            scores(0)
            for p in range(PAIRS):
                if p + 1 < PAIRS:
                    scores(p + 1)
                turn_probs(p)
                if p:
                    values(p - 1)
            pe.wait_ge(m["probs_copied_a"], due(m["probs_copied_a"]))
            pe.wait_ge(m["probs_copied_v"], due(m["probs_copied_v"]))
            values(PAIRS - 1)
            for t in range(TT):
                turn(tok, t, ready=0 if t else TT, flipped=near)
            project(q + IN_Q, KT, ah, al, operand_steps())

        def conv(q):
            for t in range(TT):
                turn(tok, t)
            for j in range(6):
                if j >= 2:
                    freed = m["c_done"] if j < 4 else m["z_done"]
                    pe.wait_ge(freed, due(freed))
                block_channels(q + 4 * j, j % 2, operand_waits=(j == 0))
            ready = lambda: pe.wait_ge(m["conv_lo_done"], due(m["conv_lo_done"]))
            project(q + IN_Q, KT, OH, OL, {(0, 0): ready, (0, 1): ready})

        def hyena(q):
            def mlp(k):
                if k:
                    pe.wait_ge(m["mlp_done"], due(m["mlp_done"]))
                weights, x = (FW[:, 1, :], H1) if k else (FW[0:EMB, 0, :], EMBT)
                pe.matmul(aux[0:FHID, 0, 0:SEQ], weights, x[:], start=True, stop=True).then_inc(m["mlp_ready"], 1)

            def taps(r, pairs):
                t, d = r // 2, r % 2
                if r >= pairs:
                    pe.wait_ge(m["filt_done"], due(m["filt_done"]))
                for c in range(2):
                    mm = pe.matmul(aux[:, 2 * (r % pairs) + c, :], H1[:, t * P:(t + 1) * P], FW3[:, d * D + c * 512:d * D + (c + 1) * 512],
                                   start=True, stop=True)
                mm.then_inc(m["filt_ready"], 1)

            def freq(k, pairs):
                part, mats = SPECTRA[k]
                if k == 0:
                    pe.wait_ge(m["filt_done"], due(m["filt_done"], pairs))
                elif k == pairs + 2:
                    pe.wait_ge(m["norm_copied"], due(m["norm_copied"]))
                elif pairs == 1 or k == 2:
                    pe.wait_ge(m["freq_done"], due(m["freq_done"]))
                if k in (0, 3):
                    pe.wait_ge(m["eo_ready"], due(m["eo_ready"]))
                for c in range(2):
                    for t in range(TT):
                        mm = pe.matmul(aux[:, 2 * (k % pairs) + c, :], DFT[:, t, mats, :], EO[:, 2 * part + t, c * 512:(c + 1) * 512],
                                       start=(t == 0), stop=(t == TT - 1))
                mm.then_inc(m["freq_ready"], 1)

            def norm(pairs):
                pe.wait_ge(m["freq_done"], due(m["freq_done"], pairs))
                pe.wait_ge(m["filt_abs"], due(m["filt_abs"], 4))
                for c in range(2):
                    for k in range(4):
                        mm = pe.matmul(aux[:, c, :], ONES[:], FR[:, k, c * 512:(c + 1) * 512], start=(k == 0), stop=(k == 3))
                mm.then_inc(m["norm_ready"], 1)

            def turn_cv(j):
                pe.wait_ge(m["cv_ready"], due(m["cv_ready"]))
                if j:
                    pe.wait_ge(m["cv_copied"], due(m["cv_copied"]))
                for t in range(TT):
                    for c in range(4):
                        mm = pe.transpose(aux[:, 2 + t, c * P:(c + 1) * P], HCV[:, j % 2, c, t * P:(t + 1) * P], ident[:])
                mm.then_inc(m["cv_turned"], 1)

            def dft(r):
                f, c = r // 2, r % 2
                for part, mat in enumerate((f, 2 + f)):
                    for t in range(TT):
                        mm = pe.matmul(acc[:, 2 * (r % 2) + part, :], DFT[:, t, mat, :], HV[:, t, c * 512:(c + 1) * 512],
                                       start=(t == 0), stop=(t == TT - 1))
                mm.then_inc(m["dft_ready"], 1)

            for t in range(TT):
                turn(tok, t)
            pe.wait_ge(m["hyena_in"], due(m["hyena_in"], 16 * 10))
            pe.wait_ge(m["ones_set"], due(m["ones_set"]))

            def first_taps():
                pe.wait_ge(m["mlp_done"], due(m["mlp_done"]))
                taps(0, 1)

            pieces = [lambda: mlp(0), lambda: mlp(1), first_taps] + [lambda r=r: taps(r, 1) for r in (1, 2, 3)]
            pieces += [lambda: None] + [lambda k=k: freq(k, 1) for k in range(5)]
            pieces.insert(10, lambda: norm(1))
            for j in range(6):
                turned = {2: lambda: turn_cv(j - 1)} if j else {}
                block_channels(q + 4 * j, j % 2, operand_waits=(j == 0), after={1: pieces[2 * j], 3: pieces[2 * j + 1], **turned})
            pieces[12]()
            dft(0)
            turn_cv(5)
            for n in range(ORDER):
                for r in range(1 - n, 4):
                    if r >= 2:
                        pe.wait_ge(m["dft_done"], due(m["dft_done"]))
                    dft(r)
                if n == 0:
                    pe.wait_ge(m["freq_done"], due(m["freq_done"]))
                    pe.wait_ge(m["cv_copied"], due(m["cv_copied"]))
                    pe.wait_ge(m["taps2_in"], due(m["taps2_in"], 16))
                    for r in range(2):
                        taps(r, 2)
                pe.wait_ge(m["dft_done"], due(m["dft_done"], 2))
                for t in range(TT):
                    for c in range(2):
                        for f in range(4):
                            mm = pe.matmul(acc[:, 2 * t + c, :], IDFT[:, f, t * P:(t + 1) * P], FR[:, f, c * 512:(c + 1) * 512],
                                           start=(f == 0), stop=(f == 3))
                mm.then_inc(m["idft_ready"], 1)
                if n == 0:
                    for r in range(2, 4):
                        taps(r, 2)
                    for k in range(5):
                        if k == 3:
                            norm(2)
                        freq(k, 2)
                    pe.wait_ge(m["idft_done"], due(m["idft_done"]))
            pe.wait_ge(m["freq_done"], due(m["freq_done"], 2))
            for t in range(TT):
                turn(tok, t)
            project(q + IN_Q, KT, ah, al, operand_steps())

        for n, kind in enumerate(layers):
            {"rwkv": rwkv, "ffn": lambda q: ffn(q, n > LAYER_NORMS), "moba": lambda q: attention(q, False), "near": lambda q: attention(q, True),
             "conv": conv, "hyena": hyena}[kind](start[n])

    @block.scalar
    def _(act):
        due = Tally(act)

        def split(q, at=None):
            s = q % SLOTS
            act.wait_ge(w_full[s], 16 * nth(q) if at is None else at[0] * (16 * at[1] // SLOTS) + 16 * nth(q))
            if q >= SLOTS:
                act.wait_ge(w_used[s], nth(q - SLOTS, at))
            act.activation(whi[:, s, :], raw[:, s, :], ACT.Copy).then_inc(w_hi[s], 1)

        def ahead(q, n, at=None):
            for k in range(n):
                if q + k + SLOTS < quarters:
                    split(q + k + SLOTS, at)

        def operand(t):
            for h in range(2):
                act.wait_ge(m["turned"], due(m["turned"]))
                act.activation(ah[:, 4 * h:4 * h + 4, t * P:(t + 1) * P], aux[:, 2 * t + h, :].rearrange("p (k n) -> p k n", n=P), ACT.Copy)\
                   .then_inc(m["hi_ready"], 1)

        def both_operands():
            for t in range(TT):
                operand(t)

        def residual(n, q):
            more = n < len(layers) - 1
            rms = more and n >= LAYER_NORMS - 1

            def square(t):
                if n >= LAYER_NORMS:
                    act.wait_ge(m["residual_done"], TT * n + t + 1)
                else:
                    act.wait_ge(m["ln_done"], due(m["ln_done"]))
                act.activation(tok[:, t, :], X[:, t, :], ACT.Square, accum_out=stat[:, 56 + t:57 + t]).then_inc(m["square_ready"], 1)

            if rms:
                square(0)
            ahead(q - 4, 3)
            if more:
                operand(0)
            if n < LAYER_NORMS:
                ahead(q - 1, 1)
            if rms:
                square(1)
            if n >= LAYER_NORMS:
                ahead(q - 1, 1)
            if more:
                operand(1)

        def rwkv(q):
            def copy_out(dst, c, s, q):
                act.wait_ge(w_used[s], nth(q))
                for t in range(TT):
                    last = act.activation(dst[:, t, c * 512:(c + 1) * 512], acc[:, 2 * c + t, :], ACT.Copy)
                last.then_inc(m["rkv_done"], 1)

            def mix_hi(src, h):
                act.wait_ge(m["mix_f_ready"], due(m["mix_f_ready"]))
                ks = slice(4 * h, 4 * h + 4)
                act.activation(ah[:, ks, :], MIX[src][:, ks, :], ACT.Copy).then_inc(m["hi_ready"], 1)

            def project_out(dst, q, mixes_between):
                for c in range(2):
                    ahead(q + 4 * c, 4)
                    if c and mixes_between is not None:
                        act.wait_ge(w_used[(q + 7) % SLOTS], nth(q + 7))
                        due(m["mix_f_ready"], 2 * mixes_between)
                        for h in range(2):
                            mix_hi(1, h)
                    copy_out(dst, c, (q + 4 * c + 3) % SLOTS, q + 4 * c + 3)

            for h in range(2):
                split(q + h)
                mix_hi(0, h)
            split(q + 2)
            split(q + 3)
            act.wait_ge(m["halves_set"], due(m["halves_set"], 3))
            project_out(R, q, 0)
            act.wait_ge(m["lora1_ready"], due(m["lora1_ready"]))
            act.activation(LW[0:LORA, :], aux[0:LORA, 0, 0:SEQ], ACT.Tanh).then_inc(m["lora_mid"], 1)
            project_out(K, q + 8, 1)
            act.wait_ge(m["lora1_ready"], due(m["lora1_ready"]))
            act.activation(LA[0:LORA, :], aux[0:LORA, 1, 0:SEQ], ACT.Copy).then_inc(m["lora_mid"], 1)
            project_out(V, q + 16, None)
            act.wait_ge(m["lora1_ready"], due(m["lora1_ready"]))
            act.activation(SG[:], aux[:, 2, 0:SEQ], ACT.Sigmoid)
            act.activation(SGb[:], aux[0:GLORA - P, 3, 0:SEQ], ACT.Sigmoid).then_inc(m["lora_mid"], 1)
            for dst, src in ((DEC, aux), (IC, acc)):
                act.wait_ge(m["lora2_ready"], due(m["lora2_ready"]))
                for t in range(TT):
                    for c in range(2):
                        last = act.activation(dst[:, t, c * 512:(c + 1) * 512], src[:, 2 * t + c, :], ACT.Sigmoid)
                last.then_inc(m["lora_out"], 1)
            for t in range(TT):
                act.wait_ge(m["cum_ready"], due(m["cum_ready"]))
                if t:
                    act.wait_ge(m["scaled_ready"], due(m["scaled_ready"], 2))
                for dst, b, sign in zip(DECAYS, (0, 0, 2), (1.0, -1.0, 1.0)):
                    if t == 0 and b:
                        act.wait_ge(m["k_done"], due(m["k_done"]))
                    act.activation(dst.rearrange("p (c n) -> p c n", c=2), acc[:, b:b + 2, :], ACT.Exp, scale=sign).then_inc(m["exp_ready"], 1)
            act.wait_ge(m["span_ready"], due(m["span_ready"]))
            act.activation(DCOL[:], aux[:, 0, 0:KT], ACT.Exp).then_inc(m["exp_ready"], 1)
            bank = lambda c, b: (acc, aux)[c][:, b, :]
            for g in range(HEADS // GROUP):
                for n in range(2):
                    act.wait_ge(m["group_turned"], due(m["group_turned"]))
                    act.activation(ART[:, :, :, 1 - n, :], aux[:, n, :].rearrange("p (k t n) -> p k t n", k=2, t=TT), ACT.Copy)\
                       .then_inc(m["group_copied"], 1)
                due(m["group_turned"], 2)
                for n in range(len(LEVELS)):
                    for c in range(TT):
                        act.wait_ge(m["level2_ready"], due(m["level2_ready"]))
                        last = act.activation(INVT[:, c], bank(c, 1), ACT.Copy)
                        if n < len(LEVELS) - 1:
                            last = act.activation(INV[:, c], bank(c, 2), ACT.Copy)
                        last.then_inc(m["level_copied"], 1)
                for c in range(TT):
                    act.wait_ge(m["rhs_ready"], due(m["rhs_ready"]))
                    act.activation(RHS[:], bank(c, 0)[:, 0:GROUP * HD], ACT.Copy).then_inc(m["rhs_copied"], 1)
                    act.wait_ge(m["u_ready"], due(m["u_ready"]))
                    act.activation(U[:, c, :], bank(c, 1)[:, 0:GROUP * HD], ACT.Copy).then_inc(m["u_copied"], 1)
                    act.wait_ge(m["y_ready"], due(m["y_ready"]))
                    act.activation(tok[:, c, g * GROUP * HD:(g + 1) * GROUP * HD], bank(c, 2)[:, 0:GROUP * HD], ACT.Copy)\
                       .then_inc(m["y_copied"], 1)
            both_operands()
            ahead(q + IN_Q, OUT_Q - 4)

        def ffn(q):

            def silu(q, odd, pair, at=None):
                act.wait_ge(w_used[(q + 3) % SLOTS], nth(q + 3, at))
                for t in range(TT):
                    last = act.activation(SILU[:, odd, t, :], acc[:, 2 * pair + t, 0:256], ACT.Silu)
                last.then_inc(m["silu_ready"], 1)

            def hidden_hi(dst, odd):
                act.wait_ge(m["hidden_turned"], due(m["hidden_turned"]))
                act.activation(dst, aux[:, odd, :].rearrange("p (k n) -> p k n", k=2), ACT.Copy).then_inc(m["hidden_hi"], 1)

            ahead(q, 4)
            silu(q, 0, 0)
            with due.loop((FB - 1) // 2, {m["hidden_turned"]: 2}) as i:
                for b in range(2):
                    ahead(q + 4 + 4 * b, 4, (i, 8))
                    silu(q + 4 + 4 * b, 1 - b, 1 - b, (i, 8))
                    hidden_hi(HH[:, bass.ds(i * 4 + 2 * b, 2), :], b)
            hidden_hi(HH[:, FK - 2:FK, :], 0)
            ahead(q + FB * 4, FK - 4)

        def attention(q, near):
            for j in range(6):
                ahead(q + 4 * j, 4)
                if near and j < 4:
                    act.wait_ge(w_used[(q + 4 * j + 3) % SLOTS], nth(q + 4 * j + 3))
                    dst = (QTOK, KTOK)[j // 2]
                    act.activation(dst[:, :, (j % 2) * 512:(j % 2 + 1) * 512], acc[:, 2 * (j % 2):2 * (j % 2) + 2, :], ACT.Copy)
                    if j:
                        act.wait_ge(m["qk_summed"], due(m["qk_summed"]))
                    act.activation(ROT[:], acc[:, 2 * (j % 2):2 * (j % 2) + 2, :], ACT.Square).then_inc(m["qk_square"], 1)
                if j == 4:
                    for b in range(4):
                        act.wait_ge(m["qk_turned"], due(m["qk_turned"]))
                        act.activation(QT[:, 2 * b:2 * b + 2, :], aux[:, b, :], ACT.Copy).then_inc(m["qk_copied"], 1)
            for b in range(4):
                act.wait_ge(m["qk_turned"], due(m["qk_turned"]))
                act.activation(KTT2[:, 2 * b:2 * b + 2, :], aux[:, b, :], ACT.Copy).then_inc(m["qk_copied"], 1)

            def copy_probs(p):
                act.wait_ge(m["probs_turned"], due(m["probs_turned"]))
                if near:
                    act.activation(PT[:, p % 2, 0], aux[:, 0, :], ACT.Copy).then_inc(m["probs_copied_a"], 1)
                else:
                    act.activation(PT[:, p % 2, 0, 0, :], aux[:, 0, 0:SEQ], ACT.Copy)
                    act.activation(PT[:, p % 2, 0, 1, P:SEQ], aux[:, 0, SEQ + P:2 * SEQ], ACT.Copy).then_inc(m["probs_copied_a"], 1)
                due(m["probs_turned"])

            for p in range(PAIRS):
                act.wait_ge(m["max_ready"], due(m["max_ready"]))
                for t in range(TT):
                    keys = SEQ if near else (t + 1) * P
                    for h in range(2):
                        src = SC[:, p % 2, t, h, :] if near else acc[:, 2 * (p % 2) + h, t * SEQ:t * SEQ + keys]
                        last = act.activation(PR[:, p % 2, t, h, 0:keys], src, ACT.Exp, bias=NMAX[:, t, 2 * p + h:2 * p + h + 1],
                                              accum_out=SUMS[:, t, 2 * p + h:2 * p + h + 1])
                    last.then_inc(m["probs_ready"], 1)
                if p:
                    copy_probs(p - 1)
            copy_probs(PAIRS - 1)
            both_operands()
            ahead(q + IN_Q, OUT_Q - 4)

        def conv(q):
            for j in range(6):
                ahead(q + 4 * j, 4)
                if j < 2:
                    act.wait_ge(w_used[(q + 4 * j + 3) % SLOTS], nth(q + 4 * j + 3))
                    act.activation(CT[:, 4 * j:4 * j + 4, :].rearrange("p (b k) n -> p b (k n)", b=2), acc[:, 2 * j:2 * j + 2, :], ACT.Copy)\
                       .then_inc(m["c_done"], 1)
                if j >= 4:
                    act.wait_ge(m["y_done"], due(m["y_done"]))
                    act.activation(OH[:, 4 * (j - 4):4 * (j - 3), :], YT[:, 4 * (j - 4):4 * (j - 3), :], ACT.Copy).then_inc(m["conv_hi_done"], 1)
            ahead(q + IN_Q, OUT_Q - 4)

        def hyena(q):
            def sine():
                act.wait_ge(m["arg_ready"], due(m["arg_ready"]))
                act.activation(H1[:], ARG[:, 0, :], ACT.Sin).then_inc(m["mlp_done"], 1)

            def absolute():
                act.wait_ge(m["eo_ready"], due(m["eo_ready"], 2))
                for k in range(4):
                    act.activation(FR[:, k, :], FR[:, k, :], ACT.Abs).then_inc(m["filt_abs"], 1)

            two = lambda x: x.rearrange("p (c n) -> p c n", c=2)

            def freq(k, pairs):
                act.wait_ge(m["freq_ready"], due(m["freq_ready"]))
                b = 2 * (k % pairs)
                act.activation(two(HF[:, k, :]), aux[:, b:b + 2, :], ACT.Copy).then_inc(m["freq_done"], 1)

            def norm():
                act.wait_ge(m["norm_ready"], due(m["norm_ready"]))
                act.activation(two(RN[:]), aux[:, 0:2, :], ACT.Copy).then_inc(m["norm_copied"], 1)

            def copy_cv(j):
                act.wait_ge(m["cv_turned"], due(m["cv_turned"]))
                dst, c = (HV, HX1, HX2)[j // 2], j % 2
                act.activation(dst[:, :, c * 512:(c + 1) * 512], aux[:, 2:4, :], ACT.Copy).then_inc(m["cv_copied"], 1)

            nothing = lambda: None
            pieces = [sine, sine, nothing, nothing, nothing, nothing, absolute] + [lambda k=k: freq(k, 1) for k in range(5)]
            pieces.insert(10, norm)
            for j in range(6):
                ahead(q + 4 * j, 2)
                pieces[2 * j]()
                ahead(q + 4 * j + 2, 1)
                if j:
                    copy_cv(j - 1)
                ahead(q + 4 * j + 3, 1)
                pieces[2 * j + 1]()
            pieces[12]()
            copy_cv(5)
            absolute()
            for k in range(5):
                if k == 3:
                    act.wait_ge(m["idft_done"], due(m["idft_done"]))
                    norm()
                freq(k, 2)
            both_operands()
            ahead(q + IN_Q, OUT_Q - 4)

        for n, kind in enumerate(layers):
            {"rwkv": rwkv, "ffn": ffn, "moba": lambda q: attention(q, False), "near": lambda q: attention(q, True),
             "conv": conv, "hyena": hyena}[kind](start[n])
            residual(n, start[n] + (FFN_Q if kind == "ffn" else IN_Q + OUT_Q))

    @block.vector
    def _(dve):
        due = Tally(dve)

        def split(q, at=None):
            s = q % SLOTS
            dve.wait_ge(w_hi[s], nth(q, at))
            dve.tensor_tensor(wlo[:, s, :], raw[:, s, :], whi[:, s, :].bitcast(F32), ALU.subtract).then_inc(w_lo[s], 1)

        def ahead(q, n, at=None):
            for k in range(n):
                if q + k + SLOTS < quarters:
                    split(q + k + SLOTS, at)

        def used(q, at=None):
            dve.wait_ge(w_used[q % SLOTS], nth(q, at))

        def step(instruction):
            instruction.then_inc(m["dve_step"], 1)
            dve.wait_ge(m["dve_step"], due(m["dve_step"]))

        def operand(t):
            for h in range(2):
                dve.wait_ge(m["hi_ready"], due(m["hi_ready"]))
                own = (slice(None), slice(4 * h, 4 * h + 4), slice(t * P, (t + 1) * P))
                dve.tensor_tensor(al[own], aux[:, 2 * t + h, :].rearrange("p (k n) -> p k n", n=P), ah[own].bitcast(F32), ALU.subtract)\
                   .then_inc(m["operand_ready"], 1)

        def both_operands():
            for t in range(TT):
                operand(t)

        def wide(v, shape, axis):
            return v.unsqueeze(axis).to_broadcast(shape)

        def by_head(x):
            return x.rearrange("p t (h d) -> p (t h) d", d=HD)

        def residual(n, q):
            more = n < len(layers) - 1
            layer_norm = n < LAYER_NORMS
            rms = more and n >= LAYER_NORMS - 1
            gain = lng if n >= LAYER_NORMS else FIRSTG

            def add(t):
                if t == 0:
                    dve.wait_ge(m["half_done"], due(m["half_done"]))
                else:
                    used(q - 1)
                cols = X[:, t, :].rearrange("p (c n) -> p c n", c=2)
                if layer_norm:
                    last = dve.scalar_tensor_tensor(out=cols, in0=cols, scalar=ALPHA, in1=acc[:, 2 * t:2 * t + 2, :], op0=ALU.mult, op1=ALU.add)
                else:
                    last = dve.tensor_tensor(cols, cols, acc[:, 2 * t:2 * t + 2, :], ALU.add)
                last.then_inc(m["residual_done"] if more or layer_norm else m["y_final"], 1)

            def norm(t):
                if layer_norm:
                    dve.wait_ge(m["residual_done"], TT * n + t + 1)
                    for c in range(2):
                        last = dve.bn_stats(stat[:, 32 + 6 * c:38 + 6 * c], X[:, t, c * 512:(c + 1) * 512])
                    step(last)
                    dve.bn_aggr(mom[:, t, :], stat[:, 32:44]).then_inc(m["ms_ready"], 1)
                    dve.wait_ge(m["rstd_ready"], due(m["rstd_ready"]))
                    step(dve.tensor_scalar(X[:, t, :], X[:, t, :], mom[:, t, 0:1], rstd[:, t:t + 1], ALU.subtract, ALU.mult))
                    step(dve.tensor_tensor(X[:, t, :], X[:, t, :], lng[:], ALU.mult))
                    dve.tensor_tensor(X[:, t, :], X[:, t, :], lnb[:], ALU.add)\
                       .then_inc(m["ln_done"] if rms else m["token_ready"] if more else m["y_final"], 1)
                if rms:
                    dve.wait_ge(m["rstd_ready"], due(m["rstd_ready"]))
                    dve.scalar_tensor_tensor(out=tok[:, t, :], in0=X[:, t, :], scalar=rstd[:, t:t + 1], in1=gain[:], op0=ALU.mult, op1=ALU.mult)\
                       .then_inc(m["token_ready"], 1)

            if n == 0:
                dve.wait_ge(m["res_in"], due(m["res_in"], 16 * TT))
            if layer_norm:
                dve.wait_ge(m["ln_in"], due(m["ln_in"], 32))
            if rms:
                dve.wait_ge(m["gain_in"], due(m["gain_in"], 16))
            add(0)
            norm(0)
            ahead(q - 4, 1)
            if layer_norm:
                ahead(q - 3, 1)
                if more:
                    operand(0)
                ahead(q - 2, 1)
                ahead(q - 1, 1)
                add(1)
                norm(1)
            else:
                add(1)
                if more:
                    operand(0)
                ahead(q - 3, 1)
                norm(1)
                ahead(q - 2, 2)
            if more:
                operand(1)

        def rwkv(q):
            def differences(h):
                ks = slice(4 * h, 4 * h + 4)
                dve.tensor_tensor(XX[:, ks, 1:SEQ], XT[:, ks, 0:SEQ - 1], XT[:, ks, 1:SEQ], ALU.subtract)
                step(dve.tensor_scalar(XX[:, ks, 0:1], XT[:, ks, 0:1], -1.0, None, ALU.mult))

            def mix(n, dst, h):
                for k in range(4 * h, 4 * h + 4):
                    last = dve.scalar_tensor_tensor(out=MIX[dst][:, k, :], in0=XX[:, k, :], scalar=MU[:, n, k:k + 1], in1=XT[:, k, :],
                                                    op0=ALU.mult, op1=ALU.add)
                last.then_inc(m["mix_f_ready"], 1)

            def mix_all(n, dst):
                for h in range(2):
                    mix(n, dst, h)

            def mix_lo(src):
                for h in range(2):
                    dve.wait_ge(m["hi_ready"], due(m["hi_ready"]))
                    ks = slice(4 * h, 4 * h + 4)
                    dve.tensor_tensor(al[:, ks, :], MIX[src][:, ks, :], ah[:, ks, :].bitcast(F32), ALU.subtract).then_inc(m["mix_ready"], 1)
                dve.wait_ge(m["mix_ready"], due(m["mix_ready"], 2))

            dve.wait_ge(m["x_in"], due(m["x_in"], 32))
            differences(0)
            mix(0, 0, 0)
            dve.wait_ge(m["x2_in"], due(m["x2_in"], 16))
            differences(1)
            mix(0, 0, 1)
            split(q)
            split(q + 1)
            mix_lo(0)
            split(q + 2)
            split(q + 3)
            mix_all(2, 1)
            ahead(q, 2)
            mix_all(1, 0)
            ahead(q + 2, 6)
            mix_lo(1)
            mix_all(3, 1)
            ahead(q + 8, 4)
            dve.wait_ge(m["lora1_ready"], due(m["lora1_ready"]))
            mix_all(4, 0)
            ahead(q + 12, 4)
            mix_lo(1)
            ahead(q + 16, 4)
            dve.wait_ge(m["lora1_ready"], due(m["lora1_ready"]))
            mix_all(5, 0)
            dve.wait_ge(m["vec_in"], due(m["vec_in"], 16 * 11))
            dve.wait_ge(m["rkv_done"], due(m["rkv_done"], 4))
            vec = lambda n: wide(VEC[:, n, :], [P, TT, D], 1)
            step(dve.tensor_tensor(KK[:], K[:], vec(0), ALU.mult))
            ahead(q + 20, 2)
            step(dve.tensor_tensor(tok[:], KK[:], KK[:], ALU.mult))
            step(dve.tensor_reduce(stat[:, 0:32], by_head(tok[:]), AX_X, ALU.add))
            dve.tensor_scalar(stat[:, 0:32], stat[:, 0:32], 1e-24, None, ALU.max).then_inc(m["ms_ready"], 1)
            ahead(q + 22, 2)
            dve.wait_ge(m["rkv_done"], due(m["rkv_done"], 2))
            dve.wait_ge(m["lora1_ready"], due(m["lora1_ready"]))
            step(dve.tensor_tensor(TMP[:], R[:], vec(2), ALU.mult))
            dve.wait_ge(m["rstd_ready"], due(m["rstd_ready"]))
            step(dve.tensor_tensor(by_head(KK[:]), by_head(KK[:]), wide(rstd[:], [P, TT * HEADS, HD], 2), ALU.mult))
            dve.wait_ge(m["lora_out"], due(m["lora_out"], 2))
            step(dve.scalar_tensor_tensor(out=tok[:], in0=IC[:], scalar=-1.0, in1=vec(1), op0=ALU.add, op1=ALU.mult))
            dve.scalar_tensor_tensor(out=K[:], in0=tok[:], scalar=1.0, in1=K[:], op0=ALU.add, op1=ALU.mult).then_inc(m["k_done"], 1)
            dve.wait_ge(m["k_done"], due(m["k_done"]))
            dve.tensor_tensor(TMP[:], TMP[:], K[:], ALU.mult)
            dve.tensor_tensor(IC[:], KK[:], IC[:], ALU.mult).then_inc(m["scaled_ready"], 1)
            dve.wait_ge(m["scaled_ready"], due(m["scaled_ready"]))
            for t in range(TT):
                dve.wait_ge(m["exp_ready"], due(m["exp_ready"], 3))
                dve.tensor_tensor(R[:, t, :], R[:, t, :], DECAYS[0], ALU.mult)
                dve.tensor_tensor(K[:, t, :], K[:, t, :], DECAYS[1], ALU.mult)
                dve.tensor_tensor(IC[:, t, :], IC[:, t, :], DECAYS[1], ALU.mult)
                dve.scalar_tensor_tensor(out=KK[:, t, :], in0=KK[:, t, :], scalar=-1.0, in1=DECAYS[2], op0=ALU.mult, op1=ALU.mult)\
                   .then_inc(m["scaled_ready"], 1)
            due(m["scaled_ready"], TT)
            dve.tensor_reduce(BONUS[:].rearrange("p t h -> p (t h)"), by_head(TMP[:]), AX_X, ALU.add)
            dve.wait_ge(m["exp_ready"], due(m["exp_ready"]))
            dve.wait_ge(m["presets"], due(m["presets"], 6))
            bank = lambda c, b: (acc, aux)[c][:, b, :]
            heads4 = lambda v: wide(v, [P, GROUP, P], 1)
            heads2 = lambda v: wide(v, [P, 2, P], 1)
            def head_norm(g):
                cs = slice(g * GROUP * HD, (g + 1) * GROUP * HD)
                heads = lambda x: x[:, :, cs].rearrange("p t (h d) -> p t h d", d=HD)
                spread = lambda v: v.unsqueeze(3).to_broadcast([P, TT, GROUP, HD])
                sums = stat[:, 0:TT * GROUP].rearrange("p (t h) -> p t h", t=TT)
                dve.wait_ge(m["y_copied"], due(m["y_copied"], TT))
                step(dve.tensor_reduce(sums, heads(tok), AX_X, ALU.add))
                step(dve.tensor_scalar(sums, sums, 1.0 / HD, None, ALU.mult))
                step(dve.tensor_tensor(heads(tok), heads(tok), spread(sums), ALU.subtract))
                step(dve.tensor_tensor(KK[:, :, cs], tok[:, :, cs], tok[:, :, cs], ALU.mult))
                step(dve.tensor_reduce(sums, heads(KK), AX_X, ALU.add))
                dve.tensor_scalar(sums, sums, 1.0 / HD, GN_EPS, ALU.mult, ALU.add).then_inc(m["ms_ready"], 1)
                step(dve.tensor_tensor(heads(IC), heads(V), spread(BONUS[:, :, g * GROUP:(g + 1) * GROUP]), ALU.mult))
                gn = lambda k: wide(DEC[:, k, cs], [P, TT, GROUP * HD], 1)
                step(dve.tensor_tensor(IC[:, :, cs], IC[:, :, cs], gn(1), ALU.add))
                dve.wait_ge(m["rstd_ready"], due(m["rstd_ready"]))
                step(dve.tensor_tensor(heads(tok), heads(tok), spread(rstd[:, 0:TT * GROUP].rearrange("p (t h) -> p t h", t=TT)), ALU.mult))
                step(dve.tensor_tensor(tok[:, :, cs], tok[:, :, cs], gn(0), ALU.mult))
                step(dve.tensor_tensor(tok[:, :, cs], tok[:, :, cs], IC[:, :, cs], ALU.add))

            dve.wait_ge(m["gn_in"], due(m["gn_in"], 32))
            for g in range(HEADS // GROUP):
                for n, dst in enumerate((KTT, BTT)):
                    dve.wait_ge(m["group_turned"], due(m["group_turned"], 3 - 2 * n))
                    for e in range(2):
                        of = slice(e * HD, (e + 1) * HD)
                        last = dve.tensor_copy(dst[of, e:GROUP:2, :], aux[of, 2 + n, :].rearrange("p (k n) -> p k n", k=2))
                    last.then_inc(m["group_copied"], 1)
                for c in range(TT):
                    dve.wait_ge(m["pair_ready"], due(m["pair_ready"]))
                    one = bank(c, 0).rearrange("p (h n) -> p h n", h=GROUP)
                    dve.tensor_tensor(NM[:, c], one, heads4(STRICT[:]), ALU.mult)
                    dve.tensor_tensor(INV[:, c], one, heads4(LMASK[:, 0, :]), ALU.mult)
                    for k in range(2):
                        two = bank(c, 1 + k).rearrange("p (h x n) -> p h x n", h=2, x=2)
                        dve.tensor_tensor(INVT[:, c, 2 * k:2 * k + 2, :], two[:, :, 0, :], heads2(LMASK[:, 1, :]), ALU.mult)
                        last = dve.copy_predicated(RB[:, c, 2 * k:2 * k + 2, :], heads2(PICK[:, 1, :]), two[:, :, 1, :])
                    step(last)
                    dve.tensor_tensor(INV[:, c], INV[:, c], heads4(ident[:]), ALU.add)
                    dve.tensor_tensor(INVT[:, c], INVT[:, c], heads4(ident[:]), ALU.add).then_inc(m["pair_masked"], 1)
                for c in range(TT):
                    dve.wait_ge(m["pair2_ready"], due(m["pair2_ready"]))
                    for k in range(2):
                        two = bank(c, (3, 0)[k]).rearrange("p (h x n) -> p h x n", h=2, x=2)
                        dve.copy_predicated(AK[:, c, 2 * k:2 * k + 2, :], heads2(PICK[:, 0, :]), two[:, :, 0, :])
                        last = dve.copy_predicated(RK[:, c, 2 * k:2 * k + 2, :], heads2(PICK[:, 1, :]), two[:, :, 1, :])
                    last.then_inc(m["pair_masked"], 1)
                for n in range(len(LEVELS)):
                    for c in range(TT):
                        dve.wait_ge(m["level_ready"], due(m["level_ready"]))
                        dve.tensor_tensor(QM[:, c], bank(c, 0).rearrange("p (h n) -> p h n", h=GROUP), heads4(LMASK[:, 2 + n, :]), ALU.mult)\
                           .then_inc(m["level_masked"], 1)
                dve.wait_ge(m["state_ready"], due(m["state_ready"]))
                for k in range(2):
                    for h in range(2):
                        of = slice(h * HD, (h + 1) * HD)
                        dve.tensor_scalar(ST[of, k, h, :], bank(0, 3)[of, k * P + h * HD:k * P + (h + 1) * HD], DCOL[of, 2 * g + k:2 * g + k + 1], None,
                                          ALU.mult).then_inc(m["state_copied"], 1)
                if g:
                    head_norm(g - 1)
            head_norm(HEADS // GROUP - 1)
            dve.wait_ge(m["gate_ready"], due(m["gate_ready"]))
            for t in range(TT):
                cols = tok[:, t, :].rearrange("p (c n) -> p c n", c=2)
                dve.tensor_tensor(cols, cols, acc[:, 2 * t:2 * t + 2, :], ALU.mult).then_inc(m["token_ready"], 1)
            both_operands()
            ahead(q + IN_Q, OUT_Q - 4)

        def ffn(q):

            def hidden(odd, pair):
                dve.wait_ge(m["silu_ready"], due(m["silu_ready"]))
                for t in range(TT):
                    dve.tensor_tensor(HM[:, odd, t, :], SILU[:, odd, t, :], acc[:, 2 * pair + t, 256:512], ALU.mult).then_inc(m["hidden_ready"], 1)

            def hidden_lo(dst, src_hi, odd, done):
                dve.wait_ge(m["hidden_hi"], due(m["hidden_hi"]))
                dve.tensor_tensor(dst, aux[:, odd, :].rearrange("p (k n) -> p k n", k=2), src_hi.bitcast(F32), ALU.subtract).then_inc(done, 1)

            ahead(q, 4)
            hidden(0, 0)
            with due.loop((FB - 1) // 2, {m["silu_ready"]: 2, m["hidden_hi"]: 2}) as i:
                for b in range(2):
                    ahead(q + 4 + 4 * b, 4, (i, 8))
                    hidden(1 - b, 1 - b)
                    ks = bass.ds(i * 4 + 2 * b, 2)
                    hidden_lo(HL[:, ks, :], HH[:, ks, :], b, m["hidden_lo"])
            hidden_lo(HL[:, FK - 2:FK, :], HH[:, FK - 2:FK, :], 0, m["hidden_last"])
            ahead(q + FB * 4, FK - 4)

        def attention(q, near):
            if near:
                dve.wait_ge(m["near_in"], due(m["near_in"], 48))
                step(dve.tensor_scalar(QG[:, 2, :], QG[:, 0, :], HD ** -0.5, None, ALU.mult))
            else:
                dve.wait_ge(m["moba_in"], due(m["moba_in"], 16))
            for j in range(6):
                ahead(q + 4 * j, 4)
                used(q + 4 * j + 3)
                dst, cs, banks = (QTOK, KTOK, VTOK)[j // 2], slice((j % 2) * 512, (j % 2 + 1) * 512), acc[:, 2 * (j % 2):2 * (j % 2) + 2, :]
                if j >= 4:
                    dve.tensor_copy(dst[:, :, cs], banks).then_inc(m["in_done"], 1)
                elif near:
                    own = dst[:, :, cs].rearrange("p t (h d) -> p t h d", d=HD)
                    dve.wait_ge(m["qk_square"], due(m["qk_square"]))
                    dve.tensor_reduce(stat[:, 0:16], ROT[:].rearrange("p t (h d) -> p (t h) d", d=HD), AX_X, ALU.add).then_inc(m["qk_summed"], 1)
                    dve.wait_ge(m["qk_summed"], due(m["qk_summed"]))
                    dve.tensor_scalar(stat[:, 0:16], stat[:, 0:16], 1.0 / HD, RMS_EPS, ALU.mult, ALU.add).then_inc(m["ms_ready"], 1)
                    dve.wait_ge(m["rstd_ready"], due(m["rstd_ready"]))
                    for t in range(TT):
                        last = dve.tensor_tensor(own[:, t], own[:, t], wide(rstd[:, 8 * t:8 * t + 8], [P, 8, HD], 2), ALU.mult)
                    last.then_inc(m["in_done"], 1)
                    dve.wait_ge(m["in_done"], due(m["in_done"]))
                    for t in range(TT):
                        last = dve.tensor_tensor(own[:, t], own[:, t], wide(QG[:, 2 - j // 2, :], [P, 8, HD], 1), ALU.mult)
                    last.then_inc(m["qk_done"], 1)
                    dve.wait_ge(m["qk_done"], due(m["qk_done"]))
                else:
                    for t in range(TT):
                        src = banks[:, t, :].rearrange("p (h d) -> p h d", d=HD)
                        own = dst[:, t, cs].rearrange("p (h d) -> p h d", d=HD)
                        rot = ROT[:, t, :].rearrange("p (h d) -> p h d", d=HD)
                        cos, sin = ROPE[:, t, j // 2, 0, :], ROPE[:, t, j // 2, 1, :]
                        dve.tensor_tensor(own, src, wide(cos, [P, 8, HD], 1), ALU.mult)
                        dve.tensor_tensor(rot[:, :, 0:32], src[:, :, 32:64], wide(sin[:, 0:32], [P, 8, 32], 1), ALU.mult)
                        last = dve.tensor_tensor(rot[:, :, 32:64], src[:, :, 0:32], wide(sin[:, 32:64], [P, 8, 32], 1), ALU.mult)
                    last.then_inc(m["in_done"], 1)
                    dve.wait_ge(m["in_done"], due(m["in_done"]))
                    last = dve.tensor_tensor(dst[:, :, cs], dst[:, :, cs], ROT[:], ALU.add)
                    last.then_inc(m["qk_done"], 1)
                    dve.wait_ge(m["qk_done"], due(m["qk_done"]))
            due(m["in_done"], 2)
            if near:
                dve.wait_ge(m["bias_ready"], due(m["bias_ready"], TT))

            def maxima(p):
                dve.wait_ge(m["scores_ready"], due(m["scores_ready"]))
                for t in range(TT):
                    keys = SEQ if near else (t + 1) * P
                    src = acc[:, 2 * (p % 2):2 * (p % 2) + 2, t * SEQ:(t + 1) * SEQ]
                    if near:
                        step(dve.tensor_tensor(SC[:, p % 2, t], src, BIAS[:, t, 2 * p:2 * p + 2, :], ALU.add))
                        src = SC[:, p % 2, t]
                    last = dve.tensor_reduce(NMAX[:, t, 2 * p:2 * p + 2], src[:, :, 0:keys], AX_X, ALU.max, negate=True)
                last.then_inc(m["max_ready"], 1)

            def copy_probs(p):
                dve.wait_ge(m["probs_turned"], due(m["probs_turned"], 2))
                if near:
                    last = dve.tensor_copy(PT[:, p % 2, 1], aux[:, 1, :].rearrange("p (k n) -> p k n", k=TT))
                else:
                    dve.tensor_copy(PT[:, p % 2, 1, 0, :], aux[:, 1, 0:SEQ])
                    last = dve.tensor_copy(PT[:, p % 2, 1, 1, P:SEQ], aux[:, 1, SEQ + P:2 * SEQ])
                last.then_inc(m["probs_copied_v"], 1)

            def outputs(p):
                dve.wait_ge(m["o_ready"], due(m["o_ready"]))
                two = slice(2 * p, 2 * p + 2)
                step(dve.reciprocal(RSUM[:, :, two], SUMS[:, :, two]))
                for t in range(TT):
                    last = dve.tensor_tensor(tok[:, t, 2 * p * HD:2 * (p + 1) * HD].rearrange("p (h d) -> p h d", h=2),
                                             aux[:, 2 + p % 2, 2 * t * HD:2 * (t + 1) * HD].rearrange("p (h d) -> p h d", h=2),
                                             wide(RSUM[:, t, two], [P, 2, HD], 2), ALU.mult)
                    if p == PAIRS - 1:
                        last.then_inc(m["token_ready"], 1)
                if p < PAIRS - 2:
                    last.then_inc(m["o_done"], 1)

            for p in range(PAIRS + 2):
                if p < PAIRS:
                    maxima(p)
                if 1 <= p <= PAIRS:
                    copy_probs(p - 1)
                if p >= 2:
                    outputs(p - 2)
            both_operands()
            ahead(q + IN_Q, OUT_Q - 4)

        def conv(q, layer):
            tap = lambda n, k: taps[:, layer, n, k:k + 1]
            for j in range(6):
                ahead(q + 4 * j, 4)
                banks = acc[:, 2 * (j % 2):2 * (j % 2) + 2, :]
                ks = range(4 * (j % 2), 4 * (j % 2) + 4)
                part = lambda x: x[:, ks[0]:ks[-1] + 1, :]
                pairs = lambda x: part(x).rearrange("p (b k) n -> p b (k n)", b=2)
                if j >= 2:
                    used(q + 4 * j + 3)
                if j in (2, 3):
                    dve.wait_ge(m["c_done"], due(m["c_done"]))
                    dve.tensor_tensor(pairs(ZT), pairs(CT), banks, ALU.mult).then_inc(m["z_done"], 1)
                    dve.wait_ge(m["z_done"], due(m["z_done"]))
                    for k in ks:
                        last = dve.tensor_scalar(CV[:, k, :], ZT[:, k, :], tap(1, k), None, ALU.mult)
                    step(last)
                    for k in ks:
                        last = dve.scalar_tensor_tensor(out=CV[:, k, 1:SEQ], in0=ZT[:, k, 0:SEQ - 1], scalar=tap(0, k), in1=CV[:, k, 1:SEQ],
                                                        op0=ALU.mult, op1=ALU.add)
                    step(last)
                    for k in ks:
                        last = dve.scalar_tensor_tensor(out=CV[:, k, 0:SEQ - 1], in0=ZT[:, k, 1:SEQ], scalar=tap(2, k), in1=CV[:, k, 0:SEQ - 1],
                                                        op0=ALU.mult, op1=ALU.add)
                    step(last)
                if j >= 4:
                    dve.tensor_tensor(pairs(YT), pairs(CV), banks, ALU.mult).then_inc(m["y_done"], 1)
                    dve.wait_ge(m["conv_hi_done"], due(m["conv_hi_done"]))
                    dve.tensor_tensor(part(OL), part(YT), part(OH).bitcast(F32), ALU.subtract).then_inc(m["conv_lo_done"], 1)
            ahead(q + IN_Q, OUT_Q - 4)

        def hyena(q):
            two = lambda x: x.rearrange("p (c n) -> p c n", c=2)

            def argument(n):
                dve.wait_ge(m["mlp_ready"], due(m["mlp_ready"]))
                step(dve.tensor_scalar(ARG[:, 0, :], aux[0:FHID, 0, 0:SEQ], FCOL[:, n:n + 1], FCOL[:, 2:3], ALU.add, ALU.mult))
                step(dve.tensor_scalar(ARG[:, 1, :], ARG[:, 0, :], 1.0 / TWO_PI, MAGIC, ALU.mult, ALU.add))
                step(dve.tensor_scalar(ARG[:, 1, :], ARG[:, 1, :], -MAGIC, None, ALU.add))
                for c in (-TWO_PI_HI, -TWO_PI_LO):
                    step(dve.scalar_tensor_tensor(out=ARG[:, 0, :], in0=ARG[:, 1, :], scalar=c, in1=ARG[:, 0, :], op0=ALU.mult, op1=ALU.add))
                dve.tensor_scalar(ARG[:, 0, :], ARG[:, 0, :], PI_BELOW, -PI_BELOW, ALU.min, ALU.max).then_inc(m["arg_ready"], 1)

            def window(r, pairs):
                t, d = r // 2, r % 2
                b = 2 * (r % pairs)
                dve.wait_ge(m["filt_ready"], due(m["filt_ready"]))
                dve.tensor_tensor(two(FR[:, 2 * d + t, :]), aux[:, b:b + 2, :], two(WIN[:, t, :]), ALU.mult).then_inc(m["filt_done"], 1)

            def even_odd():
                dve.wait_ge(m["filt_done"], due(m["filt_done"], 4))
                step(dve.tensor_tensor(FR[0:1, 0, :], FR[0:1, 0, :], FR[0:1, 2, :], ALU.add))
                step(dve.memset(FR[0:1, 2, :], 0.0))
                for k, op in enumerate((ALU.add, ALU.subtract)):
                    for t in range(TT):
                        last = dve.tensor_tensor(EO[:, 2 * k + t, :], FR[:, t, :], FR[:, 2 + t, :], op)
                    last.then_inc(m["eo_ready"], 1)

            def convolve(j):
                used(q + 4 * j + 3)
                if j >= 2:
                    dve.wait_ge(m["cv_turned"], due(m["cv_turned"]))
                src = lambda c: acc[:, 2 * (j % 2) + c // 2, (c % 2) * SEQ:(c % 2 + 1) * SEQ]
                tap = lambda n, c: TAPS3[:, n, 4 * j + c:4 * j + c + 1]
                for c in range(4):
                    last = dve.tensor_scalar(HCV[:, j % 2, c, :], src(c), tap(1, c), tap(3, c), ALU.mult, ALU.add)
                step(last)
                for c in range(4):
                    last = dve.scalar_tensor_tensor(out=HCV[:, j % 2, c, 1:SEQ], in0=src(c)[:, 0:SEQ - 1], scalar=tap(0, c),
                                                    in1=HCV[:, j % 2, c, 1:SEQ], op0=ALU.mult, op1=ALU.add)
                step(last)
                for c in range(4):
                    last = dve.scalar_tensor_tensor(out=HCV[:, j % 2, c, 0:SEQ - 1], in0=src(c)[:, 1:SEQ], scalar=tap(2, c),
                                                    in1=HCV[:, j % 2, c, 0:SEQ - 1], op0=ALU.mult, op1=ALU.add)
                last.then_inc(m["cv_ready"], 1)

            def reciprocal():
                dve.wait_ge(m["norm_copied"], due(m["norm_copied"]))
                step(dve.reciprocal(RN[:], RN[:]))

            dve.wait_ge(m["hyena_in"], due(m["hyena_in"], 16 * 10))
            nothing = lambda: None
            pieces = [lambda: argument(0), lambda: argument(1)] + [lambda r=r: window(r, 1) for r in range(4)] + [even_odd] + [nothing] * 4 + [reciprocal]
            for j in range(6):
                ahead(q + 4 * j, 2)
                pieces[2 * j]()
                ahead(q + 4 * j + 2, 2)
                pieces[2 * j + 1]()
                convolve(j)
            due(m["cv_turned"], 2)
            dve.wait_ge(m["freq_done"], due(m["freq_done"], 5))
            for n in range(ORDER):
                for r in range(4):
                    f, c = r // 2, r % 2
                    cs = slice(c * 512, (c + 1) * 512)
                    re, im = acc[:, 2 * (r % 2), :], acc[:, 2 * (r % 2) + 1, :]
                    dve.wait_ge(m["dft_ready"], due(m["dft_ready"]))
                    dve.tensor_tensor(FR[:, f, cs], re, HF[:, f, cs], ALU.mult)
                    dve.tensor_tensor(EO[:, 0, cs], im, HF[:, 3 + f, cs], ALU.mult)
                    dve.tensor_tensor(FR[:, 2 + f, cs], re, HF[:, 3 + f, cs], ALU.mult)
                    step(dve.tensor_tensor(EO[:, 1, cs], im, HF[:, 1 if f else 2, cs], ALU.mult))
                    dve.tensor_tensor(FR[:, f, cs], FR[:, f, cs], EO[:, 0, cs], ALU.subtract)
                    dve.tensor_tensor(FR[:, 2 + f, cs], FR[:, 2 + f, cs], EO[:, 1, cs], ALU.add).then_inc(m["dft_done"], 1)
                    dve.wait_ge(m["dft_done"], due(m["dft_done"]))
                if n:
                    dve.wait_ge(m["skip2_in"], due(m["skip2_in"], 16))
                step(dve.tensor_tensor(HV[:], HV[:], wide(SKIP[:], [P, TT, D], 1), ALU.mult))
                dve.wait_ge(m["idft_ready"], due(m["idft_ready"]))
                if n == 0:
                    for r in range(4):
                        window(r, 2)
                    even_odd()
                    dve.wait_ge(m["cv_copied"], due(m["cv_copied"], 6))
                for t in range(TT):
                    step(dve.tensor_tensor(two(tok[:, t, :]), acc[:, 2 * t:2 * t + 2, :], two(RN[:]), ALU.mult))
                    step(dve.tensor_tensor(tok[:, t, :], tok[:, t, :], HV[:, t, :], ALU.add))
                    if n == 0:
                        last = dve.tensor_tensor(HV[:, t, :], tok[:, t, :], HX1[:, t, :], ALU.mult)
                    else:
                        dve.tensor_tensor(tok[:, t, :], tok[:, t, :], HX2[:, t, :], ALU.mult).then_inc(m["token_ready"], 1)
                if n == 0:
                    last.then_inc(m["idft_done"], 1)
                    dve.wait_ge(m["idft_done"], due(m["idft_done"]))
                    reciprocal()
                    dve.wait_ge(m["freq_done"], due(m["freq_done"], 5))
            both_operands()
            ahead(q + IN_Q, OUT_Q - 4)

        convs = 0
        for n, kind in enumerate(layers):
            if kind == "conv":
                conv(start[n], convs)
                convs += 1
            else:
                {"rwkv": rwkv, "ffn": ffn, "moba": lambda q: attention(q, False), "near": lambda q: attention(q, True),
                 "hyena": hyena}[kind](start[n])
            residual(n, start[n] + (FFN_Q if kind == "ffn" else IN_Q + OUT_Q))

    @block.gpsimd
    def _(pool):
        due = Tally(pool)

        def load(dst, src, done):
            pool.dma_start(dst, src).then_inc(done, 16)

        def rsqrt(n):
            pool.wait_ge(m["ms_ready"], due(m["ms_ready"]))
            pool.tensor_tensor(rstd[:, 0:n], stat[:, 0:n], half[:, 0:n], ALU.pow).then_inc(m["rstd_ready"], 1)

        def power(t, mean_square, scale, eps):
            pool.tensor_scalar(stat[:, t:t + 1], mean_square, scale, eps, ALU.mult, ALU.add).then_inc(m["eps_added"], 1)
            pool.wait_ge(m["eps_added"], due(m["eps_added"]))
            pool.tensor_tensor(rstd[:, t:t + 1], stat[:, t:t + 1], half[:, 0:1], ALU.pow).then_inc(m["rstd_ready"], 1)

        def load_ln(n):
            load(lng[:], A["ln_g"][n].partition_broadcast(P), m["ln_in"])
            load(lnb[:], A["ln_b"][n].partition_broadcast(P), m["ln_in"])

        pool.memset(half[:], -0.5).then_inc(m["halves_set"], 1)
        pool.memset(LW[:], 1.0).then_inc(m["halves_set"], 1)
        pool.memset(LA[:], 1.0).then_inc(m["halves_set"], 1)
        first_loads = [(VEC[:, k, :], A["vec"][k].partition_broadcast(P), m["vec_in"]) for k in range(3)]
        first_loads += [(dst[:], A[name], m["consts_in"]) for dst, name in ((ident, "ident"), (taps, "taps"))]
        first_loads += [(dst[:], A[name], m["vec_in"]) for dst, name in (
            (L2, "lora2"), (CUM, "cum"), (SPAN, "span"), (LMASK, "level_masks"), (STRICT, "strict"), (PICK, "pick"), (G2, "g2a"), (G2b, "g2b"))]
        first_loads += [(X[:, t, :], A["x"][:, t], m["res_in"]) for t in range(TT)]
        for k, what in enumerate(first_loads):
            pool.wait_ge(w_used[k % SLOTS], k // SLOTS + 1)
            load(*what)
        load_ln(0)
        pool.wait_ge(m["consts_in"], due(m["consts_in"], 16 * 2))
        for h in range(GROUP):
            pool.tensor_copy(identb[:, h * P:(h + 1) * P], ident[:]).then_inc(m["identb_set"], 1)
        pool.wait_ge(m["halves_set"], due(m["halves_set"], 3))
        for _ in range(2):
            pool.memset(stat[:, 60:61], 0.0).then_inc(m["hidden_lo"], 1)
            pool.wait_ge(m["hidden_lo"], due(m["hidden_lo"]))

        def rwkv():
            rsqrt(32)
            pool.wait_ge(m["scaled_ready"], due(m["scaled_ready"]))
            for zeros in (AK, RB, RK, KTT, BTT, ST):
                pool.memset(zeros[:], 0.0).then_inc(m["presets"], 1)
            pool.wait_ge(m["exp_ready"], due(m["exp_ready"], 7))
            for k, name in enumerate(("gn_g", "gn_b")):
                load(DEC[:, k, :], A[name].partition_broadcast(P), m["gn_in"])
            for _ in range(HEADS // GROUP):
                rsqrt(TT * GROUP)

        def before(n):
            pool.wait_ge(m["residual_done"], TT * n)

        def load_moba():
            load(ROPE[:], A["rope"], m["moba_in"])
            load(FLIP[:], A["causal"], m["causal_in"])
            pool.wait_ge(m["causal_in"], due(m["causal_in"], 16))
            pool.tensor_copy(CAUSAL[:], FLIP[:]).then_inc(m["causal_set"], 1)

        def load_near():
            load(FLIP[:], A["flip"], m["near_in"])
            load(QG[:, 0, :], A["q_gain"].partition_broadcast(P), m["near_in"])
            load(QG[:, 1, :], A["k_gain"].partition_broadcast(P), m["near_in"])
            load(BMASK[:], A["near_mask"], m["bias_in"])
            rpb = A["rpb"]
            for r in range(ROWS):
                for s in range(ROWS):
                    src = bass.AP(tensor=rpb.tensor, offset=rpb.offset + (s - r + RPB_ROWS // 2) * RPB_PAD,
                                  ap=[[1, GRID_W], [RPB_ROWS * RPB_PAD, HEADS], [1, GRID_W]])
                    of = slice((r % 2) * GRID_W, (r % 2 + 1) * GRID_W)
                    load(BIAS[of, r // 2, :, s * GRID_W:(s + 1) * GRID_W], src, m["bias_in"])
            pool.wait_ge(m["bias_in"], due(m["bias_in"], 16 * (1 + ROWS * ROWS)))
            for t in range(TT):
                pool.tensor_tensor(BIAS[:, t], BIAS[:, t], BMASK[:, t, :].unsqueeze(1).to_broadcast([P, HEADS, SEQ]), ALU.add)\
                    .then_inc(m["bias_ready"], 1)

        def load_hyena():
            pool.memset(ONES[:], 1.0).then_inc(m["ones_set"], 1)
            for dst, name in ((WIN, "window"), (DFT, "dft"), (IDFT, "idft"), (EMBT, "emb"), (TAPS3, "taps3"), (FCOL, "f_cols")):
                load(dst[:], A[name], m["hyena_in"])
            load(SKIP[:], A["f_skip"][0].partition_broadcast(P), m["hyena_in"])
            load(FW[0:EMB, 0, :], A["f_w1"], m["hyena_in"])
            load(FW[:, 1, :], A["f_w2"], m["hyena_in"])
            load(FW3[:], A["f_w3"][0], m["hyena_in"])

        def near():
            for _ in range(4):
                rsqrt(16)

        def hyena():
            pool.wait_ge(m["filt_done"], due(m["filt_done"], 4))
            load(FW3[:], A["f_w3"][1], m["taps2_in"])
            pool.wait_ge(m["idft_done"], due(m["idft_done"]))
            load(SKIP[:], A["f_skip"][1].partition_broadcast(P), m["skip2_in"])

        def norms(n):
            rms = LAYER_NORMS - 1 <= n < len(layers) - 1
            for t in range(TT):
                if n < LAYER_NORMS:
                    pool.wait_ge(m["ms_ready"], due(m["ms_ready"]))
                    power(t, mom[:, t, 1:2], 1.0, LN_EPS)
                if rms:
                    pool.wait_ge(m["square_ready"], due(m["square_ready"]))
                    power(t, stat[:, 56 + t:57 + t], 1.0 / D, RMS_EPS)
            operands = sum(8 if kind in ("rwkv", "moba", "near", "hyena") else 4 for kind in layers[:n + 1])
            if n + 1 < len(layers):
                pool.wait_ge(m["operand_ready"], operands)
                if n + 1 < LAYER_NORMS:
                    load_ln(n + 1)
                elif n + 2 < len(layers):
                    load(lng[:], A["gains"][n + 1 - LAYER_NORMS + 1].partition_broadcast(P), m["gain_in"])

        ahead_of = {"moba": load_moba, "near": load_near, "hyena": load_hyena}
        inside = {"rwkv": rwkv, "near": near, "hyena": hyena}
        for n, kind in enumerate(layers):
            if kind in inside:
                inside[kind]()
            if n + 1 < len(layers):
                before(n)
                if layers[n + 1] in ahead_of:
                    ahead_of[layers[n + 1]]()
                if n == LAYER_NORMS - 1:
                    load(FIRSTG[:], A["gains"][0].partition_broadcast(P), m["gain_in"])
            norms(n)

    ctx.close()


def constants():
    c = {}
    f32 = np.float32
    i, j = np.arange(P)[:, None], np.arange(P)[None, :]
    c["ident"] = np.eye(P, dtype=f32)
    middle = i < P // 2
    c["cum"] = np.stack([-DECAY * ((i <= j).astype(f32) - middle), -DECAY * ((i < j).astype(f32) - middle)], 1).astype(f32)
    c["span"] = (-DECAY * np.stack([np.arange(P) >= P // 2, np.arange(P) < P // 2], 1)).astype(f32)
    c["strict"] = (j < i).astype(f32)
    low = lambda a, b, n: (a // n % 2 == 1) & (b // n % 2 == 0) & (a // (2 * n) == b // (2 * n))
    eye = np.eye(P)
    c["level_masks"] = np.stack([low(i, j, 1) + 0 * eye, low(j, i, 1) + 0 * eye] + [low(j, i, n) + eye for n in LEVELS], 1).astype(f32)
    c["pick"] = np.stack([(i < j), (i <= j)], 1).astype(np.uint32)
    inv = (f32(10000.0) ** (-np.arange(0, HD, 2, dtype=f32) / f32(HD))).astype(f32)
    ang = np.arange(SEQ, dtype=f32)[:, None] * inv[None, :]
    cos, sin = np.cos(ang).astype(f32), np.sin(ang).astype(f32)
    both = np.stack([np.concatenate([cos, cos], 1), np.concatenate([-sin, sin], 1)], 1)
    rope = np.stack([both * f32(HD ** -0.5), both], 1)
    c["rope"] = rope.reshape(TT, P, 2, 2, HD).transpose(1, 0, 2, 3, 4).astype(f32)
    c["causal"] = np.where(j <= i, 0.0, -3.0e38).astype(f32)
    c["flip"] = (i // GRID_W * GRID_W + GRID_W - 1 - i % GRID_W == j).astype(f32)
    col = np.arange(GRID_W)
    first = np.clip(col - 8, 0, GRID_W - 16)
    sees = (col[None, :] >= first[:, None]) & (col[None, :] < first[:, None] + 16)
    c["near_mask"] = np.tile(np.where(sees[::-1], 0.0, -3.0e38), (ROWS, ROWS)).reshape(TT, P, SEQ).transpose(1, 0, 2).astype(f32)
    t = np.linspace(0.0, 1.0, SEQ, dtype=f32)[:, None]
    bands = np.linspace(1e-4, BANDS - 1, BANDS, dtype=f32)
    ang = (f32(TWO_PI) * np.arange(SEQ, dtype=f32)[:, None] / f32(SEQ) * bands).astype(f32)
    c["emb"] = np.concatenate([t, np.cos(ang), -np.sin(ang)], 1).astype(f32).T
    lt = np.log(1e-2)
    deltas = np.abs(np.linspace(lt / 1.5, lt / 0.3, D, dtype=f32))
    c["window"] = np.exp(-t * deltas).astype(f32).reshape(TT, P, D).transpose(1, 0, 2)
    n = 2 * SEQ
    w = 2.0 * np.pi / n * (np.arange(SEQ)[:, None] * np.arange(SEQ)[None, :] % n)
    re, im, nyquist = np.cos(w), -np.sin(w), np.cos(np.pi * np.arange(SEQ))
    put = lambda a: np.concatenate([nyquist[:, None], a[:, 1:P]], 1)
    dft = np.stack([re[:, :P], re[:, P:], put(im), im[:, P:], im[:, :P], put(re)], 1)
    c["dft"] = dft.reshape(TT, P, 6, P).transpose(1, 0, 2, 3).astype(f32)
    back_re, back_im = 2.0 * re.T / n, 2.0 * im.T / n
    back_re[0] /= 2.0
    back_im[0] = nyquist / n
    c["idft"] = np.concatenate([back_re, back_im]).reshape(4, P, SEQ).transpose(1, 0, 2).astype(f32)
    return {k: np.ascontiguousarray(v) for k, v in c.items()}


def column_blocks(w):
    return w.reshape(4, 2, P, -1, 512).transpose(3, 0, 2, 1, 4).reshape(-1, P, QW)


def layout(x, **w):
    a = constants()
    rows = lambda v: v.reshape(-1, P)
    quarters = []

    def ffn(w_in, w_down):
        blocks = w_in.reshape(4, 2, P, 2, FB, 256).transpose(4, 0, 2, 1, 3, 5).reshape(-1, P, QW)
        quarters.extend([blocks, w_down.reshape(FK, P, D)])

    def mixer(w_in, w_out):
        quarters.extend([column_blocks(w_in), w_out.reshape(KT, P, D)])

    def gated(w_in):
        b, c, u = np.split(w_in, 3, axis=1)
        return np.concatenate([c, u, b], axis=1)

    mixer(np.concatenate(list(w["rwkv_w_rkv"][0]), axis=1), w["rwkv_w_o"][0])
    ffn(w["ffn_w_in"][0], w["ffn_w_down"][0])
    mixer(w["moba_w_qkv"][0], w["moba_w_o"][0])
    ffn(w["ffn_w_in"][1], w["ffn_w_down"][1])
    mixer(gated(w["a_w_in_2"][0]), w["a_w_out_2"][0])
    ffn(w["f_w13_2"][0], w["f_w2_2"][0])
    mixer(w["b_w_qkv_2"][0], w["b_w_out_2"][0])
    ffn(w["f_w13_2"][1], w["f_w2_2"][1])
    mixer(w["c_w_in_2"][0], w["c_w_out_2"][0])
    ffn(w["f_w13_2"][2], w["f_w2_2"][2])
    mixer(gated(w["a_w_in_2"][1]), w["a_w_out_2"][1])
    ffn(w["f_w13_2"][3], w["f_w2_2"][3])
    a["weights"] = np.concatenate(quarters)

    a["x"] = x[0].reshape(TT, P, D).transpose(1, 0, 2)
    a["xT"] = x[0].T.reshape(KT, P, SEQ).transpose(1, 0, 2)
    a["mu"] = w["rwkv_mu"][0].reshape(6, KT, P).transpose(2, 0, 1)
    lora1 = np.concatenate([w["rwkv_w1"][0], w["rwkv_a1"][0], w["rwkv_g1"][0]], axis=1)
    a["lora1"] = lora1.reshape(KT, P, -1).transpose(1, 0, 2)
    a["lora2"] = np.stack([np.concatenate([w["rwkv_w2"][0], w["rwkv_w0"]]), np.concatenate([w["rwkv_a2"][0], w["rwkv_a0"]])], axis=1)
    a["vec"] = np.concatenate([w["rwkv_k_k"], w["rwkv_k_a"], w["rwkv_r_k"].reshape(1, D)])
    a["g2a"], a["g2b"] = w["rwkv_g2"][0, :P], w["rwkv_g2"][0, P:]
    a["gn_g"], a["gn_b"] = w["rwkv_gn_g"][0], w["rwkv_gn_b"][0]
    a["ln_g"] = np.stack([w["ln_mix_g"][0], w["ln_ffn_g"][0], w["ln_mix_g"][1], w["ln_ffn_g"][1]])
    a["ln_b"] = np.stack([w["ln_mix_b"][0], w["ln_ffn_b"][0], w["ln_mix_b"][1], w["ln_ffn_b"][1]])
    a["gains"] = np.stack([w["norm_mix_g_2"], w["norm_ffn_g_2"]], 1).reshape(8, D)
    a["taps"] = w["a_conv_w_2"].reshape(2, 3, KT, P).transpose(3, 0, 1, 2)
    a["q_gain"], a["k_gain"] = w["b_q_norm_g_2"][0], w["b_k_norm_g_2"][0]
    pad = (RPB_PAD - RPB_COLS) // 2
    a["rpb"] = np.pad(w["b_rpb_2"][0], ((0, 0), (0, 0), (pad, pad)))
    a["taps3"] = np.concatenate([w["c_short_w_2"][0], w["c_short_b_2"]]).reshape(4, 3 * KT, P).transpose(2, 0, 1)
    a["f_w1"], a["f_w2"] = w["c_f_w1_2"][0], w["c_f_w2_2"][0]
    a["f_w3"] = w["c_f_w3_2"][0].reshape(FHID, ORDER, 2 * D).transpose(1, 0, 2)
    a["f_cols"] = np.stack([w["c_f_b1_2"][0], w["c_f_b2_2"][0], w["c_f_freq_2"][0]], axis=1)
    a["f_skip"] = w["c_f_skip_2"][0]
    return {k: np.ascontiguousarray(v) for k, v in a.items()}


def kernel(**inputs):
    import concourse.bacc as bacc
    from concourse.bass_utils import run_bass_kernel_spmd

    arrays = layout(**{k: np.asarray(v) for k, v in inputs.items()})
    nc = bacc.Bacc("TRN2", target_bir_lowering=False, num_devices=1)
    A = {k: nc.dram_tensor(f"in_{k}", v.shape, mybir.dt.from_np(v.dtype), kind="ExternalInput").ap() for k, v in arrays.items()}
    out = nc.dram_tensor("out_x", (SEQ, D), F32, kind="ExternalOutput").ap()
    program(nc, A, out.rearrange("(t p) c -> p t c", p=P))
    r = run_bass_kernel_spmd(nc, [{f"in_{k}": v for k, v in arrays.items()}], core_ids=[0])
    return r.results[0]["out_x"].reshape(1, SEQ, D)
```

```python
from contextlib import ExitStack, contextmanager

import numpy as np

import concourse.bass as bass
from concourse import mybir

F32 = mybir.dt.float32
F32R = mybir.dt.float32r
BF16 = mybir.dt.bfloat16
U32 = mybir.dt.uint32
ALU = mybir.AluOpType
ACT = mybir.ActivationFunctionType
AX_X = mybir.AxisListType.X

P = 128
SEQ, D = 256, 1024
TT, KT = SEQ // P, D // P
HEADS, HD = 16, 64
PAIRS = HEADS // 2
FF = 2816
FK = FF // P
FB = FF // 256
SLOTS = 4
QW = 1024
LORA, GLORA = 64, 160
ALPHA = 4.0 ** 0.25
LN_EPS, RMS_EPS, GN_EPS = 1e-5, 1e-6, HD * 1e-5
DECAY = float(np.exp(-0.5))
LEVELS = (2, 4, 8, 16, 32, 64)
GROUP = 4
GRID_W, ROWS = 64, SEQ // 64
RPB_ROWS, RPB_COLS, RPB_PAD = 15, 31, 127
MAGIC = 1.5 * 2.0 ** 23
TWO_PI = 2.0 * np.pi
TWO_PI_HI = float(np.float32(TWO_PI))
TWO_PI_LO = float(TWO_PI - TWO_PI_HI)
PI_BELOW = 3.1415925
ORDER, BANDS, FHID = 2, 16, 64
SPECTRA = ((0, 0), (0, 1), (0, 5), (1, 4), (1, 3))
EMB = 1 + 2 * BANDS
IN_Q, OUT_Q, FFN_Q = 3 * D // 512 * 4, KT, FB * 4 + FK
LAYERS = ("rwkv", "ffn", "moba", "ffn", "conv", "ffn", "near", "ffn", "hyena", "ffn", "conv", "ffn")
LAYER_NORMS = 4


class Tally:

    def __init__(self, engine):
        self.engine, self.count, self.inside = engine, {}, None

    def __call__(self, sem, n=1):
        self.count[sem.name] = self.count.get(sem.name, 0) + n
        if self.inside is None:
            return self.count[sem.name]
        i, each = self.inside
        return i * each[sem.name] + self.count[sem.name]

    @contextmanager
    def loop(self, times, each):
        each = {sem.name: n for sem, n in each.items()}
        before = dict(self.count)
        with self.engine.Fori(0, times) as i:
            self.inside = (i, each)
            yield i
            self.inside = None
        for name, n in self.count.items():
            assert n - before.get(name, 0) == each.get(name, 0), (name, n - before.get(name, 0))
        for name, n in each.items():
            self.count[name] = before.get(name, 0) + n * times


def program(nc, A, out, layers=LAYERS):
    ctx = ExitStack()
    quarters = sum(FFN_Q if kind == "ffn" else IN_Q + OUT_Q for kind in layers)

    def keep(name, shape, dtype=F32):
        return ctx.enter_context(nc.sbuf_tensor(name, shape, dtype))

    def sem(name):
        return ctx.enter_context(nc.semaphore(name))

    def scope(*tensors):
        with ExitStack() as s:
            return [s.enter_context(nc.sbuf_tensor(n, shape, (dtype or [F32])[0])) for n, shape, *dtype in tensors]

    X = keep("residual", [P, TT, D])
    raw = keep("w_raw", [P, SLOTS, QW])
    whi = keep("w_hi", [P, SLOTS, QW], F32R)
    wlo = keep("w_lo", [P, SLOTS, QW], F32R)
    ah, al = scope(("operand_hi", [P, KT, SEQ], F32R), ("operand_lo", [P, KT, SEQ], F32R))
    taps2 = keep("second_taps", [P, 4, D])
    tok = keep("token_scratch", [P, TT, D])
    ident = keep("ident_sb", [P, P])
    identb = keep("identb_sb", [P, GROUP * P], BF16)
    taps = keep("taps_sb", [P, 2, 3, KT])
    lng = keep("ln_gain", [P, D])
    lnb = keep("ln_bias", [P, D])
    half = keep("minus_half", [P, 32])
    stat = keep("stat", [P, 64])
    mom = keep("moments", [P, TT, 2])
    rstd = keep("rstd", [P, 32])
    acc = ctx.enter_context(nc.psum_tensor("acc", [P, 4, 512], F32))
    aux = ctx.enter_context(nc.psum_tensor("aux", [P, 4, 512], F32))

    with ExitStack() as s:
        def rwkv(name, shape, dtype=F32):
            return s.enter_context(nc.sbuf_tensor(name, shape, dtype))

        R, K, V = rwkv("r_rw", [P, TT, D]), rwkv("k_rw", [P, TT, D]), rwkv("v_rw", [P, TT, D])
        IC = rwkv("iclr_rw", [P, TT, D])
        KK = rwkv("kk_rw", [P, TT, D])
        DEC = rwkv("decay_rw", [P, TT, D])
        TMP = rwkv("tmp_rw", [P, TT, D])
        G2 = rwkv("g2_rw", [P, D])
        G2b = rwkv("g2b_rw", [GLORA - P, D])
        SG, SGb = rwkv("sg_rw", [P, SEQ]), rwkv("sgb_rw", [GLORA - P, SEQ])
        CUM = rwkv("cum_rw", [P, 2, P])
        SPAN = rwkv("span_rw", [P, TT])
        DCOL = rwkv("decay_col", [P, KT])
        LMASK = rwkv("level_masks", [P, len(LEVELS), P])
        STRICT = rwkv("strict_mask", [P, P])
        PICK = rwkv("pick_masks", [P, 4, P], U32)
        BONUS = rwkv("bonus_rw", [P, TT, HEADS])
        VEC, L1, L2, LW, LA, MU = scope(
            ("vec_rw", [P, 3, D]), ("l1_rw", [P, KT, 2 * LORA + GLORA]), ("l2_rw", [LORA + 1, 2, D]),
            ("lora_w", [LORA + 1, SEQ]), ("lora_a", [LORA + 1, SEQ]), ("mu_sb", [P, 6, KT]))
        NM, INV, INVT, QM, U, RHS, ART, KTT, BTT, AK, RB, RK, ST = scope(
            ("n_rw", [P, TT, GROUP, P]), ("inv_rw", [P, TT, GROUP, P]), ("invt_rw", [P, TT, GROUP, P]),
            ("q_rw", [P, TT, GROUP, P]), ("u_rw", [P, TT, GROUP * HD]), ("rhs_rw", [P, GROUP * HD]),
            ("ar_turned", [P, 2, TT, 2, P]), ("k_turned", [P, GROUP, SEQ]), ("b_turned", [P, GROUP, SEQ]),
            ("ak_rw", [P, TT, GROUP, P]), ("rb_rw", [P, TT, GROUP, P]), ("rk_rw", [P, TT, GROUP, P]),
            ("state_rw", [P, 2, 2, HD]))
    L1_FLAT = L1[:].rearrange("p k n -> p (k n)")
    DECAYS = [(L1_FLAT[:, 0:D], L1_FLAT[:, D:2 * D], tok[:, 0, :]), (VEC[:, 1, :], VEC[:, 0, :], VEC[:, 2, :])]
    XT, XX = IC[:].rearrange("p t (k n) -> p (t k) n", n=SEQ), DEC[:].rearrange("p t (k n) -> p (t k) n", n=SEQ)
    MIX = [TMP[:].rearrange("p t (k n) -> p (t k) n", n=SEQ), KK[:].rearrange("p t (k n) -> p (t k) n", n=SEQ)]

    HH, HL, SILU, HM, FIRSTG = scope(
        ("hidden_hi", [P, FK, SEQ], F32R), ("hidden_lo", [P, FK, SEQ], F32R),
        ("silu_ff", [P, 2, TT, 256]), ("hidden_ff", [P, 2, TT, 256]), ("first_rms_gain", [P, D]))
    QTOK, KTOK, VTOK, QT, KTT2, SC, PR, PT, SUMS, NMAX, RSUM, ROPE, ROT, CAUSAL, QG, BIAS, BMASK, FLIP = scope(
        ("q_at", [P, TT, D]), ("k_at", [P, TT, D]), ("v_at", [P, TT, D]), ("q_turned", [P, KT, SEQ]),
        ("k_turned_at", [P, KT, SEQ]), ("scores_at", [P, 2, TT, 2, SEQ]), ("probs_at", [P, 2, TT, 2, SEQ]),
        ("probs_turned", [P, 2, 2, TT, SEQ]), ("sums_at", [P, TT, HEADS]), ("nmax_at", [P, TT, HEADS]),
        ("rsum_at", [P, TT, HEADS]), ("rope_sb", [P, TT, 2, 2, HD]), ("rot_at", [P, TT, 512]),
        ("causal_sb", [P, P], BF16), ("qk_gain", [P, 3, HD]), ("bias_at", [P, TT, HEADS, SEQ]),
        ("bias_mask", [P, TT, SEQ]), ("flip_sb", [P, P]))
    OH, OL, CT, ZT, CV, YT = scope(
        ("conv_hi", [P, KT, SEQ], F32R), ("conv_lo", [P, KT, SEQ], F32R), ("c_conv", [P, KT, SEQ]),
        ("z_conv", [P, KT, SEQ]), ("conv_out", [P, KT, SEQ]), ("y_conv", [P, KT, SEQ]))
    HV, HX1, HX2, HF, FR, EO, WIN, SKIP, RN, DFT, IDFT, EMBT, FW, FW3, TAPS3, FCOL, H1, ARG, ONES = scope(
        ("v_hy", [P, TT, D]), ("x1_hy", [P, TT, D]), ("x2_hy", [P, TT, D]), ("filter_freq", [P, 5, D]),
        ("taps_or_freq", [P, 4, D]), ("even_odd", [P, 4, D]), ("window_sb", [P, TT, D]), ("skip_sb", [P, D]),
        ("norm_hy", [P, D]), ("dft_sb", [P, TT, 6, P]), ("idft_sb", [P, 4, SEQ]), ("emb_sb", [EMB, SEQ]),
        ("f_w12", [FHID, 2, FHID]), ("f_w3_sb", [FHID, 2 * D]), ("taps3_sb", [P, 4, 3 * KT]), ("f_cols", [FHID, 3]),
        ("hid_hy", [FHID, SEQ]), ("arg_hy", [FHID, 2, SEQ]), ("ones_sb", [P, P]))
    HCV = tok[:].rearrange("p b (k n) -> p b k n", n=SEQ)
    TAPS = [[x[:, k, :] for k in range(4)] for x in (FR, taps2)]

    w_full = [sem(f"w_full{s}") for s in range(SLOTS)]
    w_hi = [sem(f"w_hi{s}") for s in range(SLOTS)]
    w_lo = [sem(f"w_lo{s}") for s in range(SLOTS)]
    w_used = [sem(f"w_used{s}") for s in range(SLOTS)]
    m = {n: sem(n) for n in (
        "x_in", "x2_in", "rwkv_in", "vec_in", "gn_in", "consts_in", "res_in", "ln_in", "moba_in", "causal_in", "near_in", "bias_in", "hyena_in", "taps2_in", "skip2_in",
        "halves_set", "presets", "ones_set", "identb_set", "causal_set", "bias_ready",
        "gain_in", "half_done", "residual_done", "ln_done", "square_ready", "eps_added", "ms_ready", "rstd_ready", "token_ready", "turned", "hi_ready", "operand_ready", "dve_step",
        "mix_f_ready", "mix_ready", "rkv_done", "lora1_ready", "lora_mid", "lora2_ready", "lora_out", "cum_ready", "span_ready",
        "exp_ready", "k_done", "bonus_ready", "scaled_ready",
        "group_turned", "group_copied", "pair_ready", "pair_masked", "pair2_ready", "pair2_masked", "inverse_set", "art_used", "level_ready", "level_masked", "level2_ready",
        "level_copied", "rhs_ready", "rhs_copied", "u_ready", "u_copied", "state_ready", "state_copied", "y_ready", "y_copied",
        "gate_ready",
        "silu_ready", "hidden_ready", "hidden_turned", "hidden_hi", "hidden_lo", "hidden_last",
        "in_done", "qk_square", "qk_summed", "qk_done", "qk_turned", "qk_copied", "scores_ready", "max_ready", "probs_ready",
        "probs_turned", "probs_copied_a", "probs_copied_v", "o_ready", "o_done",
        "c_done", "z_done", "y_done", "conv_hi_done", "conv_lo_done",
        "mlp_ready", "arg_ready", "mlp_done", "filt_ready", "filt_done", "filt_abs", "filt_summed", "tap0_joined", "eo_ready", "norm_ready", "norm_copied", "freq_ready", "freq_done",
        "cv_ready", "cv_turned", "cv_copied", "dft_ready", "dft_done", "idft_ready", "idft_done",
        "y_final", "out_written")}

    PE_PASSES = ((0, 0), (0, 1), (1, 0))
    W = (whi, wlo)

    def freq_pair(k, pairs):
        return (k + (k == 4)) % pairs

    def nth(q, at=None):
        n = q // SLOTS + 1
        return n if at is None else at[0] * (at[1] // SLOTS) + n

    start = {}
    total = 0
    for n, kind in enumerate(layers):
        start[n] = total
        total += FFN_Q if kind == "ffn" else IN_Q + OUT_Q

    block = ctx.enter_context(nc.Block())

    @block.sync
    def _(sp):
        sp.dma_start(MU[:], A["mu"]).then_inc(m["x_in"], 16)
        sp.dma_start(XT[:, 0:4, :], A["xT"][:, 0:4, :]).then_inc(m["x_in"], 16)
        sp.dma_start(XT[:, 4:KT, :], A["xT"][:, 4:KT, :]).then_inc(m["x2_in"], 16)
        for q in range(SLOTS):
            sp.dma_start(raw[:, q, :], A["weights"][q]).then_inc(w_full[q], 16)
        sp.dma_start(L1[:], A["lora1"]).then_inc(m["rwkv_in"], 16)
        rest = (quarters - SLOTS) // SLOTS
        with sp.Fori(0, rest) as i:
            for s in range(SLOTS):
                sp.wait_ge(w_lo[s], i + 1)
                sp.dma_start(raw[:, s, :], A["weights"][bass.ds(i * SLOTS + (SLOTS + s), 1)].rearrange("q p n -> (q p) n"))\
                  .then_inc(w_full[s], 16)
        for q in range((rest + 1) * SLOTS, quarters):
            sp.wait_ge(w_lo[q % SLOTS], nth(q) - 1)
            sp.dma_start(raw[:, q % SLOTS, :], A["weights"][q]).then_inc(w_full[q % SLOTS], 16)
        for t in range(TT):
            sp.wait_ge(m["y_final"], t + 1)
            sp.dma_start(out[:, t], X[:, t, :]).then_inc(m["out_written"], 16)
        sp.wait_ge(m["out_written"], 16 * TT)

    @block.tensor
    def _(pe):
        due = Tally(pe)

        def part_tokens(q, i, pair, t):
            s = (q + i) % SLOTS
            for kk in range(2):
                kt = 2 * i + kk
                for x, w in PE_PASSES:
                    mm = pe.matmul(acc[:, 2 * pair + t, :], (ah, al)[x][:, kt, t * P:(t + 1) * P],
                                   W[w][:, s, kk * 512:(kk + 1) * 512],
                                   start=(kt == 0 and (x, w) == (0, 0)), stop=(kt == KT - 1 and (x, w) == (1, 0)))
            return mm

        def block_tokens(q, pair, at=None, operand_half=None):
            for i in range(4):
                if operand_half and i % 2 == 0:
                    operand_half()
                pe.wait_ge(w_lo[(q + i) % SLOTS], nth(q + i, at))
                for t in range(TT):
                    mm = part_tokens(q, i, pair, t)
                mm.then_inc(w_used[(q + i) % SLOTS], 1)

        def first_block(q, src, turn_after):
            turn(src, 0)
            for t in range(TT):
                for i in range(4):
                    if i % 2 == 0:
                        pe.wait_ge(m["operand_ready"], due(m["operand_ready"]))
                    if t == 0:
                        pe.wait_ge(w_lo[(q + i) % SLOTS], nth(q + i))
                    mm = part_tokens(q, i, 0, t)
                    if t == TT - 1:
                        mm.then_inc(w_used[(q + i) % SLOTS], 1)
                    elif i == turn_after:
                        turn(src, 1)

        def block_channels(q, pair, operand_waits=False, after={}):
            for i in range(4):
                s = (q + i) % SLOTS
                if operand_waits and i % 2 == 0:
                    pe.wait_ge(m["operand_ready"], due(m["operand_ready"], 3 if i == 0 else 1))
                pe.wait_ge(w_lo[s], nth(q + i))
                for kk in range(2):
                    kt = 2 * i + kk
                    for c in range(4):
                        for x, w in PE_PASSES:
                            mm = pe.matmul(acc[:, 2 * pair + c // 2, (c % 2) * SEQ:(c % 2 + 1) * SEQ],
                                           W[w][:, s, kk * 512 + c * P:kk * 512 + (c + 1) * P], (ah, al)[x][:, kt, :],
                                           start=(kt == 0 and c % 2 == 0 and (x, w) == (0, 0)),
                                           stop=(kt == KT - 1 and c % 2 == 1 and (x, w) == (1, 0)), skip_group_check=True)
                mm.then_inc(w_used[s], 1)
                if i in after:
                    after[i]()

        def project(q, tiles, hi, lo, before, first=0):
            steps = [(kt, t) for t in (first, 1 - first) for kt in range(4)]
            steps += [(kt, t) for kt in range(4, tiles - 4) for t in range(TT)]
            steps += [(kt, t) for t in range(TT) for kt in range(tiles - 4, tiles)]
            seen = set()
            for kt, t in steps:
                s = (q + kt) % SLOTS
                if (kt, t) in before:
                    before[kt, t]()
                if kt not in seen:
                    pe.wait_ge(w_lo[s], nth(q + kt))
                for c in range(2):
                    for x, w in PE_PASSES:
                        mm = pe.matmul(acc[:, 2 * t + c, :], (hi, lo)[x][:, kt, t * P:(t + 1) * P],
                                       W[w][:, s, c * 512:(c + 1) * 512],
                                       start=(kt == 0 and (x, w) == (0, 0)), stop=(kt == tiles - 1 and (x, w) == (1, 0)))
                if kt in seen:
                    mm.then_inc(w_used[s], 1)
                elif kt == tiles - 1:
                    mm.then_inc(m["half_done"], 1)
                seen.add(kt)

        def operand_steps():
            wait = lambda n: lambda: pe.wait_ge(m["operand_ready"], due(m["operand_ready"], n))
            return {(0, 0): wait(1), (0, 1): wait(2), (4, 1): wait(1)}

        def turn_tile(dst, src, flipped=False):
            return pe.matmul(dst, src, FLIP[:], start=True, stop=True) if flipped else pe.transpose(dst, src, ident[:])

        def turn(src, t, ready=1, flipped=False):
            if ready:
                pe.wait_ge(m["token_ready"], due(m["token_ready"], ready))
            for kt in range(KT):
                mm = turn_tile(aux[:, 2 * t + kt // 4, (kt % 4) * P:(kt % 4 + 1) * P], src[:, t, kt * P:(kt + 1) * P], flipped)
                if kt % 4 == 3:
                    mm.then_inc(m["turned"], 1)

        def rwkv(q):
            def lora1(lo, hi, bank, src):
                for kt in range(KT):
                    mm = pe.matmul(aux[0:hi - lo, bank, 0:SEQ], L1[:, kt, lo:hi], src[:, kt, :],
                                   start=(kt == 0), stop=(kt == KT - 1))
                return mm

            def mix_half():
                pe.wait_ge(m["mix_ready"], due(m["mix_ready"]))

            def mixed(mixes):
                pe.wait_ge(m["mix_f_ready"], due(m["mix_f_ready"], 2 * mixes))

            def pair(q, first=False):
                for b in range(2):
                    if not first:
                        pe.wait_ge(m["rkv_done"], due(m["rkv_done"]))
                    block_tokens(q + 4 * b, b, operand_half=None if b else mix_half)

            pair(q, True)
            pe.wait_ge(m["rwkv_in"], due(m["rwkv_in"], 16))
            mixed(3)
            lora1(0, LORA, 0, MIX[0]).then_inc(m["lora1_ready"], 1)
            pair(q + 8)
            mixed(2)
            lora1(LORA, 2 * LORA, 1, MIX[0]).then_inc(m["lora1_ready"], 1)
            pair(q + 16)
            mixed(1)
            lora1(2 * LORA, 2 * LORA + P, 2, MIX[0])
            lora1(2 * LORA + P, 2 * LORA + GLORA, 3, MIX[0]).then_inc(m["lora1_ready"], 1)
            pe.wait_ge(m["vec_in"], due(m["vec_in"], 16 * 11))
            pe.wait_ge(m["consts_in"], due(m["consts_in"], 16 * 2))
            pe.wait_ge(m["identb_set"], due(m["identb_set"], GROUP))
            pe.wait_ge(m["lora_mid"], due(m["lora_mid"], 3))
            for t in range(TT):
                for c in range(2):
                    mm = pe.matmul(aux[:, 2 * t + c, :], LW[:, t * P:(t + 1) * P], L2[:, 0, c * 512:(c + 1) * 512], start=True, stop=True)
            mm.then_inc(m["lora2_ready"], 1)
            pe.wait_ge(m["rkv_done"], due(m["rkv_done"], 2))
            for t in range(TT):
                for c in range(2):
                    mm = pe.matmul(acc[:, 2 * t + c, :], LA[:, t * P:(t + 1) * P], L2[:, 1, c * 512:(c + 1) * 512], start=True, stop=True)
            mm.then_inc(m["lora2_ready"], 1)
            for t, banks in enumerate((aux, acc)):
                pe.wait_ge(m["lora_out"], due(m["lora_out"]))
                for e in range(2):
                    for c in range(2):
                        mm = pe.matmul(banks[:, 2 * e + c, :], CUM[:, e, :], DEC[:, t, c * 512:(c + 1) * 512], start=True, stop=True)
                mm.then_inc(m["cum_ready"], 1)
            pe.wait_ge(m["exp_ready"], due(m["exp_ready"], 3))
            for k in range(KT):
                for t in range(TT):
                    mm = pe.matmul(aux[:, 0, k:k + 1], DEC[:, t, k * P:(k + 1) * P], SPAN[:, t:t + 1], start=(t == 0), stop=(t == TT - 1))
            mm.then_inc(m["span_ready"], 1)
            pe.wait_ge(m["exp_ready"], due(m["exp_ready"], 4))
            due(m["scaled_ready"])
            bank = lambda c, b: (acc, aux)[c][:, b, :]
            groups = HEADS // GROUP
            head = lambda g, h: slice((GROUP * g + h) * HD, (GROUP * g + h + 1) * HD)
            tiles = lambda g, k: slice((2 * g + k) * P, (2 * g + k + 1) * P)
            own = lambda h: slice(h * HD, (h + 1) * HD)

            def turn_group(n, g):
                for k in range(2):
                    for t in range(TT):
                        mm = pe.transpose(acc[:, (0, 1, 3, 2)[n], k * SEQ + t * P:k * SEQ + (t + 1) * P],
                                          (R, KK, K, IC)[n][:, t, tiles(g, k)], ident[:])
                mm.then_inc(m["group_turned"], 1)

            def key_pairs(k):
                for c in range(TT):
                    if k:
                        pe.wait_ge(m["pair2_masked"], due(m["pair2_masked"]))
                    for h in (2 * k, 2 * k + 1):
                        mm = pe.matmul(bank(c, 3)[:, (h % 2) * SEQ:(h % 2 + 1) * SEQ], KTT[:, h, c * P:(c + 1) * P],
                                       ART[:, k, c, :, :], start=True, stop=True, skip_group_check=True)
                    mm.then_inc(m["pair2_ready"], 1)

            def level(n, c):
                if n == 0:
                    pe.wait_ge(m["pair_masked"], due(m["pair_masked"]))
                else:
                    pe.wait_ge(m["level_copied"], due(m["level_copied"]))
                pe.matmul(bank(c, 0), identb[:, 0:P], identb[:, :], start=True, stop=False, skip_group_check=True)
                for h in range(GROUP):
                    mm = pe.matmul(bank(c, 0)[:, h * P:(h + 1) * P], NM[:, c, h, :], INVT[:, c, h, :],
                                   start=False, stop=(h == GROUP - 1), skip_group_check=True)
                mm.then_inc(m["level_ready"], 1)

            def level2(n, c):
                pe.wait_ge(m["level_masked"], due(m["level_masked"]))
                for h in range(GROUP):
                    mm = pe.matmul(bank(c, 1)[:, h * P:(h + 1) * P], INV[:, c, h, :], QM[:, c, h, :], start=True, stop=True,
                                   skip_group_check=True)
                    if n < len(LEVELS) - 1:
                        mm = pe.matmul(bank(c, 2)[:, h * P:(h + 1) * P], QM[:, c, h, :], INV[:, c, h, :], start=True, stop=True,
                                       skip_group_check=True)
                mm.then_inc(m["level2_ready"], 1)

            def by_values(g, c, b, weights, stop=False):
                for h in range(GROUP):
                    mm = pe.matmul(bank(c, b)[:, own(h)], weights[:, c, h, :], V[:, c, head(g, h)], start=(h == 0),
                                   stop=(stop and h == GROUP - 1), skip_group_check=True)
                return mm

            def by_state(b, e, stop=False):
                for k in range(2):
                    mm = pe.matmul(bank(1, b)[:, k * P:(k + 1) * P], ART[:, k, 1, e, :], ST[:, k], start=False, stop=(stop and k == 1),
                                   skip_group_check=True)
                return mm

            def solve(c):
                pe.wait_ge(m["rhs_copied"], due(m["rhs_copied"]))
                for h in range(GROUP):
                    mm = pe.matmul(bank(c, 1)[:, own(h)], INVT[:, c, h, :], RHS[:, own(h)], start=True, stop=True, skip_group_check=True)
                mm.then_inc(m["u_ready"], 1)

            def by_solution(c):
                for h in range(GROUP):
                    mm = pe.matmul(bank(c, 2)[:, own(h)], RB[:, c, h, :], U[:, c, own(h)], start=False, stop=(h == GROUP - 1),
                                   skip_group_check=True)
                mm.then_inc(m["y_ready"], 1)

            for n in range(4):
                pe.wait_ge(m["scaled_ready"], due(m["scaled_ready"]))
                turn_group(n, 0)
            for g in range(groups):
                more = g + 1 < groups
                pe.wait_ge(m["group_copied"], due(m["group_copied"], 4))
                for c in range(TT):
                    if g and c:
                        pe.wait_ge(m["y_copied"], due(m["y_copied"]))
                    at = slice(c * P, (c + 1) * P)
                    for k in range(2):
                        mm = pe.matmul(bank(c, 0)[:, k * SEQ:(k + 1) * SEQ], ART[:, k, c, 0, :], BTT[:, 2 * k:2 * k + 2, at],
                                       start=True, stop=True, skip_group_check=True)
                    for h in range(GROUP):
                        mm = pe.matmul(bank(c, 1 + h // 2)[:, (h % 2) * SEQ:(h % 2 + 1) * SEQ], BTT[:, h, at],
                                       ART[:, h // 2, c, :, :], start=True, stop=True, skip_group_check=True)
                    mm.then_inc(m["pair_ready"], 1)
                key_pairs(0)
                for n in range(len(LEVELS)):
                    for c in range(TT):
                        level(n, c)
                    for c in range(TT):
                        level2(n, c)
                    if n == 0:
                        key_pairs(1)
                pe.wait_ge(m["pair2_masked"], due(m["pair2_masked"], TT))
                by_values(g, 0, 0, AK, stop=True).then_inc(m["rhs_ready"], 1)
                for k in range(2):
                    pe.matmul(bank(0, 3)[:, k * P:(k + 1) * P], K[:, 0, tiles(g, k)], V[:, 0, tiles(g, k)], start=(k == 0), stop=False,
                              skip_group_check=True)
                by_values(g, 0, 2, RK)
                by_values(g, 1, 0, AK)
                by_values(g, 1, 2, RK)
                pe.wait_ge(m["level_copied"], due(m["level_copied"], TT))
                solve(0)
                if more:
                    turn_group(0, g + 1)
                pe.wait_ge(m["u_copied"], due(m["u_copied"]))
                for k in range(2):
                    mm = pe.matmul(bank(0, 3)[:, k * P:(k + 1) * P], IC[:, 0, tiles(g, k)], U[:, 0, k * P:(k + 1) * P], start=False, stop=(k == 1),
                                   skip_group_check=True)
                mm.then_inc(m["state_ready"], 1)
                by_solution(0)
                if more:
                    turn_group(1, g + 1)
                pe.wait_ge(m["state_copied"], due(m["state_copied"], 4))
                by_state(0, 0, stop=True).then_inc(m["rhs_ready"], 1)
                by_state(2, 1).then_inc(m["art_used"], 1)
                if more:
                    turn_group(2, g + 1)
                solve(1)
                if more:
                    pe.wait_ge(m["y_copied"], due(m["y_copied"]))
                    turn_group(3, g + 1)
                pe.wait_ge(m["u_copied"], due(m["u_copied"]))
                by_solution(1)
            pe.wait_ge(m["y_copied"], due(m["y_copied"], TT))
            for t in range(TT):
                for c in range(2):
                    cs = slice(c * 512, (c + 1) * 512)
                    pe.matmul(acc[:, 2 * t + c, :], SG[:, t * P:(t + 1) * P], G2[:, cs], start=True, stop=False)
                    mm = pe.matmul(acc[:, 2 * t + c, :], SGb[:, t * P:(t + 1) * P], G2b[:, cs], start=False, stop=True)
            mm.then_inc(m["gate_ready"], 1)
            for t in range(TT):
                turn(tok, t)
            project(q + IN_Q, KT, ah, al, operand_steps())

        def ffn(q, normed):
            def turn_hidden(odd, last=False):
                pe.wait_ge(m["hidden_ready"], due(m["hidden_ready"], TT))
                pe.wait_ge(m["hidden_lo"], due(m["hidden_lo"], 0) + 1 if last else due(m["hidden_lo"]))
                for kk in range(2):
                    for t in range(TT):
                        mm = pe.transpose(aux[:, odd, kk * SEQ + t * P:kk * SEQ + (t + 1) * P],
                                          HM[:, odd, t, kk * P:(kk + 1) * P], ident[:])
                mm.then_inc(m["hidden_turned"], 1)

            first_block(q, tok if normed else X, 1 if normed else 3)
            with due.loop((FB - 1) // 2, {m["hidden_ready"]: 2 * TT, m["hidden_lo"]: 2}) as i:
                for b in range(2):
                    block_tokens(q + 4 + 4 * b, 1 - b, at=(i, 8))
                    turn_hidden(b)
            project(q + FB * 4, FK, HH, HL, {(0, 0): lambda: turn_hidden(0, last=True),
                                             (FK - 4, 0): lambda: pe.wait_ge(m["hidden_last"], due(m["hidden_last"]))}, first=1)

        def attention(q, near):
            def turn_qk(src, banks, flipped=False):
                for b in banks:
                    for kk in range(2):
                        k = 2 * b + kk
                        for t in range(TT):
                            mm = turn_tile(aux[:, b, kk * SEQ + t * P:kk * SEQ + (t + 1) * P], src[:, t, k * P:(k + 1) * P], flipped)
                    mm.then_inc(m["qk_turned"], 1)

            for j in range(6):
                if j >= 2:
                    freed = m["qk_square"] if near else m["in_done"]
                    pe.wait_ge(freed, due(freed))
                if j:
                    block_tokens(q + 4 * j, j % 2)
                else:
                    first_block(q, tok if near else X, 1 if near else 3)
                if j == 4:
                    pe.wait_ge(m["qk_done"], due(m["qk_done"], 2))
                    if near:
                        pe.wait_ge(m["near_in"], due(m["near_in"], 16 * 3))
                    turn_qk(QTOK, range(4), near)
            pe.wait_ge(m["qk_done"], due(m["qk_done"], 2))
            pe.wait_ge(m["qk_copied"], due(m["qk_copied"], 4))
            turn_qk(KTOK, (0, 1))
            if near:
                due(m["in_done"], 4)
            pe.wait_ge(m["in_done"], due(m["in_done"]))
            pe.wait_ge(m["qk_copied"], due(m["qk_copied"]))
            if not near:
                pe.wait_ge(m["causal_set"], due(m["causal_set"]))

            def scores(p):
                for t in range(TT):
                    keys = SEQ if near else (t + 1) * P
                    for h in range(2):
                        of = slice(h * HD, (h + 1) * HD)
                        mm = pe.matmul(acc[:, 2 * (p % 2) + h, t * SEQ:t * SEQ + keys], QT[of, p, t * P:(t + 1) * P], KTT2[of, p, 0:keys],
                                       start=True, stop=near, skip_group_check=True)
                        if not near:
                            mm = pe.matmul(acc[:, 2 * (p % 2) + h, t * SEQ + t * P:t * SEQ + (t + 1) * P], identb[:, 0:P], CAUSAL[:],
                                           start=False, stop=True, skip_group_check=True)
                mm.then_inc(m["scores_ready"], 1)

            def turn_probs(p):
                pe.wait_ge(m["probs_ready"], due(m["probs_ready"], TT))
                if p:
                    pe.wait_ge(m["probs_copied_a"], due(m["probs_copied_a"]))
                    pe.wait_ge(m["probs_copied_v"], due(m["probs_copied_v"]))
                for h in range(2):
                    for t in range(TT):
                        for k in range(TT if near else t + 1):
                            mm = pe.transpose(aux[:, h, k * SEQ + t * P:k * SEQ + (t + 1) * P], PR[:, p % 2, t, h, k * P:(k + 1) * P], ident[:])
                    mm.then_inc(m["probs_turned"], 1)

            def values(p):
                if p >= 2:
                    pe.wait_ge(m["o_done"], due(m["o_done"]))
                for t in range(TT):
                    for h in range(2):
                        tiles = TT if near else t + 1
                        for k in range(tiles):
                            mm = pe.matmul(aux[:, 2 + p % 2, (t * 2 + h) * HD:(t * 2 + h + 1) * HD], PT[:, p % 2, h, k, t * P:(t + 1) * P],
                                           VTOK[:, k, (2 * p + h) * HD:(2 * p + h + 1) * HD], start=(k == 0), stop=(k == tiles - 1),
                                           skip_group_check=True)
                mm.then_inc(m["o_ready"], 1)

            scores(0)
            turn_qk(KTOK, (2, 3))
            for p in range(PAIRS):
                if p == 0:
                    pe.wait_ge(m["in_done"], due(m["in_done"]))
                if p + 1 < PAIRS:
                    scores(p + 1)
                if p < 2:
                    pe.wait_ge(m["qk_copied"], due(m["qk_copied"], 1 + p))
                turn_probs(p)
                if p:
                    values(p - 1)
            pe.wait_ge(m["probs_copied_a"], due(m["probs_copied_a"]))
            pe.wait_ge(m["probs_copied_v"], due(m["probs_copied_v"]))
            values(PAIRS - 1)
            for t in range(TT):
                turn(tok, t, ready=0 if t else TT, flipped=near)
            project(q + IN_Q, KT, ah, al, operand_steps())

        def conv(q):
            for t in range(TT):
                turn(tok, t)
            for j in range(6):
                if j >= 2:
                    freed = m["c_done"] if j < 4 else m["z_done"]
                    pe.wait_ge(freed, due(freed))
                block_channels(q + 4 * j, j % 2, operand_waits=(j == 0))
            ready = lambda: pe.wait_ge(m["conv_lo_done"], due(m["conv_lo_done"]))
            project(q + IN_Q, KT, OH, OL, {(0, 0): ready, (0, 1): ready})

        def hyena(q):
            def mlp(k):
                if k:
                    pe.wait_ge(m["mlp_done"], due(m["mlp_done"]))
                weights, x = (FW[:, 1, :], H1) if k else (FW[0:EMB, 0, :], EMBT)
                pe.matmul(aux[0:FHID, 0, 0:SEQ], weights, x[:], start=True, stop=True).then_inc(m["mlp_ready"], 1)

            def taps(r, pairs):
                t, d = r // 2, r % 2
                if r >= pairs:
                    pe.wait_ge(m["filt_done"], due(m["filt_done"]))
                for c in range(2):
                    mm = pe.matmul(aux[:, 2 * (r % pairs) + c, :], H1[:, t * P:(t + 1) * P], FW3[:, d * D + c * 512:d * D + (c + 1) * 512],
                                   start=True, stop=True)
                mm.then_inc(m["filt_ready"], 1)

            def freq(k, pairs):
                part, mats = SPECTRA[k]
                if k == 0:
                    pe.wait_ge(m["filt_done"], due(m["filt_done"], pairs))
                elif pairs == 1 and k == 3:
                    pe.wait_ge(m["norm_copied"], due(m["norm_copied"]))
                elif k >= pairs:
                    pe.wait_ge(m["freq_done"], due(m["freq_done"]))
                if k in (0, 3):
                    pe.wait_ge(m["eo_ready"], due(m["eo_ready"]))
                for c in range(2):
                    for t in range(TT):
                        mm = pe.matmul(aux[:, 2 * freq_pair(k, pairs) + c, :], DFT[:, t, mats, :], EO[:, 2 * part + t, c * 512:(c + 1) * 512],
                                       start=(t == 0), stop=(t == TT - 1))
                mm.then_inc(m["freq_ready"], 1)

            def norm(pairs):
                pe.wait_ge(m["freq_done"], due(m["freq_done"]))
                pe.wait_ge(m["filt_summed"], due(m["filt_summed"], 3))
                for c in range(2):
                    mm = pe.matmul(aux[:, c, :], ONES[:], TAPS[pairs - 1][0][:, c * 512:(c + 1) * 512], start=True, stop=True)
                mm.then_inc(m["norm_ready"], 1)

            def turn_cv(j):
                pe.wait_ge(m["cv_ready"], due(m["cv_ready"]))
                if j:
                    pe.wait_ge(m["cv_copied"], due(m["cv_copied"]))
                for t in range(TT):
                    for c in range(4):
                        mm = pe.transpose(aux[:, 2 + t, c * P:(c + 1) * P], HCV[:, j % 2, c, t * P:(t + 1) * P], ident[:])
                mm.then_inc(m["cv_turned"], 1)

            def dft(r):
                f, c = r // 2, r % 2
                for part, mat in enumerate((f, 2 + f)):
                    for t in range(TT):
                        mm = pe.matmul(acc[:, 2 * (r % 2) + part, :], DFT[:, t, mat, :], HV[:, t, c * 512:(c + 1) * 512],
                                       start=(t == 0), stop=(t == TT - 1))
                mm.then_inc(m["dft_ready"], 1)

            for t in range(TT):
                turn(tok, t)
            pe.wait_ge(m["hyena_in"], due(m["hyena_in"], 16 * 10))
            pe.wait_ge(m["ones_set"], due(m["ones_set"]))

            def first_taps():
                pe.wait_ge(m["mlp_done"], due(m["mlp_done"]))
                taps(0, 1)

            pieces = [lambda: mlp(0), lambda: mlp(1), first_taps] + [lambda r=r: taps(r, 1) for r in (1, 2, 3)]
            pieces += [lambda: None] + [lambda k=k: freq(k, 1) for k in range(5)]
            pieces.insert(10, lambda: norm(1))
            for j in range(6):
                turned = {2: lambda: turn_cv(j - 1)} if j else {}
                block_channels(q + 4 * j, j % 2, operand_waits=(j == 0), after={1: pieces[2 * j], 3: pieces[2 * j + 1], **turned})
            pieces[12]()
            dft(0)
            turn_cv(5)
            for n in range(ORDER):
                for r in range(1 - n, 4):
                    if r >= 2:
                        pe.wait_ge(m["dft_done"], due(m["dft_done"]))
                    dft(r)
                if n == 0:
                    pe.wait_ge(m["freq_done"], due(m["freq_done"]))
                    pe.wait_ge(m["cv_copied"], due(m["cv_copied"]))
                    pe.wait_ge(m["taps2_in"], due(m["taps2_in"], 16))
                    for r in range(2):
                        taps(r, 2)
                pe.wait_ge(m["dft_done"], due(m["dft_done"]))
                for t in range(TT):
                    for c in range(2):
                        if (t, c) == (0, 1):
                            pe.wait_ge(m["dft_done"], due(m["dft_done"]))
                        for f in range(4):
                            mm = pe.matmul(acc[:, 2 * t + c, :], IDFT[:, f, t * P:(t + 1) * P], FR[:, f, c * 512:(c + 1) * 512],
                                           start=(f == 0), stop=(f == 3))
                    mm.then_inc(m["idft_ready"], 1)
                    if n == 0 and t == 0:
                        for r in range(2, 4):
                            taps(r, 2)
                if n == 0:
                    for k in range(5):
                        if k == 4:
                            norm(2)
                        freq(k, 2)
                    pe.wait_ge(m["idft_done"], due(m["idft_done"]))
            pe.wait_ge(m["norm_copied"], due(m["norm_copied"]))
            pe.wait_ge(m["freq_done"], due(m["freq_done"]))
            for t in range(TT):
                turn(tok, t)
            project(q + IN_Q, KT, ah, al, operand_steps())

        for n, kind in enumerate(layers):
            {"rwkv": rwkv, "ffn": lambda q: ffn(q, n > LAYER_NORMS), "moba": lambda q: attention(q, False), "near": lambda q: attention(q, True),
             "conv": conv, "hyena": hyena}[kind](start[n])

    @block.scalar
    def _(act):
        due = Tally(act)

        def split(q, at=None):
            s = q % SLOTS
            act.wait_ge(w_full[s], 16 * nth(q) if at is None else at[0] * (16 * at[1] // SLOTS) + 16 * nth(q))
            if q >= SLOTS:
                act.wait_ge(w_used[s], nth(q - SLOTS, at))
            act.activation(whi[:, s, :], raw[:, s, :], ACT.Copy).then_inc(w_hi[s], 1)

        def ahead(q, n, at=None):
            for k in range(n):
                if q + k + SLOTS < quarters:
                    split(q + k + SLOTS, at)

        def operand(t):
            for h in range(2):
                act.wait_ge(m["turned"], due(m["turned"]))
                act.activation(ah[:, 4 * h:4 * h + 4, t * P:(t + 1) * P], aux[:, 2 * t + h, :].rearrange("p (k n) -> p k n", n=P), ACT.Copy)\
                   .then_inc(m["hi_ready"], 1)

        def both_operands():
            for t in range(TT):
                operand(t)

        def residual(n, q):
            more = n < len(layers) - 1
            rms = more and n >= LAYER_NORMS - 1

            def square(t):
                if n >= LAYER_NORMS:
                    act.wait_ge(m["residual_done"], TT * n + t + 1)
                else:
                    act.wait_ge(m["ln_done"], due(m["ln_done"]))
                act.activation(tok[:, t, :], X[:, t, :], ACT.Square, accum_out=stat[:, 56 + t:57 + t]).then_inc(m["square_ready"], 1)

            if rms and n < LAYER_NORMS:
                square(0)
                ahead(q - 4, 4)
                square(1)
                both_operands()
                return
            if rms:
                square(0)
            ahead(q - 4, 3)
            if more:
                operand(0)
            if n < LAYER_NORMS:
                ahead(q - 1, 1)
            if rms:
                square(1)
            if n >= LAYER_NORMS:
                ahead(q - 1, 1)
            if more:
                operand(1)

        def rwkv(q):
            def copy_out(dst, c, q):
                act.wait_ge(w_used[q % SLOTS], nth(q))
                for t in range(TT):
                    last = act.activation(dst[:, t, c * 512:(c + 1) * 512], acc[:, 2 * c + t, :], ACT.Copy)
                last.then_inc(m["rkv_done"], 1)

            def mix_hi(src, h):
                act.wait_ge(m["mix_f_ready"], due(m["mix_f_ready"]))
                ks = slice(4 * h, 4 * h + 4)
                act.activation(ah[:, ks, :], MIX[src][:, ks, :], ACT.Copy).then_inc(m["hi_ready"], 1)

            def project_out(dst, q, mixes_between):
                for c in range(2):
                    ahead(q + 4 * c, 4)
                    if c and mixes_between is not None:
                        act.wait_ge(w_used[(q + 7) % SLOTS], nth(q + 7))
                        due(m["mix_f_ready"], 2 * mixes_between)
                        for h in range(2):
                            mix_hi(1, h)
                    copy_out(dst, c, q + 4 * c + 3)

            for h in range(2):
                split(q + h)
                mix_hi(0, h)
            split(q + 2)
            split(q + 3)
            act.wait_ge(m["halves_set"], due(m["halves_set"], 3))
            project_out(R, q, 0)
            act.wait_ge(m["lora1_ready"], due(m["lora1_ready"]))
            act.activation(LW[0:LORA, :], aux[0:LORA, 0, 0:SEQ], ACT.Tanh).then_inc(m["lora_mid"], 1)
            project_out(K, q + 8, 1)
            act.wait_ge(m["lora1_ready"], due(m["lora1_ready"]))
            act.activation(LA[0:LORA, :], aux[0:LORA, 1, 0:SEQ], ACT.Copy).then_inc(m["lora_mid"], 1)
            project_out(V, q + 16, None)
            act.wait_ge(m["lora1_ready"], due(m["lora1_ready"]))
            act.activation(SG[:], aux[:, 2, 0:SEQ], ACT.Sigmoid)
            act.activation(SGb[:], aux[0:GLORA - P, 3, 0:SEQ], ACT.Sigmoid).then_inc(m["lora_mid"], 1)
            for dst, src in ((DEC, aux), (IC, acc)):
                act.wait_ge(m["lora2_ready"], due(m["lora2_ready"]))
                for t in range(TT):
                    for c in range(2):
                        last = act.activation(dst[:, t, c * 512:(c + 1) * 512], src[:, 2 * t + c, :], ACT.Sigmoid)
                last.then_inc(m["lora_out"], 1)
            for t in range(TT):
                act.wait_ge(m["cum_ready"], due(m["cum_ready"]))
                for dst, b, sign in zip(DECAYS[t], (0, 0, 2), (1.0, -1.0, 1.0)):
                    if t == 0 and b:
                        act.wait_ge(m["k_done"], due(m["k_done"]))
                    act.activation(dst.rearrange("p (c n) -> p c n", c=2), (aux, acc)[t][:, b:b + 2, :], ACT.Exp, scale=sign)\
                       .then_inc(m["exp_ready"], 1)
            act.wait_ge(m["span_ready"], due(m["span_ready"]))
            act.activation(DCOL[:], aux[:, 0, 0:KT], ACT.Exp).then_inc(m["exp_ready"], 1)
            bank = lambda c, b: (acc, aux)[c][:, b, :]
            def turned_group(n):
                act.wait_ge(m["group_turned"], due(m["group_turned"]))
                act.activation(ART[:, :, :, 1 - n, :], acc[:, n, :].rearrange("p (k t n) -> p k t n", k=2, t=TT), ACT.Copy)\
                   .then_inc(m["group_copied"], 1)

            act.wait_ge(m["identb_set"], due(m["identb_set"], GROUP))
            turned_group(0)
            turned_group(1)
            for g in range(HEADS // GROUP):
                due(m["group_turned"], 2)
                for c in range(TT):
                    for dst in (INV, INVT):
                        last = act.activation(dst[:, c], identb[:].rearrange("p (h n) -> p h n", h=GROUP), ACT.Copy)
                    last.then_inc(m["inverse_set"], 1)
                for n in range(len(LEVELS)):
                    for c in range(TT):
                        act.wait_ge(m["level2_ready"], due(m["level2_ready"]))
                        last = act.activation(INVT[:, c], bank(c, 1), ACT.Copy)
                        if n < len(LEVELS) - 1:
                            last = act.activation(INV[:, c], bank(c, 2), ACT.Copy)
                        last.then_inc(m["level_copied"], 1)
                for c in range(TT):
                    act.wait_ge(m["rhs_ready"], due(m["rhs_ready"]))
                    act.activation(RHS[:], bank(c, 0)[:, 0:GROUP * HD], ACT.Copy).then_inc(m["rhs_copied"], 1)
                    if c and g + 1 < HEADS // GROUP:
                        act.wait_ge(m["art_used"], due(m["art_used"]))
                        turned_group(0)
                    act.wait_ge(m["u_ready"], due(m["u_ready"]))
                    act.activation(U[:, c, :], bank(c, 1)[:, 0:GROUP * HD], ACT.Copy).then_inc(m["u_copied"], 1)
                    if c and g + 1 < HEADS // GROUP:
                        turned_group(1)
                    act.wait_ge(m["y_ready"], due(m["y_ready"]))
                    act.activation(tok[:, c, g * GROUP * HD:(g + 1) * GROUP * HD], bank(c, 2)[:, 0:GROUP * HD], ACT.Copy)\
                       .then_inc(m["y_copied"], 1)
            both_operands()
            ahead(q + IN_Q, OUT_Q - 4)

        def ffn(q):
            def silu(q, odd, pair, at=None):
                act.wait_ge(w_used[(q + 3) % SLOTS], nth(q + 3, at))
                for t in range(TT):
                    last = act.activation(SILU[:, odd, t, :], acc[:, 2 * pair + t, 0:256], ACT.Silu)
                last.then_inc(m["silu_ready"], 1)

            def hidden_hi(dst, odd):
                act.wait_ge(m["hidden_turned"], due(m["hidden_turned"]))
                act.activation(dst, aux[:, odd, :].rearrange("p (k n) -> p k n", k=2), ACT.Copy).then_inc(m["hidden_hi"], 1)

            ahead(q, 4)
            silu(q, 0, 0)
            with due.loop((FB - 1) // 2, {m["hidden_turned"]: 2}) as i:
                for b in range(2):
                    ahead(q + 4 + 4 * b, 4, (i, 8))
                    silu(q + 4 + 4 * b, 1 - b, 1 - b, (i, 8))
                    hidden_hi(HH[:, bass.ds(i * 4 + 2 * b, 2), :], b)
            hidden_hi(HH[:, FK - 2:FK, :], 0)
            ahead(q + FB * 4, FK - 4)

        def attention(q, near):
            for j in range(6):
                ahead(q + 4 * j, 4)
                if near and j < 4:
                    act.wait_ge(w_used[(q + 4 * j + 3) % SLOTS], nth(q + 4 * j + 3))
                    dst = (QTOK, KTOK)[j // 2]
                    act.activation(dst[:, :, (j % 2) * 512:(j % 2 + 1) * 512], acc[:, 2 * (j % 2):2 * (j % 2) + 2, :], ACT.Copy)
                    if j:
                        act.wait_ge(m["qk_summed"], due(m["qk_summed"]))
                    act.activation(ROT[:], acc[:, 2 * (j % 2):2 * (j % 2) + 2, :], ACT.Square).then_inc(m["qk_square"], 1)
                if j == 4:
                    for b in range(4):
                        act.wait_ge(m["qk_turned"], due(m["qk_turned"]))
                        act.activation(QT[:, 2 * b:2 * b + 2, :], aux[:, b, :], ACT.Copy).then_inc(m["qk_copied"], 1)

            def copy_k(banks):
                for b in banks:
                    act.wait_ge(m["qk_turned"], due(m["qk_turned"]))
                    act.activation(KTT2[:, 2 * b:2 * b + 2, :], aux[:, b, :], ACT.Copy).then_inc(m["qk_copied"], 1)

            copy_k((0, 1))

            def copy_probs(p):
                act.wait_ge(m["probs_turned"], due(m["probs_turned"]))
                if near:
                    act.activation(PT[:, p % 2, 0], aux[:, 0, :], ACT.Copy).then_inc(m["probs_copied_a"], 1)
                else:
                    act.activation(PT[:, p % 2, 0, 0, :], aux[:, 0, 0:SEQ], ACT.Copy)
                    act.activation(PT[:, p % 2, 0, 1, P:SEQ], aux[:, 0, SEQ + P:2 * SEQ], ACT.Copy).then_inc(m["probs_copied_a"], 1)
                due(m["probs_turned"])

            for p in range(PAIRS):
                act.wait_ge(m["max_ready"], due(m["max_ready"]))
                for t in range(TT):
                    keys = SEQ if near else (t + 1) * P
                    for h in range(2):
                        src = SC[:, p % 2, t, h, :] if near else acc[:, 2 * (p % 2) + h, t * SEQ:t * SEQ + keys]
                        last = act.activation(PR[:, p % 2, t, h, 0:keys], src, ACT.Exp, bias=NMAX[:, t, 2 * p + h:2 * p + h + 1],
                                              accum_out=SUMS[:, t, 2 * p + h:2 * p + h + 1])
                    last.then_inc(m["probs_ready"], 1)
                if p:
                    copy_probs(p - 1)
                else:
                    copy_k((2, 3))
            copy_probs(PAIRS - 1)
            both_operands()
            ahead(q + IN_Q, OUT_Q - 4)

        def conv(q):
            for j in range(6):
                ahead(q + 4 * j, 4)
                if j < 2:
                    act.wait_ge(w_used[(q + 4 * j + 3) % SLOTS], nth(q + 4 * j + 3))
                    act.activation(CT[:, 4 * j:4 * j + 4, :].rearrange("p (b k) n -> p b (k n)", b=2), acc[:, 2 * j:2 * j + 2, :], ACT.Copy)\
                       .then_inc(m["c_done"], 1)
                if j >= 4:
                    act.wait_ge(m["y_done"], due(m["y_done"]))
                    act.activation(OH[:, 4 * (j - 4):4 * (j - 3), :], YT[:, 4 * (j - 4):4 * (j - 3), :], ACT.Copy).then_inc(m["conv_hi_done"], 1)
            ahead(q + IN_Q, OUT_Q - 4)

        def hyena(q):
            def sine():
                act.wait_ge(m["arg_ready"], due(m["arg_ready"]))
                act.activation(H1[:], ARG[:, 0, :], ACT.Sin).then_inc(m["mlp_done"], 1)

            def absolute(filt, h):
                if h == 0:
                    act.wait_ge(m["tap0_joined"], due(m["tap0_joined"], 2))
                for x in TAPS[filt][2 * h:2 * h + 2]:
                    act.activation(x, x, ACT.Abs).then_inc(m["filt_abs"], 1)

            two = lambda x: x.rearrange("p (c n) -> p c n", c=2)

            def freq(k, pairs):
                act.wait_ge(m["freq_ready"], due(m["freq_ready"]))
                b = 2 * freq_pair(k, pairs)
                act.activation(two(HF[:, k, :]), aux[:, b:b + 2, :], ACT.Copy).then_inc(m["freq_done"], 1)

            def norm():
                act.wait_ge(m["norm_ready"], due(m["norm_ready"]))
                act.activation(two(RN[:]), aux[:, 0:2, :], ACT.Copy).then_inc(m["norm_copied"], 1)

            def copy_cv(j):
                act.wait_ge(m["cv_turned"], due(m["cv_turned"]))
                dst, c = (HV, HX1, HX2)[j // 2], j % 2
                act.activation(dst[:, :, c * 512:(c + 1) * 512], aux[:, 2:4, :], ACT.Copy).then_inc(m["cv_copied"], 1)

            nothing = lambda: None

            def freq_and_sizes(k, pairs):
                freq(k, pairs)
                if k < 2:
                    absolute(pairs - 1, k)

            pieces = [sine, sine] + [nothing] * 5 + [lambda k=k: freq_and_sizes(k, 1) for k in range(5)]
            pieces.insert(10, norm)
            for j in range(6):
                ahead(q + 4 * j, 2)
                pieces[2 * j]()
                ahead(q + 4 * j + 2, 1)
                if j:
                    copy_cv(j - 1)
                ahead(q + 4 * j + 3, 1)
                pieces[2 * j + 1]()
            pieces[12]()
            copy_cv(5)
            for k in range(5):
                if k == 4:
                    act.wait_ge(m["idft_done"], due(m["idft_done"]))
                    norm()
                freq_and_sizes(k, 2)
            both_operands()
            ahead(q + IN_Q, OUT_Q - 4)

        for n, kind in enumerate(layers):
            {"rwkv": rwkv, "ffn": ffn, "moba": lambda q: attention(q, False), "near": lambda q: attention(q, True),
             "conv": conv, "hyena": hyena}[kind](start[n])
            residual(n, start[n] + (FFN_Q if kind == "ffn" else IN_Q + OUT_Q))

    @block.vector
    def _(dve):
        due = Tally(dve)

        def split(q, at=None):
            s = q % SLOTS
            dve.wait_ge(w_hi[s], nth(q, at))
            dve.tensor_tensor(wlo[:, s, :], raw[:, s, :], whi[:, s, :].bitcast(F32), ALU.subtract).then_inc(w_lo[s], 1)

        def ahead(q, n, at=None):
            for k in range(n):
                if q + k + SLOTS < quarters:
                    split(q + k + SLOTS, at)

        def used(q, at=None):
            dve.wait_ge(w_used[q % SLOTS], nth(q, at))

        def step(instruction):
            instruction.then_inc(m["dve_step"], 1)
            dve.wait_ge(m["dve_step"], due(m["dve_step"]))

        def operand(t):
            for h in range(2):
                dve.wait_ge(m["hi_ready"], due(m["hi_ready"]))
                own = (slice(None), slice(4 * h, 4 * h + 4), slice(t * P, (t + 1) * P))
                dve.tensor_tensor(al[own], aux[:, 2 * t + h, :].rearrange("p (k n) -> p k n", n=P), ah[own].bitcast(F32), ALU.subtract)\
                   .then_inc(m["operand_ready"], 1)

        def both_operands():
            for t in range(TT):
                operand(t)

        def wide(v, shape, axis):
            return v.unsqueeze(axis).to_broadcast(shape)

        def by_head(x):
            return x.rearrange("p t (h d) -> p (t h) d", d=HD)

        def residual(n, q):
            more = n < len(layers) - 1
            layer_norm = n < LAYER_NORMS
            rms = more and n >= LAYER_NORMS - 1
            gain = lng if n >= LAYER_NORMS else FIRSTG
            channels = more and layers[n + 1] in ("conv", "hyena")

            def add(t):
                if t == 0:
                    dve.wait_ge(m["half_done"], due(m["half_done"]))
                else:
                    used(q - 1)
                cols = X[:, t, :].rearrange("p (c n) -> p c n", c=2)
                if layer_norm:
                    last = dve.scalar_tensor_tensor(out=cols, in0=cols, scalar=ALPHA, in1=acc[:, 2 * t:2 * t + 2, :], op0=ALU.mult, op1=ALU.add)
                else:
                    last = dve.tensor_tensor(cols, cols, acc[:, 2 * t:2 * t + 2, :], ALU.add)
                last.then_inc(m["residual_done"] if more or layer_norm else m["y_final"], 1)

            def moments(t):
                dve.wait_ge(m["residual_done"], TT * n + t + 1)
                for c in range(2):
                    last = dve.bn_stats(stat[:, 32 + 6 * c:38 + 6 * c], X[:, t, c * 512:(c + 1) * 512])
                step(last)
                dve.bn_aggr(mom[:, t, :], stat[:, 32:44]).then_inc(m["ms_ready"], 1)
                dve.wait_ge(m["ms_ready"], due(m["ms_ready"]))

            def centred(t):
                step(dve.scalar_tensor_tensor(out=X[:, t, :], in0=X[:, t, :], scalar=mom[:, t, 0:1], in1=lng[:], op0=ALU.subtract, op1=ALU.mult))

            def normed(t):
                dve.wait_ge(m["rstd_ready"], due(m["rstd_ready"]))
                dve.scalar_tensor_tensor(out=X[:, t, :], in0=X[:, t, :], scalar=rstd[:, t:t + 1], in1=lnb[:], op0=ALU.mult, op1=ALU.add)\
                   .then_inc(m["ln_done"] if rms else m["token_ready"] if more else m["y_final"], 1)

            def rms_normed(t):
                dve.wait_ge(m["rstd_ready"], due(m["rstd_ready"]))
                dve.scalar_tensor_tensor(out=tok[:, t, :], in0=X[:, t, :], scalar=rstd[:, t:t + 1], in1=gain[:], op0=ALU.mult, op1=ALU.mult)\
                   .then_inc(m["token_ready"], 1)

            if n == 0:
                dve.wait_ge(m["res_in"], due(m["res_in"], 16 * TT))
            if layer_norm:
                dve.wait_ge(m["ln_in"], due(m["ln_in"], 32))
            if rms:
                dve.wait_ge(m["gain_in"], due(m["gain_in"], 16))
            add(0)
            if layer_norm and rms:
                moments(0)
                centred(0)
                normed(0)
                add(1)
                moments(1)
                centred(1)
                normed(1)
                rms_normed(0)
                ahead(q - 4, 1)
                rms_normed(1)
                operand(0)
                ahead(q - 3, 1)
                operand(1)
                ahead(q - 2, 2)
            elif layer_norm:
                moments(0)
                centred(0)
                normed(0)
                ahead(q - 4, 2)
                add(1)
                operand(0)
                moments(1)
                ahead(q - 2, 1)
                centred(1)
                ahead(q - 1, 1)
                normed(1)
                operand(1)
            else:
                if rms:
                    rms_normed(0)
                ahead(q - 4, 1)
                add(1)
                if more:
                    operand(0)
                ahead(q - 3, 1)
                if rms:
                    rms_normed(1)
                ahead(q - 2, 1)
                if channels:
                    operand(1)
                    ahead(q - 1, 1)
                else:
                    ahead(q - 1, 1)
                    if more:
                        operand(1)

        def rwkv(q):
            def differences(h):
                ks = slice(4 * h, 4 * h + 4)
                dve.tensor_tensor(XX[:, ks, 1:SEQ], XT[:, ks, 0:SEQ - 1], XT[:, ks, 1:SEQ], ALU.subtract)
                step(dve.tensor_scalar(XX[:, ks, 0:1], XT[:, ks, 0:1], -1.0, None, ALU.mult))

            def mix(n, dst, h):
                for k in range(4 * h, 4 * h + 4):
                    last = dve.scalar_tensor_tensor(out=MIX[dst][:, k, :], in0=XX[:, k, :], scalar=MU[:, n, k:k + 1], in1=XT[:, k, :],
                                                    op0=ALU.mult, op1=ALU.add)
                last.then_inc(m["mix_f_ready"], 1)

            def mix_all(n, dst):
                for h in range(2):
                    mix(n, dst, h)

            def half_lo(src, h):
                dve.wait_ge(m["hi_ready"], due(m["hi_ready"]))
                ks = slice(4 * h, 4 * h + 4)
                dve.tensor_tensor(al[:, ks, :], MIX[src][:, ks, :], ah[:, ks, :].bitcast(F32), ALU.subtract).then_inc(m["mix_ready"], 1)

            def mix_lo(src):
                for h in range(2):
                    half_lo(src, h)
                dve.wait_ge(m["mix_ready"], due(m["mix_ready"], 2))

            dve.wait_ge(m["x_in"], due(m["x_in"], 32))
            differences(0)
            mix(0, 0, 0)
            dve.wait_ge(m["x2_in"], due(m["x2_in"], 16))
            differences(1)
            split(q)
            half_lo(0, 0)
            mix(0, 0, 1)
            split(q + 1)
            half_lo(0, 1)
            dve.wait_ge(m["mix_ready"], due(m["mix_ready"], 2))
            split(q + 2)
            split(q + 3)
            mix_all(2, 1)
            ahead(q, 2)
            mix_all(1, 0)
            ahead(q + 2, 6)
            mix_lo(1)
            mix_all(3, 1)
            ahead(q + 8, 4)
            dve.wait_ge(m["lora1_ready"], due(m["lora1_ready"]))
            mix_all(4, 0)
            ahead(q + 12, 4)
            mix_lo(1)
            ahead(q + 16, 4)
            dve.wait_ge(m["lora1_ready"], due(m["lora1_ready"]))
            mix_all(5, 0)
            dve.wait_ge(m["vec_in"], due(m["vec_in"], 16 * 11))
            dve.wait_ge(m["rkv_done"], due(m["rkv_done"], 4))
            vec = lambda n: wide(VEC[:, n, :], [P, TT, D], 1)
            step(dve.tensor_tensor(KK[:], K[:], vec(0), ALU.mult))
            ahead(q + 20, 2)
            step(dve.tensor_tensor(tok[:], KK[:], KK[:], ALU.mult))
            step(dve.tensor_reduce(stat[:, 0:32], by_head(tok[:]), AX_X, ALU.add))
            dve.tensor_scalar(stat[:, 0:32], stat[:, 0:32], 1e-24, None, ALU.max).then_inc(m["ms_ready"], 1)
            due(m["ms_ready"])
            ahead(q + 22, 2)
            dve.wait_ge(m["rkv_done"], due(m["rkv_done"], 2))
            dve.wait_ge(m["lora1_ready"], due(m["lora1_ready"]))
            step(dve.tensor_tensor(TMP[:], R[:], vec(2), ALU.mult))
            dve.wait_ge(m["rstd_ready"], due(m["rstd_ready"]))
            step(dve.tensor_tensor(by_head(KK[:]), by_head(KK[:]), wide(rstd[:], [P, TT * HEADS, HD], 2), ALU.mult))
            dve.wait_ge(m["lora_out"], due(m["lora_out"], 2))
            step(dve.scalar_tensor_tensor(out=tok[:], in0=IC[:], scalar=-1.0, in1=vec(1), op0=ALU.add, op1=ALU.mult))
            dve.scalar_tensor_tensor(out=K[:], in0=tok[:], scalar=1.0, in1=K[:], op0=ALU.add, op1=ALU.mult).then_inc(m["k_done"], 1)
            dve.wait_ge(m["k_done"], due(m["k_done"]))
            dve.tensor_tensor(IC[:], KK[:], IC[:], ALU.mult).then_inc(m["scaled_ready"], 1)
            dve.wait_ge(m["scaled_ready"], due(m["scaled_ready"]))
            for t in range(TT):
                dve.wait_ge(m["exp_ready"], due(m["exp_ready"], 3))
                up_to, inverse, before = DECAYS[t]
                scaled = [dve.tensor_tensor(R[:, t, :], R[:, t, :], up_to, ALU.mult)]
                scaled += [dve.scalar_tensor_tensor(out=KK[:, t, :], in0=KK[:, t, :], scalar=-1.0, in1=before, op0=ALU.mult, op1=ALU.mult)]
                if t == 0:
                    dve.wait_ge(m["bonus_ready"], due(m["bonus_ready"]))
                scaled += [dve.tensor_tensor(x[:, t, :], x[:, t, :], inverse, ALU.mult) for x in (K, IC)]
                if t == TT - 1:
                    for x in scaled:
                        x.then_inc(m["scaled_ready"], 1)
            dve.wait_ge(m["exp_ready"], due(m["exp_ready"]))
            dve.wait_ge(m["presets"], due(m["presets"], 6))
            bank = lambda c, b: (acc, aux)[c][:, b, :]
            heads4 = lambda v: wide(v, [P, GROUP, P], 1)
            heads2 = lambda v: wide(v, [P, 2, P], 1)

            def head_norm(g):
                cs = slice(g * GROUP * HD, (g + 1) * GROUP * HD)
                heads = lambda x: x[:, :, cs].rearrange("p t (h d) -> p t h d", d=HD)
                spread = lambda v: v.unsqueeze(3).to_broadcast([P, TT, GROUP, HD])
                sums = stat[:, 0:TT * GROUP].rearrange("p (t h) -> p t h", t=TT)
                gn = lambda k: wide(DEC[:, k, cs], [P, TT, GROUP * HD], 1)

                def centre():
                    dve.wait_ge(m["y_copied"], due(m["y_copied"], TT))
                    step(dve.tensor_reduce(sums, heads(tok), AX_X, ALU.add))
                    step(dve.tensor_scalar(sums, sums, 1.0 / HD, None, ALU.mult))
                    step(dve.tensor_tensor(heads(tok), heads(tok), spread(sums), ALU.subtract))

                def variance():
                    step(dve.tensor_tensor(KK[:, :, cs], tok[:, :, cs], tok[:, :, cs], ALU.mult))
                    step(dve.tensor_reduce(sums, heads(KK), AX_X, ALU.add))
                    dve.tensor_scalar(sums, sums, 1.0 / HD, GN_EPS, ALU.mult, ALU.add).then_inc(m["ms_ready"], 1)
                    due(m["ms_ready"])
                    step(dve.tensor_tensor(heads(IC), heads(V), spread(BONUS[:, :, g * GROUP:(g + 1) * GROUP]), ALU.mult))

                def scale():
                    step(dve.tensor_tensor(IC[:, :, cs], IC[:, :, cs], gn(1), ALU.add))
                    dve.wait_ge(m["rstd_ready"], due(m["rstd_ready"]))
                    step(dve.tensor_tensor(heads(tok), heads(tok), spread(rstd[:, 0:TT * GROUP].rearrange("p (t h) -> p t h", t=TT)), ALU.mult))
                    step(dve.tensor_tensor(tok[:, :, cs], tok[:, :, cs], gn(0), ALU.mult))
                    step(dve.tensor_tensor(tok[:, :, cs], tok[:, :, cs], IC[:, :, cs], ALU.add))

                return centre, variance, scale

            def turned_group():
                for n, dst in enumerate((KTT, BTT)):
                    dve.wait_ge(m["group_turned"], due(m["group_turned"], 3 - 2 * n))
                    for e in range(2):
                        of = slice(e * HD, (e + 1) * HD)
                        last = dve.tensor_copy(dst[of, e:GROUP:2, :], acc[of, 3 - n, :].rearrange("p (k n) -> p k n", k=2))
                    last.then_inc(m["group_copied"], 1)

            def key_pairs(k):
                for c in range(TT):
                    dve.wait_ge(m["pair2_ready"], due(m["pair2_ready"]))
                    two = bank(c, 3).rearrange("p (h x n) -> p h x n", h=2, x=2)
                    dve.copy_predicated(AK[:, c, 2 * k:2 * k + 2, :], heads2(PICK[:, 0, :]), two[:, :, 0, :])
                    dve.copy_predicated(RK[:, c, 2 * k:2 * k + 2, :], heads2(PICK[:, 1, :]), two[:, :, 1, :])\
                       .then_inc(m["pair2_masked"], 1)

            def bonus():
                step(dve.tensor_reduce(BONUS[:].rearrange("p t h -> p (t h)"), by_head(TMP[:]), AX_X, ALU.add))
                dve.wait_ge(m["gn_in"], due(m["gn_in"], 32))

            for g in range(HEADS // GROUP):
                turned_group()
                for c in range(TT):
                    dve.wait_ge(m["inverse_set"], due(m["inverse_set"]))
                    dve.wait_ge(m["pair_ready"], due(m["pair_ready"]))
                    one = bank(c, 0).rearrange("p (h n) -> p h n", h=GROUP)
                    dve.tensor_tensor(NM[:, c], one, heads4(STRICT[:]), ALU.mult)
                    dve.copy_predicated(INV[:, c], heads4(PICK[:, 2, :]), one)
                    for k in range(2):
                        two = bank(c, 1 + k).rearrange("p (h x n) -> p h x n", h=2, x=2)
                        dve.copy_predicated(INVT[:, c, 2 * k:2 * k + 2, :], heads2(PICK[:, 3, :]), two[:, :, 0, :])
                        last = dve.copy_predicated(RB[:, c, 2 * k:2 * k + 2, :], heads2(PICK[:, 1, :]), two[:, :, 1, :])
                    last.then_inc(m["pair_masked"], 1)
                between = {0: [lambda: key_pairs(0)], 1: [lambda: key_pairs(1)], 2: [bonus]}
                if g:
                    between.update({2 + k: [part] for k, part in enumerate(head_norm(g - 1))})
                for n in range(len(LEVELS)):
                    for c in range(TT):
                        dve.wait_ge(m["level_ready"], due(m["level_ready"]))
                        dve.tensor_tensor(QM[:, c], bank(c, 0).rearrange("p (h n) -> p h n", h=GROUP), heads4(LMASK[:, n, :]), ALU.mult)\
                           .then_inc(m["level_masked"], 1)
                    for part in between.get(n, ()):
                        part()
                dve.wait_ge(m["state_ready"], due(m["state_ready"]))
                for k in range(2):
                    for h in range(2):
                        of = slice(h * HD, (h + 1) * HD)
                        dve.tensor_scalar(ST[of, k, h, :], bank(0, 3)[of, k * P + h * HD:k * P + (h + 1) * HD], DCOL[of, 2 * g + k:2 * g + k + 1], None,
                                          ALU.mult).then_inc(m["state_copied"], 1)
            for part in head_norm(HEADS // GROUP - 1):
                part()
            dve.wait_ge(m["gate_ready"], due(m["gate_ready"]))
            for t in range(TT):
                cols = tok[:, t, :].rearrange("p (c n) -> p c n", c=2)
                dve.tensor_tensor(cols, cols, acc[:, 2 * t:2 * t + 2, :], ALU.mult).then_inc(m["token_ready"], 1)
            both_operands()
            ahead(q + IN_Q, OUT_Q - 4)

        def ffn(q):
            def hidden(odd, pair):
                dve.wait_ge(m["silu_ready"], due(m["silu_ready"]))
                for t in range(TT):
                    dve.tensor_tensor(HM[:, odd, t, :], SILU[:, odd, t, :], acc[:, 2 * pair + t, 256:512], ALU.mult).then_inc(m["hidden_ready"], 1)

            def hidden_lo(dst, src_hi, odd, done):
                dve.wait_ge(m["hidden_hi"], due(m["hidden_hi"]))
                dve.tensor_tensor(dst, aux[:, odd, :].rearrange("p (k n) -> p k n", k=2), src_hi.bitcast(F32), ALU.subtract).then_inc(done, 1)

            ahead(q, 4)
            hidden(0, 0)
            with due.loop((FB - 1) // 2, {m["silu_ready"]: 2, m["hidden_hi"]: 2}) as i:
                for b in range(2):
                    ahead(q + 4 + 4 * b, 4, (i, 8))
                    hidden(1 - b, 1 - b)
                    ks = bass.ds(i * 4 + 2 * b, 2)
                    hidden_lo(HL[:, ks, :], HH[:, ks, :], b, m["hidden_lo"])
            hidden_lo(HL[:, FK - 2:FK, :], HH[:, FK - 2:FK, :], 0, m["hidden_last"])
            ahead(q + FB * 4, FK - 4)

        def attention(q, near):
            if near:
                dve.wait_ge(m["near_in"], due(m["near_in"], 48))
                step(dve.tensor_scalar(QG[:, 2, :], QG[:, 0, :], HD ** -0.5, None, ALU.mult))
            else:
                dve.wait_ge(m["moba_in"], due(m["moba_in"], 16))
            for j in range(6):
                split_already = 1 if near and 1 <= j <= 4 else 0
                ahead(q + 4 * j + split_already, 4 - split_already)
                used(q + 4 * j + 3)
                dst, cs, banks = (QTOK, KTOK, VTOK)[j // 2], slice((j % 2) * 512, (j % 2 + 1) * 512), acc[:, 2 * (j % 2):2 * (j % 2) + 2, :]
                if j >= 4:
                    dve.tensor_copy(dst[:, :, cs], banks).then_inc(m["in_done"], 1)
                elif near:
                    own = dst[:, :, cs].rearrange("p t (h d) -> p t h d", d=HD)
                    dve.wait_ge(m["qk_square"], due(m["qk_square"]))
                    dve.tensor_reduce(stat[:, 0:16], ROT[:].rearrange("p t (h d) -> p (t h) d", d=HD), AX_X, ALU.add).then_inc(m["qk_summed"], 1)
                    dve.wait_ge(m["qk_summed"], due(m["qk_summed"]))
                    dve.tensor_scalar(stat[:, 0:16], stat[:, 0:16], 1.0 / HD, RMS_EPS, ALU.mult, ALU.add).then_inc(m["ms_ready"], 1)
                    ahead(q + 4 * j + 4, 1)
                    dve.wait_ge(m["rstd_ready"], due(m["rstd_ready"]))
                    for t in range(TT):
                        last = dve.tensor_tensor(own[:, t], own[:, t], wide(rstd[:, 8 * t:8 * t + 8], [P, 8, HD], 2), ALU.mult)
                    last.then_inc(m["in_done"], 1)
                    dve.wait_ge(m["in_done"], due(m["in_done"]))
                    for t in range(TT):
                        last = dve.tensor_tensor(own[:, t], own[:, t], wide(QG[:, 2 - j // 2, :], [P, 8, HD], 1), ALU.mult)
                    last.then_inc(m["qk_done"], 1)
                    dve.wait_ge(m["qk_done"], due(m["qk_done"]))
                else:
                    for t in range(TT):
                        src = banks[:, t, :].rearrange("p (h d) -> p h d", d=HD)
                        own = dst[:, t, cs].rearrange("p (h d) -> p h d", d=HD)
                        rot = ROT[:, t, :].rearrange("p (h d) -> p h d", d=HD)
                        cos, sin = ROPE[:, t, j // 2, 0, :], ROPE[:, t, j // 2, 1, :]
                        dve.tensor_tensor(own, src, wide(cos, [P, 8, HD], 1), ALU.mult)
                        dve.tensor_tensor(rot[:, :, 0:32], src[:, :, 32:64], wide(sin[:, 0:32], [P, 8, 32], 1), ALU.mult)
                        last = dve.tensor_tensor(rot[:, :, 32:64], src[:, :, 0:32], wide(sin[:, 32:64], [P, 8, 32], 1), ALU.mult)
                    last.then_inc(m["in_done"], 1)
                    dve.wait_ge(m["in_done"], due(m["in_done"]))
                    last = dve.tensor_tensor(dst[:, :, cs], dst[:, :, cs], ROT[:], ALU.add)
                    last.then_inc(m["qk_done"], 1)
                    dve.wait_ge(m["qk_done"], due(m["qk_done"]))
            due(m["in_done"], 2)
            if near:
                dve.wait_ge(m["bias_ready"], due(m["bias_ready"], TT))

            def maxima(p):
                dve.wait_ge(m["scores_ready"], due(m["scores_ready"]))
                for t in range(TT):
                    keys = SEQ if near else (t + 1) * P
                    src = acc[:, 2 * (p % 2):2 * (p % 2) + 2, t * SEQ:(t + 1) * SEQ]
                    if near:
                        step(dve.tensor_tensor(SC[:, p % 2, t], src, BIAS[:, t, 2 * p:2 * p + 2, :], ALU.add))
                        src = SC[:, p % 2, t]
                    last = dve.tensor_reduce(NMAX[:, t, 2 * p:2 * p + 2], src[:, :, 0:keys], AX_X, ALU.max, negate=True)
                last.then_inc(m["max_ready"], 1)

            def copy_probs(p):
                dve.wait_ge(m["probs_turned"], due(m["probs_turned"], 2))
                if near:
                    last = dve.tensor_copy(PT[:, p % 2, 1], aux[:, 1, :].rearrange("p (k n) -> p k n", k=TT))
                else:
                    dve.tensor_copy(PT[:, p % 2, 1, 0, :], aux[:, 1, 0:SEQ])
                    last = dve.tensor_copy(PT[:, p % 2, 1, 1, P:SEQ], aux[:, 1, SEQ + P:2 * SEQ])
                last.then_inc(m["probs_copied_v"], 1)

            def outputs(p):
                dve.wait_ge(m["o_ready"], due(m["o_ready"]))
                two = slice(2 * p, 2 * p + 2)
                step(dve.reciprocal(RSUM[:, :, two], SUMS[:, :, two]))
                for t in range(TT):
                    last = dve.tensor_tensor(tok[:, t, 2 * p * HD:2 * (p + 1) * HD].rearrange("p (h d) -> p h d", h=2),
                                             aux[:, 2 + p % 2, 2 * t * HD:2 * (t + 1) * HD].rearrange("p (h d) -> p h d", h=2),
                                             wide(RSUM[:, t, two], [P, 2, HD], 2), ALU.mult)
                    if p == PAIRS - 1:
                        last.then_inc(m["token_ready"], 1)
                if p < PAIRS - 2:
                    last.then_inc(m["o_done"], 1)

            for p in range(PAIRS + 2):
                if p < PAIRS:
                    maxima(p)
                if 1 <= p <= PAIRS:
                    copy_probs(p - 1)
                if p >= 2:
                    outputs(p - 2)
            both_operands()
            ahead(q + IN_Q, OUT_Q - 4)

        def conv(q, layer):
            tap = lambda n, k: taps[:, layer, n, k:k + 1]
            for j in range(6):
                ahead(q + 4 * j, 4)
                banks = acc[:, 2 * (j % 2):2 * (j % 2) + 2, :]
                ks = range(4 * (j % 2), 4 * (j % 2) + 4)
                part = lambda x: x[:, ks[0]:ks[-1] + 1, :]
                pairs = lambda x: part(x).rearrange("p (b k) n -> p b (k n)", b=2)
                if j >= 2:
                    used(q + 4 * j + 3)
                if j in (2, 3):
                    dve.wait_ge(m["c_done"], due(m["c_done"]))
                    dve.tensor_tensor(pairs(ZT), pairs(CT), banks, ALU.mult).then_inc(m["z_done"], 1)
                    dve.wait_ge(m["z_done"], due(m["z_done"]))
                    for k in ks:
                        last = dve.tensor_scalar(CV[:, k, :], ZT[:, k, :], tap(1, k), None, ALU.mult)
                    step(last)
                    for k in ks:
                        last = dve.scalar_tensor_tensor(out=CV[:, k, 1:SEQ], in0=ZT[:, k, 0:SEQ - 1], scalar=tap(0, k), in1=CV[:, k, 1:SEQ],
                                                        op0=ALU.mult, op1=ALU.add)
                    step(last)
                    for k in ks:
                        last = dve.scalar_tensor_tensor(out=CV[:, k, 0:SEQ - 1], in0=ZT[:, k, 1:SEQ], scalar=tap(2, k), in1=CV[:, k, 0:SEQ - 1],
                                                        op0=ALU.mult, op1=ALU.add)
                    step(last)
                if j >= 4:
                    dve.tensor_tensor(pairs(YT), pairs(CV), banks, ALU.mult).then_inc(m["y_done"], 1)
                    dve.wait_ge(m["conv_hi_done"], due(m["conv_hi_done"]))
                    dve.tensor_tensor(part(OL), part(YT), part(OH).bitcast(F32), ALU.subtract).then_inc(m["conv_lo_done"], 1)
            ahead(q + IN_Q, OUT_Q - 4)

        def hyena(q):
            two = lambda x: x.rearrange("p (c n) -> p c n", c=2)

            def argument(n):
                dve.wait_ge(m["mlp_ready"], due(m["mlp_ready"]))
                step(dve.tensor_scalar(ARG[:, 0, :], aux[0:FHID, 0, 0:SEQ], FCOL[:, n:n + 1], FCOL[:, 2:3], ALU.add, ALU.mult))
                step(dve.tensor_scalar(ARG[:, 1, :], ARG[:, 0, :], 1.0 / TWO_PI, MAGIC, ALU.mult, ALU.add))
                step(dve.tensor_scalar(ARG[:, 1, :], ARG[:, 1, :], -MAGIC, None, ALU.add))
                for c in (-TWO_PI_HI, -TWO_PI_LO):
                    step(dve.scalar_tensor_tensor(out=ARG[:, 0, :], in0=ARG[:, 1, :], scalar=c, in1=ARG[:, 0, :], op0=ALU.mult, op1=ALU.add))
                dve.tensor_scalar(ARG[:, 0, :], ARG[:, 0, :], PI_BELOW, -PI_BELOW, ALU.min, ALU.max).then_inc(m["arg_ready"], 1)

            def window(r, pairs):
                t, d = r // 2, r % 2
                b = 2 * (r % pairs)
                dve.wait_ge(m["filt_ready"], due(m["filt_ready"]))
                dve.tensor_tensor(two(TAPS[pairs - 1][2 * d + t]), aux[:, b:b + 2, :], two(WIN[:, t, :]), ALU.mult).then_inc(m["filt_done"], 1)

            def even_odd(filt):
                x = TAPS[filt]
                dve.wait_ge(m["filt_done"], due(m["filt_done"], 4))
                for k, op in enumerate((ALU.add, ALU.subtract)):
                    for t in range(TT):
                        last = dve.tensor_tensor(EO[:, 2 * k + t, :], x[t], x[2 + t], op)
                    last.then_inc(m["eo_ready"], 1)

            def convolve(j):
                used(q + 4 * j + 3)
                if j >= 2:
                    dve.wait_ge(m["cv_turned"], due(m["cv_turned"]))
                src = lambda c: acc[:, 2 * (j % 2) + c // 2, (c % 2) * SEQ:(c % 2 + 1) * SEQ]
                tap = lambda n, c: TAPS3[:, n, 4 * j + c:4 * j + c + 1]
                for c in range(4):
                    last = dve.tensor_scalar(HCV[:, j % 2, c, :], src(c), tap(1, c), tap(3, c), ALU.mult, ALU.add)
                step(last)
                for c in range(4):
                    last = dve.scalar_tensor_tensor(out=HCV[:, j % 2, c, 1:SEQ], in0=src(c)[:, 0:SEQ - 1], scalar=tap(0, c),
                                                    in1=HCV[:, j % 2, c, 1:SEQ], op0=ALU.mult, op1=ALU.add)
                step(last)
                for c in range(4):
                    last = dve.scalar_tensor_tensor(out=HCV[:, j % 2, c, 0:SEQ - 1], in0=src(c)[:, 1:SEQ], scalar=tap(2, c),
                                                    in1=HCV[:, j % 2, c, 0:SEQ - 1], op0=ALU.mult, op1=ALU.add)
                last.then_inc(m["cv_ready"], 1)

            def reciprocal(c):
                if c == 0:
                    dve.wait_ge(m["norm_copied"], due(m["norm_copied"]))
                step(dve.reciprocal(two(RN[:])[:, c], two(RN[:])[:, c]))

            dve.wait_ge(m["hyena_in"], due(m["hyena_in"], 16 * 10))
            nothing = lambda: None
            pieces = [lambda: argument(0), lambda: argument(1)] + [lambda r=r: window(r, 1) for r in range(4)] + [lambda: even_odd(0)] + [nothing] * 5
            for j in range(6):
                ahead(q + 4 * j, 2)
                pieces[2 * j]()
                ahead(q + 4 * j + 2, 2)
                pieces[2 * j + 1]()
                convolve(j)
            due(m["cv_turned"], 2)
            dve.wait_ge(m["freq_done"], due(m["freq_done"], 5))
            for n in range(ORDER):
                for r in range(4):
                    f, c = r // 2, r % 2
                    cs = slice(c * 512, (c + 1) * 512)
                    re, im = acc[:, 2 * (r % 2), :], acc[:, 2 * (r % 2) + 1, :]
                    dve.wait_ge(m["dft_ready"], due(m["dft_ready"]))
                    dve.tensor_tensor(FR[:, f, cs], re, HF[:, f, cs], ALU.mult)
                    dve.tensor_tensor(EO[:, 0, cs], im, HF[:, 3 + f, cs], ALU.mult)
                    dve.tensor_tensor(FR[:, 2 + f, cs], re, HF[:, 3 + f, cs], ALU.mult)
                    step(dve.tensor_tensor(EO[:, 1, cs], im, HF[:, 1 if f else 2, cs], ALU.mult))
                    dve.tensor_tensor(FR[:, f, cs], FR[:, f, cs], EO[:, 0, cs], ALU.subtract)
                    dve.tensor_tensor(FR[:, 2 + f, cs], FR[:, 2 + f, cs], EO[:, 1, cs], ALU.add).then_inc(m["dft_done"], 1)
                    dve.wait_ge(m["dft_done"], due(m["dft_done"]))
                if n:
                    dve.wait_ge(m["skip2_in"], due(m["skip2_in"], 16))
                step(dve.tensor_tensor(HV[:], HV[:], wide(SKIP[:], [P, TT, D], 1), ALU.mult))
                if n == 0:
                    for r in range(4):
                        window(r, 2)
                    even_odd(1)
                    dve.wait_ge(m["cv_copied"], due(m["cv_copied"], 6))
                    reciprocal(0)
                reciprocal(1)
                for t in range(TT):
                    dve.wait_ge(m["idft_ready"], due(m["idft_ready"]))
                    step(dve.tensor_tensor(two(tok[:, t, :]), acc[:, 2 * t:2 * t + 2, :], two(RN[:]), ALU.mult))
                    step(dve.tensor_tensor(tok[:, t, :], tok[:, t, :], HV[:, t, :], ALU.add))
                    if n == 0:
                        last = dve.tensor_tensor(HV[:, t, :], tok[:, t, :], HX1[:, t, :], ALU.mult)
                    else:
                        dve.tensor_tensor(tok[:, t, :], tok[:, t, :], HX2[:, t, :], ALU.mult).then_inc(m["token_ready"], 1)
                if n == 0:
                    last.then_inc(m["idft_done"], 1)
                    dve.wait_ge(m["idft_done"], due(m["idft_done"]))
                    reciprocal(0)
                    dve.wait_ge(m["freq_done"], due(m["freq_done"], 5))
            both_operands()
            ahead(q + IN_Q, OUT_Q - 4)

        convs = 0
        for n, kind in enumerate(layers):
            if kind == "conv":
                conv(start[n], convs)
                convs += 1
            else:
                {"rwkv": rwkv, "ffn": ffn, "moba": lambda q: attention(q, False), "near": lambda q: attention(q, True),
                 "hyena": hyena}[kind](start[n])
            residual(n, start[n] + (FFN_Q if kind == "ffn" else IN_Q + OUT_Q))

    @block.gpsimd
    def _(pool):
        due = Tally(pool)

        def load(dst, src, done):
            pool.dma_start(dst, src).then_inc(done, 16)

        def rsqrt(n):
            pool.wait_ge(m["ms_ready"], due(m["ms_ready"]))
            pool.tensor_tensor(rstd[:, 0:n], stat[:, 0:n], half[:, 0:n], ALU.pow).then_inc(m["rstd_ready"], 1)

        def power(t, mean_square, scale, eps):
            pool.tensor_scalar(stat[:, t:t + 1], mean_square, scale, eps, ALU.mult, ALU.add).then_inc(m["eps_added"], 1)
            pool.wait_ge(m["eps_added"], due(m["eps_added"]))
            pool.tensor_tensor(rstd[:, t:t + 1], stat[:, t:t + 1], half[:, 0:1], ALU.pow).then_inc(m["rstd_ready"], 1)

        def load_ln(n):
            load(lng[:], A["ln_g"][n].partition_broadcast(P), m["ln_in"])
            load(lnb[:], A["ln_b"][n].partition_broadcast(P), m["ln_in"])

        pool.memset(half[:], -0.5).then_inc(m["halves_set"], 1)
        pool.memset(LW[:], 1.0).then_inc(m["halves_set"], 1)
        pool.memset(LA[:], 1.0).then_inc(m["halves_set"], 1)
        first_loads = [(VEC[:, k, :], A["vec"][k].partition_broadcast(P), m["vec_in"]) for k in range(3)]
        first_loads += [(dst[:], A[name], m["consts_in"]) for dst, name in ((ident, "ident"), (taps, "taps"))]
        first_loads += [(dst[:], A[name], m["vec_in"]) for dst, name in (
            (L2, "lora2"), (CUM, "cum"), (SPAN, "span"), (LMASK, "level_masks"), (STRICT, "strict"), (PICK, "pick"), (G2, "g2a"), (G2b, "g2b"))]
        first_loads += [(X[:, t, :], A["x"][:, t], m["res_in"]) for t in range(TT)]
        for k, what in enumerate(first_loads):
            pool.wait_ge(w_used[k % SLOTS], k // SLOTS + 1)
            load(*what)
        load_ln(0)
        pool.wait_ge(m["consts_in"], due(m["consts_in"], 16 * 2))
        for h in range(GROUP):
            pool.tensor_copy(identb[:, h * P:(h + 1) * P], ident[:]).then_inc(m["identb_set"], 1)
        pool.wait_ge(m["halves_set"], due(m["halves_set"], 3))
        for _ in range(2):
            pool.memset(stat[:, 60:61], 0.0).then_inc(m["hidden_lo"], 1)
            pool.wait_ge(m["hidden_lo"], due(m["hidden_lo"]))

        def rwkv():
            rsqrt(32)
            pool.wait_ge(m["k_done"], due(m["k_done"]))
            pool.tensor_tensor(TMP[:], TMP[:], K[:], ALU.mult).then_inc(m["bonus_ready"], 1)
            pool.wait_ge(m["scaled_ready"], due(m["scaled_ready"]))
            for zeros in (AK, RB, RK, KTT, BTT, ST):
                pool.memset(zeros[:], 0.0).then_inc(m["presets"], 1)
            pool.wait_ge(m["exp_ready"], due(m["exp_ready"], 7))
            for k, name in enumerate(("gn_g", "gn_b")):
                load(DEC[:, k, :], A[name].partition_broadcast(P), m["gn_in"])
            for _ in range(HEADS // GROUP):
                rsqrt(TT * GROUP)

        def before(n):
            pool.wait_ge(m["residual_done"], TT * n)

        def load_moba():
            load(ROPE[:], A["rope"], m["moba_in"])
            load(FLIP[:], A["causal"], m["causal_in"])
            pool.wait_ge(m["causal_in"], due(m["causal_in"], 16))
            pool.tensor_copy(CAUSAL[:], FLIP[:]).then_inc(m["causal_set"], 1)

        def load_near():
            load(FLIP[:], A["flip"], m["near_in"])
            load(QG[:, 0, :], A["q_gain"].partition_broadcast(P), m["near_in"])
            load(QG[:, 1, :], A["k_gain"].partition_broadcast(P), m["near_in"])
            load(BMASK[:], A["near_mask"], m["bias_in"])
            rpb = A["rpb"]
            for r in range(ROWS):
                for s in range(ROWS):
                    src = bass.AP(tensor=rpb.tensor, offset=rpb.offset + (s - r + RPB_ROWS // 2) * RPB_PAD,
                                  ap=[[1, GRID_W], [RPB_ROWS * RPB_PAD, HEADS], [1, GRID_W]])
                    of = slice((r % 2) * GRID_W, (r % 2 + 1) * GRID_W)
                    load(BIAS[of, r // 2, :, s * GRID_W:(s + 1) * GRID_W], src, m["bias_in"])
            pool.wait_ge(m["bias_in"], due(m["bias_in"], 16 * (1 + ROWS * ROWS)))
            for t in range(TT):
                pool.tensor_tensor(BIAS[:, t], BIAS[:, t], BMASK[:, t, :].unsqueeze(1).to_broadcast([P, HEADS, SEQ]), ALU.add)\
                    .then_inc(m["bias_ready"], 1)

        def load_hyena():
            pool.memset(ONES[:], 1.0).then_inc(m["ones_set"], 1)
            for dst, name in ((WIN, "window"), (DFT, "dft"), (IDFT, "idft"), (EMBT, "emb"), (TAPS3, "taps3"), (FCOL, "f_cols")):
                load(dst[:], A[name], m["hyena_in"])
            load(SKIP[:], A["f_skip"][0].partition_broadcast(P), m["hyena_in"])
            load(FW[0:EMB, 0, :], A["f_w1"], m["hyena_in"])
            load(FW[:, 1, :], A["f_w2"], m["hyena_in"])
            load(FW3[:], A["f_w3"][0], m["hyena_in"])

        def near():
            for _ in range(4):
                rsqrt(16)

        def hyena():
            def sum_taps(filt):
                x = TAPS[filt]
                pool.wait_ge(m["eo_ready"], due(m["eo_ready"], 2))
                pool.tensor_tensor(x[0][0:1, :], x[0][0:1, :], x[2][0:1, :], ALU.add).then_inc(m["tap0_joined"], 1)
                pool.wait_ge(m["tap0_joined"], due(m["tap0_joined"]))
                pool.memset(x[2][0:1, :], 0.0).then_inc(m["tap0_joined"], 1)
                due(m["tap0_joined"])
                for k, (a, b) in enumerate(((0, 1), (2, 3), (0, 2))):
                    if k < 2:
                        pool.wait_ge(m["filt_abs"], due(m["filt_abs"], 2))
                    else:
                        pool.wait_ge(m["filt_summed"], due(m["filt_summed"], 2))
                    pool.tensor_tensor(x[a], x[a], x[b], ALU.add).then_inc(m["filt_summed"], 1)
                due(m["filt_summed"])

            pool.wait_ge(m["filt_done"], due(m["filt_done"], 4))
            load(FW3[:], A["f_w3"][1], m["taps2_in"])
            sum_taps(0)
            sum_taps(1)
            pool.wait_ge(m["idft_done"], due(m["idft_done"]))
            load(SKIP[:], A["f_skip"][1].partition_broadcast(P), m["skip2_in"])

        def norms(n):
            rms = LAYER_NORMS - 1 <= n < len(layers) - 1
            if n < LAYER_NORMS:
                for t in range(TT):
                    pool.wait_ge(m["ms_ready"], due(m["ms_ready"]))
                    power(t, mom[:, t, 1:2], 1.0, LN_EPS)
            if rms:
                for t in range(TT):
                    pool.wait_ge(m["square_ready"], due(m["square_ready"]))
                    power(t, stat[:, 56 + t:57 + t], 1.0 / D, RMS_EPS)
            operands = sum(8 if kind in ("rwkv", "moba", "near", "hyena") else 4 for kind in layers[:n + 1])
            if n + 1 < len(layers):
                pool.wait_ge(m["operand_ready"], operands)
                if n + 1 < LAYER_NORMS:
                    load_ln(n + 1)
                elif n + 2 < len(layers):
                    load(lng[:], A["gains"][n + 1 - LAYER_NORMS + 1].partition_broadcast(P), m["gain_in"])

        ahead_of = {"moba": load_moba, "near": load_near, "hyena": load_hyena}
        inside = {"rwkv": rwkv, "near": near, "hyena": hyena}
        for n, kind in enumerate(layers):
            if kind in inside:
                inside[kind]()
            if n + 1 < len(layers):
                before(n)
                if layers[n + 1] in ahead_of:
                    ahead_of[layers[n + 1]]()
                if n == LAYER_NORMS - 1:
                    load(FIRSTG[:], A["gains"][0].partition_broadcast(P), m["gain_in"])
            norms(n)

    ctx.close()


def constants():
    c = {}
    f32 = np.float32
    i, j = np.arange(P)[:, None], np.arange(P)[None, :]
    c["ident"] = np.eye(P, dtype=f32)
    middle = i < P // 2
    c["cum"] = np.stack([-DECAY * ((i <= j).astype(f32) - middle), -DECAY * ((i < j).astype(f32) - middle)], 1).astype(f32)
    c["span"] = (-DECAY * np.stack([np.arange(P) >= P // 2, np.arange(P) < P // 2], 1)).astype(f32)
    c["strict"] = (j < i).astype(f32)
    low = lambda a, b, n: (a // n % 2 == 1) & (b // n % 2 == 0) & (a // (2 * n) == b // (2 * n))
    eye = np.eye(P)
    c["level_masks"] = np.stack([low(j, i, n) + eye for n in LEVELS], 1).astype(f32)
    c["pick"] = np.stack([i < j, i <= j, low(i, j, 1), low(j, i, 1)], 1).astype(np.uint32)
    inv = (f32(10000.0) ** (-np.arange(0, HD, 2, dtype=f32) / f32(HD))).astype(f32)
    ang = np.arange(SEQ, dtype=f32)[:, None] * inv[None, :]
    cos, sin = np.cos(ang).astype(f32), np.sin(ang).astype(f32)
    both = np.stack([np.concatenate([cos, cos], 1), np.concatenate([-sin, sin], 1)], 1)
    rope = np.stack([both * f32(HD ** -0.5), both], 1)
    c["rope"] = rope.reshape(TT, P, 2, 2, HD).transpose(1, 0, 2, 3, 4).astype(f32)
    c["causal"] = np.where(j <= i, 0.0, -3.0e38).astype(f32)
    c["flip"] = (i // GRID_W * GRID_W + GRID_W - 1 - i % GRID_W == j).astype(f32)
    col = np.arange(GRID_W)
    first = np.clip(col - 8, 0, GRID_W - 16)
    sees = (col[None, :] >= first[:, None]) & (col[None, :] < first[:, None] + 16)
    c["near_mask"] = np.tile(np.where(sees[::-1], 0.0, -3.0e38), (ROWS, ROWS)).reshape(TT, P, SEQ).transpose(1, 0, 2).astype(f32)
    t = np.linspace(0.0, 1.0, SEQ, dtype=f32)[:, None]
    bands = np.linspace(1e-4, BANDS - 1, BANDS, dtype=f32)
    ang = (f32(TWO_PI) * np.arange(SEQ, dtype=f32)[:, None] / f32(SEQ) * bands).astype(f32)
    c["emb"] = np.concatenate([t, np.cos(ang), -np.sin(ang)], 1).astype(f32).T
    lt = np.log(1e-2)
    deltas = np.abs(np.linspace(lt / 1.5, lt / 0.3, D, dtype=f32))
    c["window"] = np.exp(-t * deltas).astype(f32).reshape(TT, P, D).transpose(1, 0, 2)
    n = 2 * SEQ
    w = 2.0 * np.pi / n * (np.arange(SEQ)[:, None] * np.arange(SEQ)[None, :] % n)
    re, im, nyquist = np.cos(w), -np.sin(w), np.cos(np.pi * np.arange(SEQ))
    put = lambda a: np.concatenate([nyquist[:, None], a[:, 1:P]], 1)
    dft = np.stack([re[:, :P], re[:, P:], put(im), im[:, P:], im[:, :P], put(re)], 1)
    c["dft"] = dft.reshape(TT, P, 6, P).transpose(1, 0, 2, 3).astype(f32)
    back_re, back_im = 2.0 * re.T / n, 2.0 * im.T / n
    back_re[0] /= 2.0
    back_im[0] = nyquist / n
    c["idft"] = np.concatenate([back_re, back_im]).reshape(4, P, SEQ).transpose(1, 0, 2).astype(f32)
    return {k: np.ascontiguousarray(v) for k, v in c.items()}


def column_blocks(w):
    return w.reshape(4, 2, P, -1, 512).transpose(3, 0, 2, 1, 4).reshape(-1, P, QW)


def layout(x, **w):
    a = constants()
    rows = lambda v: v.reshape(-1, P)
    quarters = []

    def ffn(w_in, w_down):
        blocks = w_in.reshape(4, 2, P, 2, FB, 256).transpose(4, 0, 2, 1, 3, 5).reshape(-1, P, QW)
        quarters.extend([blocks, w_down.reshape(FK, P, D)])

    def mixer(w_in, w_out):
        quarters.extend([column_blocks(w_in), w_out.reshape(KT, P, D)])

    def gated(w_in):
        b, c, u = np.split(w_in, 3, axis=1)
        return np.concatenate([c, u, b], axis=1)

    mixer(np.concatenate(list(w["rwkv_w_rkv"][0]), axis=1), w["rwkv_w_o"][0])
    ffn(w["ffn_w_in"][0], w["ffn_w_down"][0])
    mixer(w["moba_w_qkv"][0], w["moba_w_o"][0])
    ffn(w["ffn_w_in"][1], w["ffn_w_down"][1])
    mixer(gated(w["a_w_in_2"][0]), w["a_w_out_2"][0])
    ffn(w["f_w13_2"][0], w["f_w2_2"][0])
    mixer(w["b_w_qkv_2"][0], w["b_w_out_2"][0])
    ffn(w["f_w13_2"][1], w["f_w2_2"][1])
    mixer(w["c_w_in_2"][0], w["c_w_out_2"][0])
    ffn(w["f_w13_2"][2], w["f_w2_2"][2])
    mixer(gated(w["a_w_in_2"][1]), w["a_w_out_2"][1])
    ffn(w["f_w13_2"][3], w["f_w2_2"][3])
    a["weights"] = np.concatenate(quarters)

    a["x"] = x[0].reshape(TT, P, D).transpose(1, 0, 2)
    a["xT"] = x[0].T.reshape(KT, P, SEQ).transpose(1, 0, 2)
    a["mu"] = w["rwkv_mu"][0].reshape(6, KT, P).transpose(2, 0, 1)
    lora1 = np.concatenate([w["rwkv_w1"][0], w["rwkv_a1"][0], w["rwkv_g1"][0]], axis=1)
    a["lora1"] = lora1.reshape(KT, P, -1).transpose(1, 0, 2)
    a["lora2"] = np.stack([np.concatenate([w["rwkv_w2"][0], w["rwkv_w0"]]), np.concatenate([w["rwkv_a2"][0], w["rwkv_a0"]])], axis=1)
    a["vec"] = np.concatenate([w["rwkv_k_k"], w["rwkv_k_a"], w["rwkv_r_k"].reshape(1, D)])
    a["g2a"], a["g2b"] = w["rwkv_g2"][0, :P], w["rwkv_g2"][0, P:]
    a["gn_g"], a["gn_b"] = w["rwkv_gn_g"][0], w["rwkv_gn_b"][0]
    a["ln_g"] = np.stack([w["ln_mix_g"][0], w["ln_ffn_g"][0], w["ln_mix_g"][1], w["ln_ffn_g"][1]])
    a["ln_b"] = np.stack([w["ln_mix_b"][0], w["ln_ffn_b"][0], w["ln_mix_b"][1], w["ln_ffn_b"][1]])
    a["gains"] = np.stack([w["norm_mix_g_2"], w["norm_ffn_g_2"]], 1).reshape(8, D)
    a["taps"] = w["a_conv_w_2"].reshape(2, 3, KT, P).transpose(3, 0, 1, 2)
    a["q_gain"], a["k_gain"] = w["b_q_norm_g_2"][0], w["b_k_norm_g_2"][0]
    pad = (RPB_PAD - RPB_COLS) // 2
    a["rpb"] = np.pad(w["b_rpb_2"][0], ((0, 0), (0, 0), (pad, pad)))
    a["taps3"] = np.concatenate([w["c_short_w_2"][0], w["c_short_b_2"]]).reshape(4, 3 * KT, P).transpose(2, 0, 1)
    a["f_w1"], a["f_w2"] = w["c_f_w1_2"][0], w["c_f_w2_2"][0]
    a["f_w3"] = w["c_f_w3_2"][0].reshape(FHID, ORDER, 2 * D).transpose(1, 0, 2)
    a["f_cols"] = np.stack([w["c_f_b1_2"][0], w["c_f_b2_2"][0], w["c_f_freq_2"][0]], axis=1)
    a["f_skip"] = w["c_f_skip_2"][0]
    return {k: np.ascontiguousarray(v) for k, v in a.items()}


def kernel(**inputs):
    import concourse.bacc as bacc
    from concourse.bass_utils import run_bass_kernel_spmd

    arrays = layout(**{k: np.asarray(v) for k, v in inputs.items()})
    nc = bacc.Bacc("TRN2", target_bir_lowering=False, num_devices=1)
    A = {k: nc.dram_tensor(f"in_{k}", v.shape, mybir.dt.from_np(v.dtype), kind="ExternalInput").ap() for k, v in arrays.items()}
    out = nc.dram_tensor("out_x", (SEQ, D), F32, kind="ExternalOutput").ap()
    program(nc, A, out.rearrange("(t p) c -> p t c", p=P))
    r = run_bass_kernel_spmd(nc, [{f"in_{k}": v for k, v in arrays.items()}], core_ids=[0])
    return r.results[0]["out_x"].reshape(1, SEQ, D)
```
